# Optimizing a Trainium2 kernel written in Bass

```python
import math
import jax, jax.numpy as jnp
from jax import lax
import numpy as np

D_MODEL = 1024
BATCH = 1
SEQ = 512
DEPTH = 2

MLA_HEADS = 8
MLA_NOPE = 64
MLA_ROPE = 32
MLA_V = 64
MLA_Q_RANK = 256
MLA_KV_RANK = 128
ROPE_BASE = 10000.0
Q_BLOCK = 128
POS_MAX_OFFSET = 4096

MLSTM_HEADS = 4
MLSTM_DH = 64
MLSTM_CHUNK = 64
M_INIT = -1e30

SSD_HEADS = 4
SSD_HEADDIM = 64
SSD_GROUPS = 2
SSD_HPG = SSD_HEADS // SSD_GROUPS
SSD_STATE = 128
SSD_CONV = 5
SSD_CHUNK = 128

MLA_OUT = MLA_HEADS * MLA_V
MLSTM_W = MLSTM_HEADS * MLSTM_DH
SSD_INNER = SSD_HEADS * SSD_HEADDIM
MIX_WIDTH = MLA_OUT + MLSTM_W + SSD_INNER
SSD_CONV_DIM = SSD_INNER + 2 * SSD_GROUPS * SSD_STATE
IN_SIZES = (MLA_Q_RANK, MLA_KV_RANK, MLA_ROPE,
            MLSTM_W, MLSTM_W, MLSTM_W, MLSTM_W, 4 * MLSTM_HEADS,
            SSD_INNER, SSD_CONV_DIM, 2 * SSD_HEADS)
IN_WIDTH = sum(IN_SIZES)

N_GROUPS = 4
EXPERTS_PER_GROUP = 4
N_EXPERTS = N_GROUPS * EXPERTS_PER_GROUP
TOP_K = 2
D_EXPERT = 256

DEEPNORM_ALPHA = (2 * DEPTH) ** 0.25
DEEPNORM_BETA = (8 * DEPTH) ** -0.25


F32 = jnp.float32

def _split(t, sizes):
    out, off = [], 0
    for s in sizes:
        out.append(t[..., off:off + s])
        off += s
    return out

def _layernorm(x, g, b, eps=1e-5):
    xf = x.astype(F32)
    mu = jnp.mean(xf, -1, keepdims=True)
    var = jnp.mean(jnp.square(xf - mu), -1, keepdims=True)
    return (xf - mu) * lax.rsqrt(var + eps) * g + b

def _rmsnorm(x, g, eps=1e-6):
    xf = x.astype(F32)
    return xf * lax.rsqrt(jnp.mean(xf * xf, -1, keepdims=True) + eps) * g

def _rope_table(positions):
    inv = ROPE_BASE ** (-jnp.arange(0, MLA_ROPE, 2, dtype=F32) / MLA_ROPE)
    ang = positions.astype(F32)[..., None] * inv
    return jnp.cos(ang), jnp.sin(ang)

def _apply_rope(t, cos, sin):
    half = t.shape[-1] // 2
    t1, t2 = t[..., :half].astype(F32), t[..., half:].astype(F32)
    return jnp.concatenate([t1 * cos - t2 * sin, t2 * cos + t1 * sin], -1)

def _mla(c_q, c_kv, k_r, cos, sin, q_norm, kv_norm, w_uq, w_ukv):
    Bsz, S, _ = c_q.shape
    q = (_rmsnorm(c_q, q_norm).astype(c_q.dtype) @ w_uq).reshape(Bsz, S, MLA_HEADS, MLA_NOPE + MLA_ROPE)
    q_nope = q[..., :MLA_NOPE]
    q_rope = _apply_rope(q[..., MLA_NOPE:], cos[:, :, None], sin[:, :, None]).astype(q.dtype)
    kv = (_rmsnorm(c_kv, kv_norm).astype(c_kv.dtype) @ w_ukv).reshape(Bsz, S, MLA_HEADS, MLA_NOPE + MLA_V)
    k_nope, v = kv[..., :MLA_NOPE], kv[..., MLA_NOPE:]
    k_rope = _apply_rope(k_r, cos, sin).astype(k_r.dtype)
    scale = (MLA_NOPE + MLA_ROPE) ** -0.5
    nb = S // Q_BLOCK
    qn = q_nope.reshape(Bsz, nb, Q_BLOCK, MLA_HEADS, MLA_NOPE).transpose(1, 0, 2, 3, 4)
    qr = q_rope.reshape(Bsz, nb, Q_BLOCK, MLA_HEADS, MLA_ROPE).transpose(1, 0, 2, 3, 4)

    def block(args):
        qn_b, qr_b = args
        s = (jnp.einsum('bqhd,bkhd->bhqk', qn_b, k_nope)
             + jnp.einsum('bqhr,bkr->bhqk', qr_b, k_rope)).astype(F32) * scale
        p = jax.nn.softmax(s, axis=-1).astype(v.dtype)
        return jnp.einsum('bhqk,bkhd->bqhd', p, v)

    o = lax.map(block, (qn, qr))
    return o.transpose(1, 0, 2, 3, 4).reshape(Bsz, S, MLA_OUT)

def _mlstm_scan(q, k, v, ig, lf):
    Bsz, S, H, Dh = q.shape
    L = MLSTM_CHUNK
    nc = S // L

    def chunks(t):
        t = t.reshape((Bsz, nc, L, H) + t.shape[3:])
        return jnp.moveaxis(jnp.moveaxis(t, 1, 0), 3, 2)

    mask = jnp.tril(jnp.ones((L, L), bool))

    def step(carry, inp):
        C, n, m = carry
        qc, kc, vc, igc, lfc = inp
        b = jnp.cumsum(lfc, axis=-1)
        a = jnp.where(mask, b[..., :, None] - b[..., None, :] + igc[..., None, :], -jnp.inf)
        g = b + m[..., None]
        m_t = jnp.maximum(g, jnp.max(a, -1))
        w_intra = jnp.exp(a - m_t[..., None])
        w_inter = jnp.exp(g - m_t)
        qk = jnp.einsum('bhtd,bhsd->bhts', qc, kc).astype(F32) * w_intra
        num = (jnp.einsum('bhts,bhsd->bhtd', qk, vc)
               + w_inter[..., None] * jnp.einsum('bhtd,bhde->bhte', qc, C))
        den = jnp.sum(qk, -1) + w_inter * jnp.einsum('bhtd,bhd->bht', qc, n)
        h = num / jnp.maximum(jnp.abs(den), jnp.exp(-m_t))[..., None]
        bL = b[..., -1]
        dec = bL[..., None] - b + igc
        m_new = jnp.maximum(bL + m, jnp.max(dec, -1))
        w_s = jnp.exp(dec - m_new[..., None])
        w_c = jnp.exp(bL + m - m_new)
        C = w_c[..., None, None] * C + jnp.einsum('bhs,bhsd,bhse->bhde', w_s, kc, vc)
        n = w_c[..., None] * n + jnp.einsum('bhs,bhsd->bhd', w_s, kc)
        return (C, n, m_new), h

    init = (jnp.zeros((Bsz, H, Dh, Dh), F32), jnp.zeros((Bsz, H, Dh), F32),
            jnp.full((Bsz, H), M_INIT, F32))
    _, hs = lax.scan(step, init, (chunks(q), chunks(k), chunks(v), chunks(ig), chunks(lf)))
    hs = jnp.moveaxis(jnp.moveaxis(hs, 2, 3), 0, 1)
    return hs.reshape(Bsz, S, H, Dh)

def _mlstm(q, k, v, o, gates, gate_bias, norm_g):
    Bsz, S, _ = q.shape
    shp = (Bsz, S, MLSTM_HEADS, MLSTM_DH)
    q, k, v = q.reshape(shp), k.reshape(shp) * (MLSTM_DH ** -0.5), v.reshape(shp)
    gt = gates.reshape(Bsz, S, 4, MLSTM_HEADS).astype(F32) + gate_bias
    ig_f, lf_f = gt[:, :, 0], jax.nn.log_sigmoid(gt[:, :, 1])
    ig_b, lf_b = gt[:, :, 2], jax.nn.log_sigmoid(gt[:, :, 3])
    flip = lambda t: jnp.flip(t, axis=1)
    h = (_mlstm_scan(q, k, v, ig_f, lf_f)
         + flip(_mlstm_scan(flip(q), flip(k), flip(v), flip(ig_b), flip(lf_b))))
    mu = jnp.mean(h, -1, keepdims=True)
    var = jnp.mean(jnp.square(h - mu), -1, keepdims=True)
    hn = (h - mu) * lax.rsqrt(var + 1e-5) * norm_g.reshape(MLSTM_HEADS, MLSTM_DH)
    y = jax.nn.sigmoid(o.reshape(shp).astype(F32)) * hn
    return y.reshape(Bsz, S, MLSTM_W)

def _ssd_scan(x, dt, A, Bm, Cm):
    Bsz, S, G, E, P = x.shape
    N = Bm.shape[-1]
    L = SSD_CHUNK
    nc = S // L

    def chunks(t):
        return jnp.moveaxis(t.reshape((Bsz, nc, L) + t.shape[2:]), 1, 0)

    mask = jnp.tril(jnp.ones((L, L), bool))[None, :, :, None, None]

    def step(state, inp):
        xc, dtc, Bc, Cc = inp
        cs = jnp.cumsum(dtc * A, axis=1)
        Lm = jnp.exp(jnp.where(mask, cs[:, :, None] - cs[:, None, :], -jnp.inf))
        CB = jnp.einsum('btgn,bsgn->btsg', Cc, Bc)
        xdt = xc * dtc[..., None]
        y = jnp.einsum('btsg,btsge,bsgep->btgep', CB, Lm, xdt)
        y = y + jnp.einsum('btgn,bgepn->btgep', Cc, state) * jnp.exp(cs)[..., None]
        decay_end = jnp.exp(cs[:, -1:] - cs)
        state = (jnp.exp(cs[:, -1])[..., None, None] * state
                 + jnp.einsum('bsgn,bsge,bsgep->bgepn', Bc, decay_end, xdt))
        return state, y

    init = jnp.zeros((Bsz, G, E, P, N), F32)
    _, ys = lax.scan(step, init, (chunks(x), chunks(dt), chunks(Bm), chunks(Cm)))
    return jnp.moveaxis(ys, 0, 1).reshape(Bsz, S, G, E, P)

def _ssd(z, xbc, dt_raw, conv_w, conv_b, dt_bias, a_log, d_skip, norm_g):
    Bsz, S, Cdim = xbc.shape
    pad = SSD_CONV // 2
    xbc = lax.conv_general_dilated(xbc, conv_w[:, None, :], window_strides=(1,),
                                   padding=((pad, pad),), dimension_numbers=('NWC', 'WIO', 'NWC'),
                                   feature_group_count=Cdim) + conv_b
    xbc = jax.nn.silu(xbc)
    xs, Bm, Cm = _split(xbc, (SSD_INNER, SSD_GROUPS * SSD_STATE, SSD_GROUPS * SSD_STATE))
    x = xs.reshape(Bsz, S, SSD_GROUPS, SSD_HPG, SSD_HEADDIM)
    Bm = Bm.reshape(Bsz, S, SSD_GROUPS, SSD_STATE)
    Cm = Cm.reshape(Bsz, S, SSD_GROUPS, SSD_STATE)
    dt = jax.nn.softplus(dt_raw.reshape(Bsz, S, 2, SSD_GROUPS, SSD_HPG).astype(F32)
                         + dt_bias.reshape(2, SSD_GROUPS, SSD_HPG))
    A = -jnp.exp(a_log.astype(F32)).reshape(2, SSD_GROUPS, SSD_HPG)
    flip = lambda t: jnp.flip(t, axis=1)
    y = (_ssd_scan(x, dt[:, :, 0], A[0], Bm, Cm)
         + flip(_ssd_scan(flip(x), flip(dt[:, :, 1]), A[1], flip(Bm), flip(Cm)))
         + x * d_skip.reshape(SSD_GROUPS, SSD_HPG)[..., None])
    y = y.reshape(Bsz, S, SSD_INNER) * jax.nn.silu(z.astype(F32))
    y = _rmsnorm(y.reshape(Bsz, S, SSD_GROUPS, SSD_INNER // SSD_GROUPS),
                 norm_g.reshape(SSD_GROUPS, SSD_INNER // SSD_GROUPS))
    return y.reshape(Bsz, S, SSD_INNER)

def _hier_moe(x, wg, bg, we, be, w_gate, w_up, w_down):
    glog = (jnp.einsum('bsd,dg->bsg', x, wg) + bg).astype(F32)
    gp, gi = lax.top_k(jax.nn.softmax(glog, -1), 1)
    elog = (jnp.einsum('bsd,gde->bsge', x, we) + be).astype(F32)
    elog = jnp.einsum('bsge,bsg->bse', elog, jax.nn.one_hot(gi[..., 0], N_GROUPS, dtype=F32))
    ep, ei = lax.top_k(jax.nn.softmax(elog, -1), TOP_K)
    ep = ep / jnp.sum(ep, -1, keepdims=True)
    eid = gi * EXPERTS_PER_GROUP + ei
    combine = jnp.sum(jax.nn.one_hot(eid, N_EXPERTS, dtype=F32) * (gp * ep)[..., None], axis=2)
    h = jax.nn.silu(jnp.einsum('bsd,edf->bsef', x, w_gate)) * jnp.einsum('bsd,edf->bsef', x, w_up)
    h = h * combine[..., None].astype(h.dtype)
    return jnp.einsum('bsef,efd->bsd', h, w_down)

def first_inputs(seed: int = 0) -> dict:
    key = jax.random.key(seed)
    ks = jax.random.split(key, 32)
    nrm = lambda k, shape, s: jax.random.normal(k, shape, F32) * s
    gain = lambda k, shape: 1.0 + 0.02 * jax.random.normal(k, shape, F32)

    x = jax.random.normal(ks[0], (BATCH, SEQ, D_MODEL), F32)
    positions = (jax.random.randint(ks[1], (BATCH, 1), 0, POS_MAX_OFFSET, dtype=jnp.int32)
                 + jnp.arange(SEQ, dtype=jnp.int32)[None, :])

    w_in = nrm(ks[2], (DEPTH, D_MODEL, IN_WIDTH), D_MODEL ** -0.5)
    mla_q_norm = gain(ks[3], (DEPTH, MLA_Q_RANK))
    mla_kv_norm = gain(ks[4], (DEPTH, MLA_KV_RANK))
    mla_w_uq = nrm(ks[5], (DEPTH, MLA_Q_RANK, MLA_HEADS * (MLA_NOPE + MLA_ROPE)), MLA_Q_RANK ** -0.5)
    mla_w_ukv = nrm(ks[6], (DEPTH, MLA_KV_RANK, MLA_HEADS * (MLA_NOPE + MLA_V)), MLA_KV_RANK ** -0.5)

    lin = jnp.linspace(3.0, 6.0, MLSTM_HEADS, dtype=F32)
    zer = jnp.zeros((MLSTM_HEADS,), F32)
    mlstm_gate_bias = jnp.stack([zer, lin, zer, lin])[None] + nrm(ks[7], (DEPTH, 4, MLSTM_HEADS), 0.1)
    mlstm_norm = gain(ks[8], (DEPTH, MLSTM_W))

    ssd_conv_w = nrm(ks[9], (DEPTH, SSD_CONV, SSD_CONV_DIM), SSD_CONV ** -0.5)
    ssd_conv_b = nrm(ks[10], (DEPTH, SSD_CONV_DIM), 0.01)
    dt0 = jnp.exp(jax.random.uniform(ks[11], (DEPTH, 2, SSD_HEADS), F32, math.log(1e-3), math.log(1e-1)))
    ssd_dt_bias = dt0 + jnp.log(-jnp.expm1(-dt0))
    ssd_a_log = jnp.log(jax.random.uniform(ks[12], (DEPTH, 2, SSD_HEADS), F32, 1.0, 16.0))
    ssd_d = gain(ks[13], (DEPTH, SSD_HEADS))
    ssd_norm = gain(ks[14], (DEPTH, SSD_INNER))

    w_out = nrm(ks[15], (DEPTH, MIX_WIDTH, D_MODEL), MIX_WIDTH ** -0.5 * DEEPNORM_BETA)
    ln1_g = gain(ks[16], (DEPTH, D_MODEL))
    ln1_b = nrm(ks[17], (DEPTH, D_MODEL), 0.02)

    router_group_w = nrm(ks[18], (DEPTH, D_MODEL, N_GROUPS), D_MODEL ** -0.5)
    router_group_b = nrm(ks[19], (DEPTH, N_GROUPS), 0.01)
    router_expert_w = nrm(ks[20], (DEPTH, N_GROUPS, D_MODEL, EXPERTS_PER_GROUP), D_MODEL ** -0.5)
    router_expert_b = nrm(ks[21], (DEPTH, N_GROUPS, EXPERTS_PER_GROUP), 0.01)
    expert_w_gate = nrm(ks[22], (DEPTH, N_EXPERTS, D_MODEL, D_EXPERT), D_MODEL ** -0.5)
    expert_w_up = nrm(ks[23], (DEPTH, N_EXPERTS, D_MODEL, D_EXPERT), D_MODEL ** -0.5)
    expert_w_down = nrm(ks[24], (DEPTH, N_EXPERTS, D_EXPERT, D_MODEL), D_EXPERT ** -0.5 * DEEPNORM_BETA)
    ln2_g = gain(ks[25], (DEPTH, D_MODEL))
    ln2_b = nrm(ks[26], (DEPTH, D_MODEL), 0.02)

    return {"x": x, "positions": positions, "w_in": w_in,
            "mla_q_norm": mla_q_norm, "mla_kv_norm": mla_kv_norm,
            "mla_w_uq": mla_w_uq, "mla_w_ukv": mla_w_ukv,
            "mlstm_gate_bias": mlstm_gate_bias, "mlstm_norm": mlstm_norm,
            "ssd_conv_w": ssd_conv_w, "ssd_conv_b": ssd_conv_b, "ssd_dt_bias": ssd_dt_bias,
            "ssd_a_log": ssd_a_log, "ssd_d": ssd_d, "ssd_norm": ssd_norm,
            "w_out": w_out, "ln1_g": ln1_g, "ln1_b": ln1_b,
            "router_group_w": router_group_w, "router_group_b": router_group_b,
            "router_expert_w": router_expert_w, "router_expert_b": router_expert_b,
            "expert_w_gate": expert_w_gate, "expert_w_up": expert_w_up, "expert_w_down": expert_w_down,
            "ln2_g": ln2_g, "ln2_b": ln2_b}

def first_block(x, positions, w_in, mla_q_norm, mla_kv_norm, mla_w_uq, mla_w_ukv,
              mlstm_gate_bias, mlstm_norm, ssd_conv_w, ssd_conv_b, ssd_dt_bias,
              ssd_a_log, ssd_d, ssd_norm, w_out, ln1_g, ln1_b,
              router_group_w, router_group_b, router_expert_w, router_expert_b,
              expert_w_gate, expert_w_up, expert_w_down, ln2_g, ln2_b):
    dtype = x.dtype
    cos, sin = _rope_table(positions)
    for l in range(DEPTH):
        p = jnp.einsum('bsd,dc->bsc', x, w_in[l])
        (c_q, c_kv, k_r, m_q, m_k, m_v, m_o, m_g, s_z, s_xbc, s_dt) = _split(p, IN_SIZES)
        y_a = _mla(c_q, c_kv, k_r, cos, sin, mla_q_norm[l], mla_kv_norm[l], mla_w_uq[l], mla_w_ukv[l])
        y_b = _mlstm(m_q, m_k, m_v, m_o, m_g, mlstm_gate_bias[l], mlstm_norm[l])
        y_c = _ssd(s_z, s_xbc, s_dt, ssd_conv_w[l], ssd_conv_b[l], ssd_dt_bias[l],
                   ssd_a_log[l], ssd_d[l], ssd_norm[l])
        heads = jnp.concatenate([y_a.astype(dtype), y_b.astype(dtype), y_c.astype(dtype)], -1)
        mix = jnp.einsum('bsc,cd->bsd', heads, w_out[l])
        x = _layernorm(DEEPNORM_ALPHA * x + mix, ln1_g[l], ln1_b[l]).astype(dtype)
        ffn = _hier_moe(x, router_group_w[l], router_group_b[l], router_expert_w[l], router_expert_b[l],
                        expert_w_gate[l], expert_w_up[l], expert_w_down[l]).astype(dtype)
        x = _layernorm(DEEPNORM_ALPHA * x + ffn, ln2_g[l], ln2_b[l]).astype(dtype)
    return x


HEAD_DIM = 64
MOBA_HEADS = 4
DIFF_HEADS = 4
DSA_HEADS = 4
DIFF_V_DIM = 2 * HEAD_DIM
IDX_HEADS = 8
IDX_DIM = 64
MOBA_BLOCK = 256
MOBA_TOPK = 3
DSA_TOPK_MAX = 256
ROPE_THETA = 10000.0
EPS = 1e-6
MOBA_Q_CHUNK = 32
D_FF = -(-8 * D_MODEL // (3 * 256)) * 256

MOBA_W = MOBA_HEADS * HEAD_DIM
DIFF_QK_W = DIFF_HEADS * 2 * HEAD_DIM
DIFF_V_W = DIFF_HEADS * DIFF_V_DIM
DSA_W = DSA_HEADS * HEAD_DIM
IDX_Q_W = IDX_HEADS * IDX_DIM
MIX_W = MOBA_W + DIFF_V_W + DSA_W
IN_COLS = 3 * MOBA_W + 2 * DIFF_QK_W + DIFF_V_W + 3 * DSA_W + IDX_Q_W + IDX_DIM + IDX_HEADS


def rms_norm(x, g):
    xf = x.astype(jnp.float32)
    y = xf * lax.rsqrt(jnp.mean(xf * xf, axis=-1, keepdims=True) + EPS)
    return (y * g.astype(jnp.float32)).astype(x.dtype)

def rope_tables(seq, dim):
    inv = 1.0 / (ROPE_THETA ** (jnp.arange(0, dim, 2, dtype=jnp.float32) / dim))
    ang = jnp.arange(seq, dtype=jnp.float32)[:, None] * inv[None, :]
    return jnp.cos(ang), jnp.sin(ang)

def apply_rope(x, cos, sin):
    x1, x2 = jnp.split(x, 2, axis=-1)
    c = cos.astype(x.dtype)
    s = sin.astype(x.dtype)
    return jnp.concatenate([x1 * c - x2 * s, x1 * s + x2 * c], axis=-1)

def split_heads(t, n_heads):
    b, s, _ = t.shape
    return t.reshape(b, s, n_heads, -1).transpose(0, 2, 1, 3)

def merge_heads(t):
    b, h, s, d = t.shape
    return t.transpose(0, 2, 1, 3).reshape(b, s, h * d)

def moba_attention(q, k, v):
    B, H, S, D = q.shape
    nb = -(-S // MOBA_BLOCK)
    pad = nb * MOBA_BLOCK - S
    kb = jnp.pad(k, ((0, 0), (0, 0), (0, pad), (0, 0))).reshape(B, H, nb, MOBA_BLOCK, D)
    vb = jnp.pad(v, ((0, 0), (0, 0), (0, pad), (0, 0))).reshape(B, H, nb, MOBA_BLOCK, D)
    k_mean = jnp.mean(kb.astype(jnp.float32), axis=3).astype(k.dtype)
    n_sel = min(MOBA_TOPK, nb - 1)
    scale = D ** -0.5
    blk_ids = jnp.arange(nb)
    own_off = jnp.arange(MOBA_BLOCK)
    gather = jax.vmap(jax.vmap(lambda t, i: t[i]))

    def chunk(i):
        start = i * MOBA_Q_CHUNK
        qc = lax.dynamic_slice_in_dim(q, start, MOBA_Q_CHUNK, axis=2)
        qpos = start + jnp.arange(MOBA_Q_CHUNK)
        cur = start // MOBA_BLOCK
        k_own = lax.dynamic_index_in_dim(kb, cur, axis=2, keepdims=False)
        v_own = lax.dynamic_index_in_dim(vb, cur, axis=2, keepdims=False)
        own_pos = cur * MOBA_BLOCK + own_off
        s_own = jnp.einsum('bhcd,bhkd->bhck', qc, k_own).astype(jnp.float32) * scale
        s_own = jnp.where(own_pos[None, :] <= qpos[:, None], s_own, -jnp.inf)
        if n_sel == 0:
            p_own = jax.nn.softmax(s_own, axis=-1).astype(v.dtype)
            return jnp.einsum('bhck,bhkd->bhcd', p_own, v_own)
        gate = jnp.einsum('bhcd,bhnd->bhcn', qc, k_mean).astype(jnp.float32)
        gate = jnp.where(blk_ids < cur, gate, -jnp.inf)
        _, sel = lax.top_k(gate, n_sel)
        sel_ok = jnp.arange(n_sel) < cur
        k_sel = gather(kb, sel)
        v_sel = gather(vb, sel)
        s_sel = jnp.einsum('bhcd,bhcnkd->bhcnk', qc, k_sel).astype(jnp.float32) * scale
        s_sel = jnp.where(sel_ok[:, None], s_sel, -jnp.inf).reshape(B, H, MOBA_Q_CHUNK, n_sel * MOBA_BLOCK)
        p = jax.nn.softmax(jnp.concatenate([s_sel, s_own], axis=-1), axis=-1).astype(v.dtype)
        p_sel = p[..., :n_sel * MOBA_BLOCK].reshape(B, H, MOBA_Q_CHUNK, n_sel, MOBA_BLOCK)
        p_own = p[..., n_sel * MOBA_BLOCK:]
        return (jnp.einsum('bhcnk,bhcnkd->bhcd', p_sel, v_sel)
                + jnp.einsum('bhck,bhkd->bhcd', p_own, v_own))

    out = lax.map(chunk, jnp.arange(S // MOBA_Q_CHUNK))
    return out.transpose(1, 2, 0, 3, 4).reshape(B, H, S, D)

def diff_attention(q1, q2, k1, k2, v, lam):
    B, H, S, D = q1.shape
    scale = D ** -0.5
    kpos = jnp.arange(S)

    def block(i):
        start = i * Q_BLOCK
        qpos = start + jnp.arange(Q_BLOCK)
        mask = kpos[None, :] <= qpos[:, None]

        def probs(qf, kf):
            qb = lax.dynamic_slice_in_dim(qf, start, Q_BLOCK, axis=2)
            s = jnp.einsum('bhqd,bhkd->bhqk', qb, kf).astype(jnp.float32) * scale
            return jax.nn.softmax(jnp.where(mask, s, -jnp.inf), axis=-1)

        a = probs(q1, k1) - lam * probs(q2, k2)
        return jnp.einsum('bhqk,bhkv->bhqv', a.astype(v.dtype), v)

    out = lax.map(block, jnp.arange(S // Q_BLOCK))
    return out.transpose(1, 2, 0, 3, 4).reshape(B, H, S, v.shape[-1])

def dsa_attention(q, k, v, iq, ik, iw):
    B, H, S, D = q.shape
    n_top = min(DSA_TOPK_MAX, S // 4)
    scale = D ** -0.5
    kpos = jnp.arange(S)
    gather = jax.vmap(lambda t, i: t[:, i])

    def chunk(i):
        start = i * Q_BLOCK
        qpos = start + jnp.arange(Q_BLOCK)
        iqc = lax.dynamic_slice_in_dim(iq, start, Q_BLOCK, axis=2)
        iwc = lax.dynamic_slice_in_dim(iw, start, Q_BLOCK, axis=1)
        logits = jnp.einsum('bhcd,bsd->bhcs', iqc, ik).astype(jnp.float32) * (IDX_DIM ** -0.5)
        score = jnp.einsum('bch,bhcs->bcs', iwc.astype(jnp.float32), jax.nn.relu(logits))
        score = jnp.where(kpos[None, :] <= qpos[:, None], score, -jnp.inf)
        _, sel = lax.top_k(score, n_top)
        sel_ok = sel <= qpos[None, :, None]
        qc = lax.dynamic_slice_in_dim(q, start, Q_BLOCK, axis=2)
        k_sel = gather(k, sel)
        v_sel = gather(v, sel)
        s = jnp.einsum('bhcd,bhcnd->bhcn', qc, k_sel).astype(jnp.float32) * scale
        s = jnp.where(sel_ok[:, None], s, -jnp.inf)
        p = jax.nn.softmax(s, axis=-1).astype(v.dtype)
        return jnp.einsum('bhcn,bhcnd->bhcd', p, v_sel)

    out = lax.map(chunk, jnp.arange(S // Q_BLOCK))
    return out.transpose(1, 2, 0, 3, 4).reshape(B, H, S, D)

def second_inputs(seed: int = 0) -> dict:
    key = jax.random.key(seed)
    ks = jax.random.split(key, 12)
    f32 = jnp.float32

    def nrm(k, shape, scale):
        return jax.random.normal(k, shape, f32) * scale

    return {
        "x": nrm(ks[0], (BATCH, SEQ, D_MODEL), 1.0),
        "attn_norm_g": 1.0 + nrm(ks[1], (DEPTH, D_MODEL), 0.05),
        "w_in": nrm(ks[2], (DEPTH, D_MODEL, IN_COLS), D_MODEL ** -0.5),
        "q_norm_g": 1.0 + nrm(ks[3], (DEPTH, 3, HEAD_DIM), 0.05),
        "k_norm_g": 1.0 + nrm(ks[4], (DEPTH, 3, HEAD_DIM), 0.05),
        "diff_lambda": nrm(ks[5], (DEPTH, 4, HEAD_DIM), 0.1),
        "diff_subln_g": 1.0 + nrm(ks[6], (DEPTH, DIFF_V_DIM), 0.05),
        "w_out": nrm(ks[7], (DEPTH, MIX_W, D_MODEL), MIX_W ** -0.5),
        "ffn_norm_g": 1.0 + nrm(ks[8], (DEPTH, D_MODEL), 0.05),
        "w_gate": nrm(ks[9], (DEPTH, D_MODEL, D_FF), D_MODEL ** -0.5),
        "w_up": nrm(ks[10], (DEPTH, D_MODEL, D_FF), D_MODEL ** -0.5),
        "w_down": nrm(ks[11], (DEPTH, D_FF, D_MODEL), D_FF ** -0.5),
    }

def second_block(x, attn_norm_g, w_in, q_norm_g, k_norm_g, diff_lambda, diff_subln_g,
              w_out, ffn_norm_g, w_gate, w_up, w_down):
    S = x.shape[1]
    cos, sin = rope_tables(S, HEAD_DIM)
    sizes = [MOBA_W] * 3 + [DIFF_QK_W, DIFF_QK_W, DIFF_V_W] + [DSA_W] * 3 + [IDX_Q_W, IDX_DIM, IDX_HEADS]
    offsets = []
    acc = 0
    for sz in sizes[:-1]:
        acc += sz
        offsets.append(acc)

    for l in range(DEPTH):
        h = rms_norm(x, attn_norm_g[l])
        proj = h @ w_in[l]
        (mq, mk, mv, dq, dk, dv, sq, sk, sv, iq, ik, iw) = jnp.split(proj, offsets, axis=-1)
        qg, kg = q_norm_g[l], k_norm_g[l]

        def qk(t, nh, g):
            return apply_rope(rms_norm(split_heads(t, nh), g), cos, sin)

        moba = moba_attention(qk(mq, MOBA_HEADS, qg[0]), qk(mk, MOBA_HEADS, kg[0]),
                              split_heads(mv, MOBA_HEADS))

        dq_h = qk(dq, 2 * DIFF_HEADS, qg[1])
        dk_h = qk(dk, 2 * DIFF_HEADS, kg[1])
        lam_init = 0.8 - 0.6 * math.exp(-0.3 * l)
        lp = diff_lambda[l].astype(jnp.float32)
        lam = jnp.exp(jnp.sum(lp[0] * lp[1])) - jnp.exp(jnp.sum(lp[2] * lp[3])) + lam_init
        diff = diff_attention(dq_h[:, 0::2], dq_h[:, 1::2], dk_h[:, 0::2], dk_h[:, 1::2],
                              split_heads(dv, DIFF_HEADS), lam)
        diff = rms_norm(diff, diff_subln_g[l]) * (1.0 - lam_init)

        iq_h = apply_rope(split_heads(iq, IDX_HEADS), cos, sin)
        ik_r = apply_rope(ik, cos, sin)
        dsa = dsa_attention(qk(sq, DSA_HEADS, qg[2]), qk(sk, DSA_HEADS, kg[2]),
                            split_heads(sv, DSA_HEADS), iq_h, ik_r,
                            iw * (IDX_HEADS ** -0.5))

        mix = jnp.concatenate([merge_heads(moba), merge_heads(diff), merge_heads(dsa)], axis=-1)
        x = x + mix @ w_out[l]

        h2 = rms_norm(x, ffn_norm_g[l])
        x = x + (jax.nn.silu(h2 @ w_gate[l]) * (h2 @ w_up[l])) @ w_down[l]
    return x


def setup_inputs(seed=0):
    out = dict(first_inputs(seed))
    for name, value in second_inputs(seed + 1).items():
        if name != "x":
            out[name + "_2"] = value
    return out


def reference(
    x, positions, w_in, mla_q_norm, mla_kv_norm, mla_w_uq, mla_w_ukv, mlstm_gate_bias,
    mlstm_norm, ssd_conv_w, ssd_conv_b, ssd_dt_bias, ssd_a_log, ssd_d, ssd_norm, w_out, ln1_g,
    ln1_b, router_group_w, router_group_b, router_expert_w, router_expert_b, expert_w_gate,
    expert_w_up, expert_w_down, ln2_g, ln2_b, attn_norm_g_2, w_in_2, q_norm_g_2, k_norm_g_2,
    diff_lambda_2, diff_subln_g_2, w_out_2, ffn_norm_g_2, w_gate_2, w_up_2, w_down_2,
):
    x = first_block(
        x, positions, w_in, mla_q_norm, mla_kv_norm, mla_w_uq, mla_w_ukv, mlstm_gate_bias,
        mlstm_norm, ssd_conv_w, ssd_conv_b, ssd_dt_bias, ssd_a_log, ssd_d, ssd_norm, w_out,
        ln1_g, ln1_b, router_group_w, router_group_b, router_expert_w, router_expert_b,
        expert_w_gate, expert_w_up, expert_w_down, ln2_g, ln2_b,
    )
    return second_block(
        x, attn_norm_g_2, w_in_2, q_norm_g_2, k_norm_g_2, diff_lambda_2, diff_subln_g_2,
        w_out_2, ffn_norm_g_2, w_gate_2, w_up_2, w_down_2,
    )


_drawn_inputs = setup_inputs


def setup_inputs(seed=0):
    import zlib

    import numpy as np

    out = dict(_drawn_inputs(seed))
    spreads = {}
    factors = {'mla_q_norm': 8.0,
     'mla_kv_norm': 8.0,
     'mlstm_norm': 6.533,
     'ssd_conv_b': 3.964,
     'ssd_d': 8.0,
     'ssd_norm': 4.462,
     'router_group_b': 5.733,
     'router_expert_b': 7.81}
    for name, (base, spread) in spreads.items():
        noise = np.random.default_rng([zlib.crc32(name.encode()), seed]).standard_normal(out[name].shape)
        drawn = base * np.exp(spread * noise) if base else spread * noise
        out[name] = __import__('jax').numpy.asarray(drawn.astype(out[name].dtype))
    for name, factor in factors.items():
        out[name] = (out[name] * factor).astype(out[name].dtype)
    return out
```

```python
from contextlib import ExitStack, contextmanager

import numpy as np

import concourse.bass as bass
from concourse import mybir

F32 = mybir.dt.float32
I32 = mybir.dt.int32
ALU = mybir.AluOpType
ACT = mybir.ActivationFunctionType
AX = mybir.AxisListType.X

P = 128
S = 512
T = S // P
D = 1024
KD = D // P
DEPTH = 2
BANK = 512
NBANK = 8
MASKED = -1e30
ALPHA = (2 * DEPTH) ** 0.25

MLA_H, NOPE, ROPE, MLA_V = 8, 64, 32, 64
QK = NOPE + ROPE
Q_RANK, KV_RANK = 256, 128
ML_H, ML_D = 4, 64
SSD_H, SSD_P, SSD_G, SSD_N, CONV = 4, 64, 2, 128, 5
PAD = CONV // 2
CQ = 0
CKV = CQ + Q_RANK
KR = CKV + KV_RANK
MQ = KR + ROPE
MK = MQ + ML_H * ML_D
MV = MK + ML_H * ML_D
MO = MV + ML_H * ML_D
MG = MO + ML_H * ML_D
SZ = MG + 4 * ML_H
XBC = SZ + SSD_H * SSD_P
NXBC = SSD_H * SSD_P + 2 * SSD_G * SSD_N
SDT = XBC + NXBC
IN1 = SDT + 2 * SSD_H
CC = NXBC // P
GROUPS, PER_GROUP = 4, 4
EXPERTS = GROUPS * PER_GROUP
NR = GROUPS + EXPERTS
F_CH = 256

V_Q, V_KV, V_GB, V_MN, V_DTB, V_AL, V_SD, V_SN, V_RB = np.cumsum(
    [0, Q_RANK, KV_RANK, 4 * ML_H, ML_H * ML_D, 2 * SSD_H, 2 * SSD_H, SSD_H, SSD_H * SSD_P]).tolist()
NV1 = V_RB + NR

HD = 64
HALF = HD // 2
B_MQ, B_MK, B_MV, B_DQ, B_DK, B_DV, B_SQ, B_SK, B_SV, B_IQ, B_IK, B_IW, IN2 = np.cumsum(
    [0, 256, 256, 256, 512, 512, 512, 256, 256, 256, 512, 64, 8]).tolist()
IDX_H = 8
N_TOP = min(256, S // 4)
D_FF = 2816
FF_CH = D_FF // F_CH
V2_Q, V2_K, V2_L, V2_S = 0, 192, 384, 640
NV2 = 768

K_ID, K_GE, K_LE, K_CAUSAL, K_COS, K_SIN, K_INV, K_LAM = np.cumsum(
    [0, P, P, P, P, T * HALF, T * HALF, ROPE // 2]).tolist()
NK = K_LAM + 2 * DEPTH


class Env:

    def __init__(self, nc):
        self.nc, self.ctx, self.sems = nc, None, {}

    def sem(self, stage, name):
        key = f"{stage}_{name}"
        if key not in self.sems:
            self.sems[key] = self.ctx.enter_context(self.nc.semaphore(key))
        return self.sems[key]

    @contextmanager
    def semaphores(self):
        with ExitStack() as ctx:
            self.ctx, self.sems = ctx, {}
            yield

    def end_layer(self):
        nums = [s.num for s in self.sems.values()]
        self.nc.all_engine_barrier(sems_to_clear=range(min(nums), max(nums) + 1))


class Link:

    def __init__(self, eng, sem):
        self.eng, self.sem, self.n = eng, sem, 0

    def __call__(self, ins):
        ins.then_inc(self.sem, 1)
        self.n += 1
        self.eng.wait_ge(self.sem, self.n)


def per_tile(ap, width):
    return ap.unsqueeze(2).to_broadcast([ap.shape[0], ap.shape[1], width])



def transpose_stage(env, stage, jobs):
    nc, ps, ident = env.nc, env.ps, env.ident
    turned = env.sem(stage, "turned")
    act_copied, dve_copied = env.sem(stage, "act_copied"), env.sem(stage, "dve_copied")

    with nc.Block() as block:
        @block.tensor
        def _(pe):
            for i, (srcs, dst, scale) in enumerate(jobs):
                if i >= NBANK:
                    pe.wait_ge(dve_copied if i % 2 else act_copied, (i - NBANK) // 2 + 1)
                for j, src in enumerate(srcs):
                    w = src.shape[1]
                    last = nc.tensor.transpose(ps[0:w, i % NBANK, j * P:(j + 1) * P], src, ident)
                last.then_inc(turned, 1)

        def copy_out(eng, i):
            srcs, dst, scale = jobs[i]
            w, n = srcs[0].shape[1], len(srcs) * P
            src = ps[0:w, i % NBANK, 0:n]
            eng.wait_ge(turned, i + 1)
            return src, dst, scale

        @block.scalar
        def _(act):
            for i in range(0, len(jobs), 2):
                src, dst, scale = copy_out(act, i)
                nc.scalar.activation(dst, src, ACT.Copy if scale is None else ACT.Identity,
                                     scale=1.0 if scale is None else scale).then_inc(act_copied, 1)

        @block.vector
        def _(dve):
            for i in range(1, len(jobs), 2):
                src, dst, scale = copy_out(dve, i)
                if scale is None:
                    nc.vector.tensor_copy(dst, src).then_inc(dve_copied, 1)
                else:
                    nc.vector.tensor_scalar(dst, src, scale, None, ALU.mult).then_inc(dve_copied, 1)


def project_stage(env, stage, jobs, alpha_x=None):
    nc, ps, ring = env.nc, env.ps, env.ring
    slots = env.slots
    loaded = [env.sem(stage, f"weights_loaded{s}") for s in range(slots)]
    summed = env.sem(stage, "summed")
    act_done, dve_done = env.sem(stage, "act_stored"), env.sem(stage, "dve_stored")

    def slot(c, k, w):
        return ring[:, c % slots, 0:k * w].rearrange("p (k w) -> p k w", k=k)

    with nc.Block() as block:
        @block.sync
        def _(sp):
            for c, (lhs, weights, pieces) in enumerate(jobs):
                if c >= slots:
                    sp.wait_ge(summed, T * (c - slots + 1))
                k, w = len(lhs), weights.shape[-1]
                src = weights.rearrange("(k p) w -> p k w", p=P)
                sp.dma_start(slot(c, k, w), src).then_inc(loaded[c % slots], 16)

        @block.tensor
        def _(pe):
            for c, (lhs, weights, pieces) in enumerate(jobs):
                pe.wait_ge(loaded[c % slots], 16 * (c // slots + 1))
                k, w = len(lhs), weights.shape[-1]
                for t in range(T):
                    i = c * T + t
                    if i >= NBANK:
                        if alpha_x is not None:
                            pe.wait_ge(dve_done, i - NBANK + 1)
                        else:
                            pe.wait_ge(dve_done if i % 2 else act_done, (i - NBANK) // 2 + 1)
                    for kk in range(k):
                        last = nc.tensor.matmul(ps[:, i % NBANK, 0:w], lhs[kk][:, t * P:(t + 1) * P],
                                                slot(c, k, w)[:, kk, :], start=(kk == 0), stop=(kk == k - 1))
                    last.then_inc(summed, 1)

        @block.scalar
        def _(act):
            if alpha_x is not None:
                return
            for i in range(0, len(jobs) * T, 2):
                act.wait_ge(summed, i + 1)
                for view, dst in jobs[i // T][2]:
                    last = nc.scalar.activation(dst(i % T), view(ps[:, i % NBANK, :]), ACT.Copy)
                last.then_inc(act_done, 1)

        @block.vector
        def _(dve):
            for i in range(0 if alpha_x is not None else 1, len(jobs) * T, 1 if alpha_x is not None else 2):
                dve.wait_ge(summed, i + 1)
                for view, dst in jobs[i // T][2]:
                    d, src = dst(i % T), view(ps[:, i % NBANK, :])
                    if alpha_x is None:
                        last = nc.vector.tensor_copy(d, src)
                    else:
                        last = nc.vector.scalar_tensor_tensor(out=d, in0=d, scalar=alpha_x, in1=src,
                                                              op0=ALU.mult, op1=ALU.add)
                last.then_inc(dve_done, 1)


def attention_stage(env, stage, units, scale):
    nc, ps, ident, causal = env.nc, env.ps, env.ident, env.causal
    N = len(units)
    scores_ready, max_ready = env.sem(stage, "scores_ready"), env.sem(stage, "max_ready")
    exp_done, turned = env.sem(stage, "exp_done"), env.sem(stage, "turned")
    turned_copied, out_ready = env.sem(stage, "turned_copied"), env.sem(stage, "out_ready")
    out_stored, step = env.sem(stage, "out_stored"), env.sem(stage, "vector_step")

    with ExitStack() as local:
        prob = local.enter_context(nc.sbuf_tensor(f"{stage}_prob", [P, 3, S], F32))
        prob_t = local.enter_context(nc.sbuf_tensor(f"{stage}_prob_t", [P, 2, S], F32))
        top = local.enter_context(nc.sbuf_tensor(f"{stage}_top", [P, N], F32))
        total = local.enter_context(nc.sbuf_tensor(f"{stage}_total", [P, N], F32))
        recip = local.enter_context(nc.sbuf_tensor(f"{stage}_recip", [P, N], F32))

        def score_bank(i, nk):
            return ps[:, i % 3, 0:nk]

        with nc.Block() as block:
            @block.tensor
            def _(pe):
                for i in range(N + 3):
                    if i < N:
                        u = units[i]
                        if i >= 3:
                            pe.wait_ge(exp_done, i - 2)
                        nc.tensor.matmul(score_bank(i, u["nk"]), u["q"], u["k"], start=True, stop=True
                                         ).then_inc(scores_ready, 1)
                    if 2 <= i < N + 2:
                        j = i - 2
                        pe.wait_ge(exp_done, j + 1)
                        if j >= 2:
                            pe.wait_ge(turned_copied, j - 1)
                        for b in range(units[j]["nk"] // P):
                            last = nc.tensor.transpose(ps[:, 3 + j % 2, b * P:(b + 1) * P],
                                                       prob[:, j % 3, b * P:(b + 1) * P], ident)
                        last.then_inc(turned, 1)
                    if i >= 3:
                        j = i - 3
                        u = units[j]
                        nb = u["nk"] // P
                        pe.wait_ge(turned_copied, j + 1)
                        if j >= 2:
                            pe.wait_ge(out_stored, j - 1)
                        for b in range(nb):
                            w = u["v"][b].shape[1]
                            last = nc.tensor.matmul(ps[:, 5 + j % 2, 0:w], prob_t[:, j % 2, b * P:(b + 1) * P],
                                                    u["v"][b], start=(b == 0), stop=(b == nb - 1))
                        last.then_inc(out_ready, 1)

            @block.vector
            def _(dve):
                link = Link(dve, step)
                for i in range(N + 3):
                    if i < N:
                        u = units[i]
                        dve.wait_ge(scores_ready, i + 1)
                        sc = score_bank(i, u["nk"])
                        if u["mask"] == "diag":
                            last = ps[:, i % 3, u["nk"] - P:u["nk"]]
                            link(nc.vector.tensor_tensor(last, last, causal, ALU.add))
                        elif u["mask"] is not None:
                            link(nc.vector.tensor_tensor(sc, sc, u["mask"], ALU.add))
                        link(nc.vector.reduce_max(top[:, i:i + 1], sc, AX))
                        nc.vector.tensor_scalar(top[:, i:i + 1], top[:, i:i + 1], -scale, None, ALU.mult
                                                ).then_inc(max_ready, 1)
                    if i >= 3:
                        j = i - 3
                        u = units[j]
                        dve.wait_ge(exp_done, j + 1)
                        link(nc.vector.reciprocal(recip[:, j:j + 1], total[:, j:j + 1]))
                        dve.wait_ge(out_ready, j + 1)
                        nc.vector.tensor_scalar(u["dst"], ps[:, 5 + j % 2, 0:u["dst"].shape[1]], recip[:, j:j + 1],
                                                None, ALU.mult).then_inc(out_stored, 1)

            @block.scalar
            def _(act):
                for i in range(N + 2):
                    if i < N:
                        u = units[i]
                        act.wait_ge(max_ready, i + 1)
                        if i >= 3:
                            act.wait_ge(turned, i - 2)
                        nc.scalar.activation(prob[:, i % 3, 0:u["nk"]], score_bank(i, u["nk"]), ACT.Exp,
                                             bias=top[:, i:i + 1], scale=scale,
                                             accum_out=total[:, i:i + 1]).then_inc(exp_done, 1)
                    if i >= 2:
                        j = i - 2
                        nk = units[j]["nk"]
                        act.wait_ge(turned, j + 1)
                        if j >= 2:
                            act.wait_ge(out_ready, j - 1)
                        nc.scalar.activation(prob_t[:, j % 2, 0:nk], ps[:, 3 + j % 2, 0:nk], ACT.Copy
                                             ).then_inc(turned_copied, 1)


def layernorm_stage(env, stage, gains, out_x):
    nc = env.nc
    gains_loaded, var_ready = env.sem(stage, "gains_loaded"), env.sem(stage, "var_ready")
    root_ready, centred = env.sem(stage, "root_ready"), env.sem(stage, "centred")
    scaled, step = env.sem(stage, "scaled"), env.sem(stage, "vector_step")
    with ExitStack() as local:
        gb = local.enter_context(nc.sbuf_tensor(f"{stage}_gb", [P, 2 * D], F32))
        st = local.enter_context(nc.sbuf_tensor(f"{stage}_stats", [P, T, 2, 6], F32))
        mv = local.enter_context(nc.sbuf_tensor(f"{stage}_mv", [P, T, 2], F32))
        rs = local.enter_context(nc.sbuf_tensor(f"{stage}_rs", [P, T], F32))
        with nc.Block() as block:
            @block.sync
            def _(sp):
                sp.dma_start(gb[:, :], gains.to_broadcast([P, 2 * D])).then_inc(gains_loaded, 16)

            @block.vector
            def _(dve):
                link = Link(dve, step)
                for t in range(T):
                    for h in range(2):
                        last = nc.vector.bn_stats(st[:, t, h, :], out_x[:, t, h * BANK:(h + 1) * BANK])
                link(last)
                for t in range(T):
                    last = nc.vector.bn_aggr(mv[:, t, :], st[:, t, :, :])
                last.then_inc(var_ready, 1)
                dve.wait_ge(root_ready, 1)
                link(nc.vector.reciprocal(rs[:, :], rs[:, :]))
                for t in range(T):
                    nc.vector.tensor_scalar(out_x[:, t, :], out_x[:, t, :], mv[:, t, 0:1], rs[:, t:t + 1],
                                            ALU.subtract, ALU.mult).then_inc(centred, 1)
                dve.wait_ge(gains_loaded, 16)
                for t in range(T):
                    dve.wait_ge(scaled, t + 1)
                    last = nc.vector.tensor_tensor(out_x[:, t, :], out_x[:, t, :], gb[:, D:2 * D], ALU.add)

            @block.scalar
            def _(act):
                act.wait_ge(var_ready, 1)
                nc.scalar.activation(rs[:, :], mv[:, :, 1], ACT.Sqrt, bias=env.eps5).then_inc(root_ready, 1)

            @block.gpsimd
            def _(pool):
                pool.wait_ge(gains_loaded, 16)
                for t in range(T):
                    pool.wait_ge(centred, t + 1)
                    nc.gpsimd.tensor_tensor(out_x[:, t, :], out_x[:, t, :], gb[:, 0:D], ALU.mult).then_inc(scaled, 1)


def hidden_stage(env, stage, xt, w_gate, w_up, chunks, hidden, combine=None):
    nc, ps, ident = env.nc, env.ps, env.ident
    FC = F_CH // P
    loaded = [env.sem(stage, f"weights_loaded{s}") for s in range(2)]
    summed, spread = env.sem(stage, "summed"), env.sem(stage, "combine_spread")
    gated, sized = env.sem(stage, "silu_done"), env.sem(stage, "times_up_done")
    stored = env.sem(stage, "hidden_stored")
    pairs = chunks // 2
    with ExitStack() as local:
        wg = local.enter_context(nc.sbuf_tensor(f"{stage}_wg", [P, 2, KD, F_CH], F32))
        wu = local.enter_context(nc.sbuf_tensor(f"{stage}_wu", [P, 2, KD, F_CH], F32))
        act_g = local.enter_context(nc.sbuf_tensor(f"{stage}_g", [P, 2, S], F32))
        gu = local.enter_context(nc.sbuf_tensor(f"{stage}_gu", [P, 2, S], F32))

        def load(sp, c, s, used):
            if used is not None:
                sp.wait_ge(summed, used)
            sp.dma_start(wg[:, s], w_gate(c)).then_inc(loaded[s], 16)
            sp.dma_start(wu[:, s], w_up(c)).then_inc(loaded[s], 16)

        def chunk_pe(pe, c, s, first, turn, comb_c):
            pe.wait_ge(loaded[s], turn * 32 + 32)
            for f in range(FC):
                if not first:
                    pe.wait_ge(stored, (c - 1) * FC + f + 1)
                if combine is not None and f == 0:
                    for t in range(T):
                        last = nc.tensor.matmul(ps[:, 4 + s, t * P:(t + 1) * P], comb_c(t), ident, start=True, stop=True)
                    last.then_inc(spread, 1)
                for b, w in ((f, wg), (2 + f, wu)):
                    for k in range(KD):
                        last = nc.tensor.matmul(ps[:, b, :], w[:, s, k, f * P:(f + 1) * P], xt[:, k, :],
                                                start=(k == 0), stop=(k == KD - 1))
                last.then_inc(summed, 1)

        def chunk_act(act, c, first):
            for f in range(FC):
                act.wait_ge(summed, c * FC + f + 1)
                if not first:
                    act.wait_ge(stored if combine is None else sized, (c - 1) * FC + f + 1)
                nc.scalar.activation(act_g[:, f, :], ps[:, f, :], ACT.Silu).then_inc(gated, 1)

        def chunk_dve(dve, c, s, dst):
            for f in range(FC):
                dve.wait_ge(gated, c * FC + f + 1)
                if combine is None:
                    nc.vector.tensor_tensor(dst(f), act_g[:, f, :], ps[:, 2 + f, :], ALU.mult).then_inc(stored, 1)
                else:
                    nc.vector.tensor_tensor(gu[:, f, :], act_g[:, f, :], ps[:, 2 + f, :], ALU.mult).then_inc(sized, 1)
                    dve.wait_ge(sized, c * FC + f + 1)
                    dve.wait_ge(spread, c + 1)
                    nc.vector.tensor_tensor(dst(f), gu[:, f, :], ps[:, 4 + s, :], ALU.mult).then_inc(stored, 1)

        def hid(c, f):
            if isinstance(c, int):
                return hidden[:, c * FC + f, :]
            return hidden[:, bass.ds(c * FC + f, 1), :].rearrange("p a n -> p (a n)")

        def comb(c):
            if combine is None:
                return None
            return lambda t: combine(t, c)

        with nc.Block() as block:
            @block.sync
            def _(sp):
                for c in range(chunks):
                    load(sp, c, c % 2, None if c < 2 else (c - 1) * FC)

            @block.tensor
            def _(pe):
                for c in range(chunks):
                    chunk_pe(pe, c, c % 2, c == 0, c // 2, comb(c))

            @block.scalar
            def _(act):
                for c in range(chunks):
                    chunk_act(act, c, c == 0)

            @block.vector
            def _(dve):
                for c in range(chunks):
                    chunk_dve(dve, c, c % 2, lambda f: hid(c, f))


def down_stage(env, stage, hidden, nf, w_down, x, alpha):
    nc, ps, ring, slots = env.nc, env.ps, env.ring, env.slots
    per = 4 if nf % 4 == 0 else 2
    loads = [(half, g) for half in range(2) for g in range(nf // per)]
    loaded = [env.sem(stage, f"weights_loaded{s}") for s in range(slots)]
    used, summed, stored = env.sem(stage, "weights_used"), env.sem(stage, "summed"), env.sem(stage, "stored")

    def slot(n):
        return ring[:, n % slots, 0:per * BANK].rearrange("p (f w) -> p f w", f=per)

    with nc.Block() as block:
        @block.sync
        def _(sp):
            for n, (half, g) in enumerate(loads):
                if n >= slots:
                    sp.wait_ge(used, n - slots + 1)
                src = w_down[g * per * P:(g + 1) * per * P, half * BANK:(half + 1) * BANK]
                sp.dma_start(slot(n), src.rearrange("(f p) w -> p f w", p=P)).then_inc(loaded[n % slots], 16)

        @block.tensor
        def _(pe):
            for n, (half, g) in enumerate(loads):
                pe.wait_ge(loaded[n % slots], 16 * (n // slots + 1))
                for f in range(per):
                    ff = g * per + f
                    for t in range(T):
                        last = nc.tensor.matmul(ps[:, half * T + t, :], hidden[:, ff, t * P:(t + 1) * P],
                                                slot(n)[:, f, :], start=(ff == 0), stop=(ff == nf - 1))
                last.then_inc(used, 1)

        @block.vector
        def _(dve):
            for half in range(2):
                dve.wait_ge(used, (half + 1) * (nf // per))
                for t in range(T):
                    d = x[:, t, half * BANK:(half + 1) * BANK]
                    nc.vector.scalar_tensor_tensor(out=d, in0=d, scalar=alpha, in1=ps[:, half * T + t, :],
                                                   op0=ALU.mult, op1=ALU.add)


def by_head(ap, heads):
    return ap.rearrange("p (h c) -> p h c", h=heads)


def x_transposes(env, src, dst, scale=None):
    return [([src[:, t, k * P:(k + 1) * P] for t in range(T)], dst[:, k, :],
             None if scale is None else scale[:, k:k + 1]) for k in range(KD)]



def rope_table_stage(env, positions, cos, sin):
    nc = env.nc
    TWO_PI = 2 * np.pi
    C1 = 6.28125
    C2 = float(np.float32(np.floor((TWO_PI - C1) * 2 ** 21) / 2 ** 21))
    C3 = float(np.float32(TWO_PI - C1 - C2))
    ROUND = 1.5 * 2 ** 23
    pos_loaded, reduced, sines = (env.sem("rope_table", n) for n in ("pos_loaded", "reduced", "sines"))
    step = env.sem("rope_table", "vector_step")
    n = T * ROPE // 2
    with ExitStack() as local:
        pos_i = local.enter_context(nc.sbuf_tensor("rope_pos_i", [P, T], I32))
        pos = local.enter_context(nc.sbuf_tensor("rope_pos", [P, T], F32))
        ang = local.enter_context(nc.sbuf_tensor("rope_ang", [P, T, ROPE // 2], F32))
        turns = local.enter_context(nc.sbuf_tensor("rope_turns", [P, T, ROPE // 2], F32))
        half = local.enter_context(nc.sbuf_tensor("rope_half", [P, T, ROPE // 2], F32))
        with nc.Block() as block:
            @block.sync
            def _(sp):
                sp.dma_start(pos_i[:, :], positions.rearrange("a (t p) -> p (a t)", p=P),
                             allow_slow_non_contiguous=True).then_inc(pos_loaded, 16)

            @block.vector
            def _(dve):
                link = Link(dve, step)
                dve.wait_ge(pos_loaded, 16)
                link(nc.vector.tensor_copy(pos[:, :], pos_i[:, :]))
                inv = env.consts[:, K_INV:K_INV + ROPE // 2].unsqueeze(1).to_broadcast([P, T, ROPE // 2])
                link(nc.vector.tensor_tensor(ang[:, :, :], per_tile(pos[:, :], ROPE // 2), inv, ALU.mult))
                link(nc.vector.tensor_scalar(turns[:, :, :], ang[:, :, :], 1 / TWO_PI, ROUND, ALU.mult, ALU.add))
                link(nc.vector.tensor_scalar(turns[:, :, :], turns[:, :, :], -ROUND, None, ALU.add))
                for c in (C1, C2, C3):
                    link(nc.vector.scalar_tensor_tensor(out=ang[:, :, :], in0=turns[:, :, :], scalar=-c,
                                                        in1=ang[:, :, :], op0=ALU.mult, op1=ALU.add))
                nc.vector.tensor_scalar(ang[:, :, :], ang[:, :, :], float(np.float32(3.1415925)),
                                        float(np.float32(-3.1415925)), ALU.min, ALU.max).then_inc(reduced, 1)
                dve.wait_ge(sines, 2)
                link(nc.vector.tensor_tensor(half[:, :, :], half[:, :, :], half[:, :, :], ALU.mult))
                nc.vector.tensor_scalar(cos, half[:, :, :], -2.0, 1.0, ALU.mult, ALU.add)

            @block.scalar
            def _(act):
                act.wait_ge(reduced, 1)
                nc.scalar.activation(sin, ang[:, :, :], ACT.Sin).then_inc(sines, 1)
                nc.scalar.activation(half[:, :, :], ang[:, :, :], ACT.Sin, scale=0.5).then_inc(sines, 1)


def rope(nc, link, x1, x2, cos, sin, a, b, shape):
    c, s = (t.to_broadcast(shape) for t in (cos, sin))
    nc_v = nc.vector
    link(nc_v.tensor_tensor(a, x1, s, ALU.mult))
    link(nc_v.tensor_tensor(b, x2, s, ALU.mult))
    link(nc_v.tensor_tensor(x1, x1, c, ALU.mult))
    link(nc_v.tensor_tensor(x2, x2, c, ALU.mult))
    link(nc_v.tensor_tensor(x1, x1, b, ALU.subtract))
    link(nc_v.tensor_tensor(x2, x2, a, ALU.add))


def latent_norm_stage(env, proj, vec, cqn):
    nc = env.nc
    squares, roots, step = (env.sem("latent_norm", n) for n in ("squares_summed", "roots", "vector_step"))
    parts = ((CQ, Q_RANK, V_Q, 0), (CKV, KV_RANK, V_KV, Q_RANK))
    with ExitStack() as local:
        ss = local.enter_context(nc.sbuf_tensor("latent_ss", [P, 2, T], F32))
        with nc.Block() as block:
            @block.vector
            def _(dve):
                link = Link(dve, step)
                for n, (c, w, g, o) in enumerate(parts):
                    for t in range(T):
                        src = proj[:, t, c:c + w]
                        last = nc.vector.tensor_tensor_reduce(out=cqn[:, t, o:o + w], in0=src, in1=src, scale=1.0,
                                                              scalar=0.0, op0=ALU.mult, op1=ALU.add,
                                                              accum_out=ss[:, n, t:t + 1])
                last.then_inc(squares, 1)
                dve.wait_ge(roots, 2)
                link(nc.vector.reciprocal(ss[:, :, :], ss[:, :, :]))
                for n, (c, w, g, o) in enumerate(parts):
                    for t in range(T):
                        nc.vector.scalar_tensor_tensor(out=cqn[:, t, o:o + w], in0=proj[:, t, c:c + w],
                                                       scalar=ss[:, n, t:t + 1], in1=vec[:, g:g + w],
                                                       op0=ALU.mult, op1=ALU.mult)

            @block.scalar
            def _(act):
                act.wait_ge(squares, 1)
                for n, (c, w, g, o) in enumerate(parts):
                    nc.scalar.activation(ss[:, n, :], ss[:, n, :], ACT.Sqrt, scale=1.0 / w, bias=env.eps6
                                         ).then_inc(roots, 1)


def mla_rope_stage(env, proj, qn, kn, cos, sin):
    nc = env.nc
    step = env.sem("mla_rope", "vector_step")
    H2 = ROPE // 2
    with ExitStack() as local:
        a = local.enter_context(nc.sbuf_tensor("mla_rope_a", [P, T, MLA_H, H2], F32))
        b = local.enter_context(nc.sbuf_tensor("mla_rope_b", [P, T, MLA_H, H2], F32))
        with nc.Block() as block:
            @block.vector
            def _(dve):
                link = Link(dve, step)
                rope(nc, link, qn[:, :, :, NOPE:NOPE + H2], qn[:, :, :, NOPE + H2:QK], cos.unsqueeze(2), sin.unsqueeze(2),
                     a[:, :, :, :], b[:, :, :, :], [P, T, MLA_H, H2])
                rope(nc, link, proj[:, :, KR:KR + H2], proj[:, :, KR + H2:KR + ROPE], cos, sin,
                     a[:, :, 0, :], b[:, :, 0, :], [P, T, H2])
                src = proj[:, :, KR:KR + ROPE].unsqueeze(2).to_broadcast([P, T, MLA_H, ROPE])
                nc.vector.tensor_copy(kn[:, :, :, NOPE:QK], src)


def gates_stage(env, proj, vec, gates, dt, vx):
    nc = env.nc
    ready, exp_done, ln_done = (env.sem("gates", n) for n in ("abs_ready", "exp_done", "ln_done"))
    a_exp, step, pool_step = (env.sem("gates", n) for n in ("a_exp", "vector_step", "pool_step"))
    with ExitStack() as local:
        pre = local.enter_context(nc.sbuf_tensor("gates_pre", [P, T, 16], F32))
        e = local.enter_context(nc.sbuf_tensor("gates_e", [P, T, 16], F32))
        u = local.enter_context(nc.sbuf_tensor("gates_u", [P, T, 16], F32))
        one = local.enter_context(nc.sbuf_tensor("gates_one", [P, T, 16], F32))
        ln = local.enter_context(nc.sbuf_tensor("gates_ln", [P, T, 16], F32))
        na = local.enter_context(nc.sbuf_tensor("gates_na", [P, 8], F32))
        with nc.Block() as block:
            @block.vector
            def _(dve):
                link = Link(dve, step)
                v = nc.vector
                for kind, dst in ((0, gates[:, :, 0:4]), (2, gates[:, :, 4:8]), (1, pre[:, :, 0:4]), (3, pre[:, :, 4:8])):
                    c = MG + kind * ML_H
                    bias = vec[:, V_GB + kind * ML_H:V_GB + (kind + 1) * ML_H].unsqueeze(1).to_broadcast([P, T, ML_H])
                    link(v.tensor_tensor(dst, proj[:, :, c:c + ML_H], bias, ALU.add))
                bias = vec[:, V_DTB:V_DTB + 8].unsqueeze(1).to_broadcast([P, T, 8])
                link(v.tensor_tensor(pre[:, :, 8:16], proj[:, :, SDT:SDT + 8], bias, ALU.add))
                v.scalar_tensor_tensor(out=e[:, :, :], in0=pre[:, :, :], scalar=-1.0, in1=pre[:, :, :],
                                       op0=ALU.mult, op1=ALU.max).then_inc(ready, 1)
                dve.wait_ge(exp_done, 1)
                link(v.tensor_scalar(u[:, :, :], e[:, :, :], 1.0, None, ALU.add))
                link(v.tensor_scalar(u[:, :, :], u[:, :, :], -1.0, None, ALU.add))
                link(v.tensor_scalar(one[:, :, :], u[:, :, :], 0.0, None, ALU.is_equal))
                link(v.tensor_tensor(one[:, :, :], one[:, :, :], e[:, :, :], ALU.mult))
                link(v.tensor_scalar(u[:, :, :], u[:, :, :], 1e-30, None, ALU.max))
                link(v.reciprocal(u[:, :, :], u[:, :, :]))
                link(v.tensor_tensor(u[:, :, :], u[:, :, :], e[:, :, :], ALU.mult))
                dve.wait_ge(ln_done, 1)
                link(v.tensor_tensor(ln[:, :, :], ln[:, :, :], u[:, :, :], ALU.mult))
                link(v.tensor_tensor(ln[:, :, :], ln[:, :, :], one[:, :, :], ALU.add))
                link(v.scalar_tensor_tensor(out=gates[:, :, 8:16], in0=pre[:, :, 0:8], scalar=0.0,
                                            in1=ln[:, :, 0:8], op0=ALU.min, op1=ALU.subtract))
                link(v.scalar_tensor_tensor(out=dt, in0=pre[:, :, 8:16], scalar=0.0,
                                            in1=ln[:, :, 8:16], op0=ALU.max, op1=ALU.add))
                dve.wait_ge(a_exp, 1)
                a = na[:, :].unsqueeze(1).to_broadcast([P, T, 8])
                link(v.tensor_tensor(gates[:, :, 16:24], dt, a, ALU.mult))
                v.tensor_scalar(gates[:, :, 16:24], gates[:, :, 16:24], -1.0, None, ALU.mult)

            @block.scalar
            def _(act):
                nc.scalar.activation(na[:, :], vec[:, V_AL:V_AL + 8], ACT.Exp).then_inc(a_exp, 1)
                act.wait_ge(ready, 1)
                nc.scalar.activation(e[:, :, :], e[:, :, :], ACT.Exp, scale=-1.0).then_inc(exp_done, 1)
                act.wait_ge(exp_done, 1)
                nc.scalar.activation(ln[:, :, :], e[:, :, :], ACT.Ln, bias=1.0).then_inc(ln_done, 1)

            @block.gpsimd
            def _(pool):
                for t in range(T):
                    nc.gpsimd.tensor_copy(vx[:, t, :, 0:ML_D],
                                          proj[:, t, MV:MV + ML_H * ML_D].rearrange("p (h c) -> p h c", h=ML_H))
                nc.gpsimd.memset(vx[:, :, :, ML_D:ML_D + 1], 1.0)


def scan_stage(env, gates, cols):
    nc, ps, ident = env.nc, env.ps, env.ident
    turned, copied, scanned, back = (env.sem("scan", n) for n in ("turned", "copied", "scanned", "turned_back"))
    step = env.sem("scan", "vector_step")
    R = slice(None, None, -1)
    with ExitStack() as local:
        def tile(name, rows):
            return local.enter_context(nc.sbuf_tensor(f"scan_{name}", [rows, S], F32))
        ig, lf = tile("ig", 8), tile("lf", 16)
        sums = [tile("sum_f", 16), tile("sum_b", 16)]
        c = [tile("c_f", 8), tile("c_b", 8)]
        mx = [tile("max_f", 8), tile("max_b", 8)]
        m = [tile("m_f", 8), tile("m_b", 8)]
        with nc.Block() as block:
            @block.tensor
            def _(pe):
                for t in range(T):
                    nc.tensor.transpose(ps[0:8, 0, t * P:(t + 1) * P], gates[:, t, 0:8], ident)
                    last = nc.tensor.transpose(ps[0:16, 1, t * P:(t + 1) * P], gates[:, t, 8:24], ident)
                last.then_inc(turned, 1)
                pe.wait_ge(scanned, 1)
                for t in range(T):
                    for q, (src, rows, first) in enumerate(((c, 8, 0), (mx, 8, 0), (m, 8, 0), (sums, 16, 8))):
                        for d in range(2):
                            o = q * 8 + d * 4
                            last = nc.tensor.matmul(ps[:, 2, t * 32 + o:t * 32 + o + 4],
                                                    src[d][0:rows, t * P:(t + 1) * P],
                                                    ident[0:rows, first + d * 4:first + d * 4 + 4],
                                                    start=True, stop=True)
                last.then_inc(back, 1)

            @block.vector
            def _(dve):
                link = Link(dve, step)
                v = nc.vector
                dve.wait_ge(turned, 1)
                link(v.tensor_copy(ig[:, :], ps[0:8, 0, :]))
                link(v.tensor_copy(lf[:, :], ps[0:16, 1, :]))
                for d, w in ((0, slice(None)), (1, R)):
                    link(v.tensor_tensor_scan(sums[d][:, w], lf[:, w], lf[:, w], 0.0, ALU.add, ALU.bypass))
                    link(v.tensor_tensor(c[d][:, :], ig[:, :], sums[d][0:8, :], ALU.subtract))
                    link(v.tensor_tensor_scan(mx[d][:, w], c[d][:, w], c[d][:, w], -3e38, ALU.max, ALU.bypass))
                    last = v.tensor_tensor(m[d][:, :], mx[d][:, :], sums[d][0:8, :], ALU.add)
                last.then_inc(scanned, 1)
                dve.wait_ge(back, 1)
                src = ps[:, 2, 0:T * 32].rearrange("p (t c) -> p t c", t=T)
                v.tensor_copy(cols[:, :, 0:24], src[:, :, 0:24])
                v.tensor_scalar(cols[:, :, 24:32], src[:, :, 24:32], -1.0, None, ALU.mult)


def conv_stage(env, xc, convw, conv_out):
    nc = env.nc
    step, ready = env.sem("conv", "vector_step"), env.sem("conv", "conv_ready")
    with nc.Block() as block:
        @block.vector
        def _(dve):
            link = Link(dve, step)
            for j in range(CONV):
                for c in range(CC):
                    src, dst, w = xc[:, c, j:j + S], conv_out[:, c, :], convw[:, c, j:j + 1]
                    if j == 0:
                        ins = nc.vector.tensor_scalar(dst, src, w, convw[:, c, CONV:CONV + 1], ALU.mult, ALU.add)
                    else:
                        dve.wait_ge(step, (j - 1) * CC + c + 1)
                        ins = nc.vector.scalar_tensor_tensor(out=dst, in0=src, scalar=w, in1=dst,
                                                             op0=ALU.mult, op1=ALU.add)
                    ins.then_inc(step, 1)

        @block.scalar
        def _(act):
            for c in range(CC):
                act.wait_ge(step, (CONV - 1) * CC + c + 1)
                nc.scalar.activation(conv_out[:, c, :], conv_out[:, c, :], ACT.Silu)


def decay_stage(env, units, cols):
    nc, ps, ident = env.nc, env.ps, env.ident
    N = len(units)
    names = ("products_ready", "row_ready", "gap_ready", "exp_done", "weighted", "masked", "out_ready",
             "out_stored", "vector_step")
    products_ready, row_ready, gap_ready, exp_done, weighted, masked, out_ready, out_stored, step = (
        env.sem("decay", n) for n in names)
    new_group = [i == 0 or units[i]["group"] != units[i - 1]["group"] for i in range(N)]

    def span(u, i):
        return (0, (i + 1) * P) if u["back"] else (i * P, S)

    with ExitStack() as local:
        gap = local.enter_context(nc.sbuf_tensor("decay_gap", [P, 2, T, S], F32))
        wq = local.enter_context(nc.sbuf_tensor("decay_weighted", [P, 2, T, S], F32))
        tmp = local.enter_context(nc.sbuf_tensor("decay_tmp", [P, T, 4], F32))
        with nc.Block() as block:
            @block.tensor
            def _(pe):
                for i in range(N + 1):
                    if i < N:
                        u = units[i]
                        if i >= 2:
                            pe.wait_ge(gap_ready, T * (i - 1))
                        for t in range(T):
                            r = cols[:, t, u["row"]:u["row"] + 1].to_broadcast([P, P])
                            last = nc.tensor.matmul(ps[:, 4 + i % 2, t * P:(t + 1) * P], r, ident, start=True, stop=True)
                        last.then_inc(row_ready, 1)
                        if new_group[i]:
                            if i:
                                pe.wait_ge(weighted, T * i)
                            for s in range(T):
                                last = nc.tensor.matmul(ps[:, s, :], u["k"][:, s * P:(s + 1) * P], u["q"],
                                                        start=True, stop=True)
                            last.then_inc(products_ready, 1)
                    if i >= 1:
                        j = i - 1
                        u = units[j]
                        pe.wait_ge(masked, T * (j + 1))
                        if j >= 2:
                            pe.wait_ge(out_stored, j - 1)
                        for t in range(T):
                            keys = range(t, T) if u["back"] else range(0, t + 1)
                            for s in keys:
                                last = nc.tensor.matmul(ps[:, 6 + j % 2, t * u["w"]:(t + 1) * u["w"]],
                                                        wq[:, j % 2, s, t * P:(t + 1) * P], u["v"](s),
                                                        start=(s == keys[0]), stop=(s == keys[-1]))
                        last.then_inc(out_ready, 1)

            @block.vector
            def _(dve):
                link = Link(dve, step)
                groups = 0
                for i in range(N + 1):
                    if i < N:
                        u = units[i]
                        groups += new_group[i]
                        dve.wait_ge(row_ready, i + 1)
                        for s in range(T):
                            a, b = span(u, s)
                            if i >= 2 and s == 0:
                                dve.wait_ge(weighted, T * (i - 1))
                            nc.vector.tensor_scalar(gap[:, i % 2, s, a:b], ps[:, 4 + i % 2, a:b],
                                                    cols[:, s, u["col"]:u["col"] + 1], 0.0, ALU.subtract, ALU.max
                                                    ).then_inc(gap_ready, 1)
                        dve.wait_ge(products_ready, groups)
                        if i >= 2:
                            dve.wait_ge(out_ready, i - 1)
                        for s in range(T):
                            a, b = span(u, s)
                            dve.wait_ge(exp_done, T * i + s + 1)
                            nc.vector.scalar_tensor_tensor(out=wq[:, i % 2, s, a:b], in0=ps[:, s, a:b],
                                                           scalar=u["weight"](s), in1=gap[:, i % 2, s, a:b],
                                                           op0=ALU.mult, op1=ALU.mult).then_inc(weighted, 1)
                    if i >= 1:
                        j = i - 1
                        dve.wait_ge(out_ready, j + 1)
                        out = ps[:, 6 + j % 2, 0:T * units[j]["w"]].rearrange("p (t c) -> p t c", t=T)
                        units[j]["store"](nc, link, out, tmp).then_inc(out_stored, 1)
                        dve.wait_ge(out_stored, j + 1)

            @block.scalar
            def _(act):
                for i in range(N):
                    for s in range(T):
                        a, b = span(units[i], s)
                        act.wait_ge(gap_ready, T * i + s + 1)
                        nc.scalar.activation(gap[:, i % 2, s, a:b], gap[:, i % 2, s, a:b], ACT.Exp, scale=-1.0
                                             ).then_inc(exp_done, 1)

            @block.gpsimd
            def _(pool):
                for i in range(N):
                    for s in range(T):
                        pool.wait_ge(weighted, T * i + s + 1)
                        d = wq[:, i % 2, s, s * P:(s + 1) * P]
                        nc.gpsimd.tensor_tensor(d, d, env.keep_le if units[i]["back"] else env.keep_ge, ALU.mult
                                                ).then_inc(masked, 1)


def decay_units(proj, mqk_t, conv_out, cols, dt, vx, xs, h_sum, y_ssd):
    units = []
    for h in range(ML_H):
        base, chunk = (h % 2) * ML_D, h // 2
        for d in range(2):
            k = d * ML_H + h

            def store(nc, link, out, tmp, h=h, d=d, k=k):
                v = nc.vector
                den = out[:, :, ML_D]
                link(v.tensor_scalar(tmp[:, :, 0], den, -1.0, None, ALU.mult))
                link(v.tensor_tensor(tmp[:, :, 0], tmp[:, :, 0], den, ALU.max))
                link(v.tensor_tensor(tmp[:, :, 0], tmp[:, :, 0], cols[:, :, 16 + k], ALU.max))
                link(v.reciprocal(tmp[:, :, 0], tmp[:, :, 0]))
                for t in range(T):
                    dst = h_sum[:, t, h * ML_D:(h + 1) * ML_D]
                    if d == 0:
                        last = v.tensor_scalar(dst, out[:, t, 0:ML_D], tmp[:, t, 0:1], None, ALU.mult)
                    else:
                        last = v.scalar_tensor_tensor(out=dst, in0=out[:, t, 0:ML_D], scalar=tmp[:, t, 0:1],
                                                      in1=dst, op0=ALU.mult, op1=ALU.add)
                return last

            units.append(dict(group=("m", h), k=mqk_t[base:base + ML_D, 2 + chunk, :], q=mqk_t[base:base + ML_D, chunk, :],
                              weight=lambda s: ML_D ** -0.5, row=8 + k, col=k, back=d == 1,
                              v=lambda s, h=h: vx[:, s, h, :], w=ML_D + 1, store=store))
    for h in range(SSD_H):
        g = h // (SSD_H // SSD_G)
        for d in range(2):
            k = d * SSD_H + h

            def store(nc, link, out, tmp, h=h, d=d):
                dst = y_ssd[:, :, h * SSD_P:(h + 1) * SSD_P]
                if d == 0:
                    return nc.vector.tensor_copy(dst, out)
                return nc.vector.tensor_tensor(dst, out, dst, ALU.add)

            units.append(dict(group=("s", g), k=conv_out[:, 2 + g, :], q=conv_out[:, 4 + g, :],
                              weight=lambda s, k=k: dt[:, s, k:k + 1], row=24 + k, col=24 + k, back=d == 1,
                              v=lambda s, h=h: xs[:, s, h * SSD_P:(h + 1) * SSD_P], w=SSD_P, store=store))
    return units


def exp_m_stage(env, cols):
    with env.nc.Block() as block:
        @block.scalar
        def _(act):
            env.nc.scalar.activation(cols[:, :, 16:24], cols[:, :, 16:24], ACT.Exp, scale=-1.0)


def mixer_end_stage(env, proj, vec, h_sum, y_ssd, xs, y):
    nc = env.nc
    names = ("vector_step", "variances", "roots", "sigmoid_done", "silu_done")
    step, variances, roots, sig, silu = (env.sem("mixer_end", n) for n in names)
    ME, GE = ML_H, SSD_G
    W = ML_H * ML_D
    with ExitStack() as local:
        sq = local.enter_context(nc.sbuf_tensor("end_sq", [P, T, W], F32))
        mean = local.enter_context(nc.sbuf_tensor("end_mean", [P, T * ME], F32))
        var = local.enter_context(nc.sbuf_tensor("end_var", [P, T * ME], F32))
        ss = local.enter_context(nc.sbuf_tensor("end_ss", [P, T * GE], F32))
        o = local.enter_context(nc.sbuf_tensor("end_o", [P, T, W], F32))
        z = local.enter_context(nc.sbuf_tensor("end_z", [P, T, W], F32))

        def flat(x, w):
            return x[:, :, :].rearrange("p t (h c) -> p (t h) c", c=w)

        def row(c):
            return vec[:, c:c + W].unsqueeze(1).to_broadcast([P, T, W])

        with nc.Block() as block:
            @block.scalar
            def _(act):
                nc.scalar.activation(o[:, :, :], proj[:, :, MO:MO + W], ACT.Sigmoid).then_inc(sig, 1)
                nc.scalar.activation(z[:, :, :], proj[:, :, SZ:SZ + W], ACT.Silu).then_inc(silu, 1)
                act.wait_ge(variances, 1)
                nc.scalar.activation(var[:, :], var[:, :], ACT.Sqrt, scale=1.0 / ML_D, bias=env.eps5).then_inc(roots, 1)
                act.wait_ge(variances, 2)
                nc.scalar.activation(ss[:, :], ss[:, :], ACT.Sqrt, scale=SSD_G / W, bias=env.eps6).then_inc(roots, 1)

            @block.vector
            def _(dve):
                link = Link(dve, step)
                v = nc.vector
                hf, sf = flat(h_sum, ML_D), flat(sq, ML_D)
                link(v.reduce_sum(mean[:, :], hf, AX))
                link(v.tensor_scalar(mean[:, :], mean[:, :], 1.0 / ML_D, None, ALU.mult))
                link(v.tensor_tensor(hf, hf, per_tile(mean[:, :], ML_D), ALU.subtract))
                link(v.tensor_tensor(sf, hf, hf, ALU.mult))
                v.reduce_sum(var[:, :], sf, AX).then_inc(variances, 1)
                for h in range(SSD_H):
                    c = slice(h * SSD_P, (h + 1) * SSD_P)
                    last = v.scalar_tensor_tensor(out=y_ssd[:, :, c], in0=xs[:, :, c], scalar=vec[:, V_SD + h:V_SD + h + 1],
                                                  in1=y_ssd[:, :, c], op0=ALU.mult, op1=ALU.add)
                link(last)
                dve.wait_ge(silu, 1)
                link(v.tensor_tensor(y_ssd[:, :, :], y_ssd[:, :, :], z[:, :, :], ALU.mult))
                dve.wait_ge(variances, 1)
                link(v.tensor_tensor(sq[:, :, :], y_ssd[:, :, :], y_ssd[:, :, :], ALU.mult))
                v.reduce_sum(ss[:, :], flat(sq, W // GE), AX).then_inc(variances, 1)
                dve.wait_ge(roots, 2)
                link(v.reciprocal(var[:, :], var[:, :]))
                link(v.reciprocal(ss[:, :], ss[:, :]))
                link(v.tensor_tensor(hf, hf, per_tile(var[:, :], ML_D), ALU.mult))
                link(v.tensor_tensor(h_sum[:, :, :], h_sum[:, :, :], row(V_MN), ALU.mult))
                dve.wait_ge(sig, 1)
                v.tensor_tensor(y[:, :, 512:768], h_sum[:, :, :], o[:, :, :], ALU.mult)
                yf = flat(y_ssd, W // GE)
                link(v.tensor_tensor(yf, yf, per_tile(ss[:, :], W // GE), ALU.mult))
                v.tensor_tensor(y[:, :, 768:1024], y_ssd[:, :, :], row(V_SN), ALU.mult)


def router_stage(env, xt, router_w, vec, combine):
    nc, ps = env.nc, env.ps
    names = ("weights_loaded", "logits_ready", "shifted", "exp_done", "vector_step")
    loaded, logits_ready, shifted, exp_done, step = (env.sem("router", n) for n in names)
    with ExitStack() as local:
        def tile(name, *shape):
            return local.enter_context(nc.sbuf_tensor(f"router_{name}", [P, *shape], F32))
        wr = tile("w", KD, NR)
        lg, e, acc = tile("logits", T, NR), tile("e", T, GROUPS), tile("acc", T, PER_GROUP)
        top, eq, rem, oh = tile("top", T, 1), tile("eq", T, 4), tile("rem", T, 1), tile("oh", T, 4)
        first, second, gp, tmp = tile("first", T, 4), tile("second", T, 4), tile("gp", T, 1), tile("tmp", T, 4)
        with nc.Block() as block:
            @block.sync
            def _(sp):
                sp.dma_start(wr[:, :, :], router_w.rearrange("(k p) c -> p k c", p=P),
                             allow_slow_non_contiguous=True).then_inc(loaded, 16)

            @block.tensor
            def _(pe):
                pe.wait_ge(loaded, 16)
                for t in range(T):
                    for k in range(KD):
                        last = nc.tensor.matmul(ps[:, 0, t * NR:(t + 1) * NR], xt[:, k, t * P:(t + 1) * P],
                                                wr[:, k, :], start=(k == 0), stop=(k == KD - 1))
                last.then_inc(logits_ready, 1)

            @block.vector
            def _(dve):
                link = Link(dve, step)
                v = nc.vector

                def wide(x):
                    return x[:, :, :].to_broadcast([P, T, 4])

                def first_of_max(x, out):
                    link(v.reduce_max(top[:, :, 0], x, AX))
                    link(v.tensor_tensor(eq[:, :, :], x, wide(top), ALU.is_equal))
                    link(v.tensor_scalar(rem[:, :, :], top[:, :, :], 0.0, 1.0, ALU.mult, ALU.add))
                    for j in range(4):
                        link(v.tensor_tensor(out[:, :, j:j + 1], eq[:, :, j:j + 1], rem[:, :, :], ALU.mult))
                        if j < 3:
                            link(v.tensor_tensor(rem[:, :, :], rem[:, :, :], out[:, :, j:j + 1], ALU.subtract))

                dve.wait_ge(logits_ready, 1)
                src = ps[:, 0, 0:T * NR].rearrange("p (t c) -> p t c", t=T)
                bias = vec[:, V_RB:V_RB + NR].unsqueeze(1).to_broadcast([P, T, NR])
                link(v.tensor_tensor(lg[:, :, :], src, bias, ALU.add))
                first_of_max(lg[:, :, 0:GROUPS], oh)
                v.tensor_tensor(e[:, :, :], lg[:, :, 0:GROUPS], wide(top), ALU.subtract).then_inc(shifted, 1)
                dve.wait_ge(exp_done, 1)
                link(v.reduce_sum(gp[:, :, 0], e[:, :, :], AX))
                link(v.reciprocal(gp[:, :, :], gp[:, :, :]))
                for g in range(GROUPS):
                    c = GROUPS + g * PER_GROUP
                    dst = acc if g == 0 else tmp
                    link(v.tensor_tensor(dst[:, :, :], lg[:, :, c:c + PER_GROUP], oh[:, :, g:g + 1].to_broadcast([P, T, 4]),
                                         ALU.mult))
                    if g:
                        link(v.tensor_tensor(acc[:, :, :], acc[:, :, :], tmp[:, :, :], ALU.add))
                first_of_max(acc[:, :, :], first)
                v.tensor_tensor(e[:, :, :], acc[:, :, :], wide(top), ALU.subtract).then_inc(shifted, 1)
                link(v.scalar_tensor_tensor(out=tmp[:, :, :], in0=first[:, :, :], scalar=-3e38, in1=acc[:, :, :],
                                            op0=ALU.mult, op1=ALU.add))
                dve.wait_ge(shifted, 2)
                first_of_max(tmp[:, :, :], second)
                dve.wait_ge(exp_done, 2)
                link(v.tensor_tensor(first[:, :, :], first[:, :, :], second[:, :, :], ALU.add))
                link(v.tensor_tensor(e[:, :, :], e[:, :, :], first[:, :, :], ALU.mult))
                link(v.reduce_sum(rem[:, :, 0], e[:, :, :], AX))
                link(v.reciprocal(rem[:, :, :], rem[:, :, :]))
                link(v.tensor_tensor(rem[:, :, :], rem[:, :, :], gp[:, :, :], ALU.mult))
                link(v.tensor_tensor(e[:, :, :], e[:, :, :], wide(rem), ALU.mult))
                for g in range(GROUPS):
                    v.tensor_tensor(combine[:, :, g * PER_GROUP:(g + 1) * PER_GROUP], e[:, :, :],
                                    oh[:, :, g:g + 1].to_broadcast([P, T, 4]), ALU.mult)

            @block.scalar
            def _(act):
                for n in range(2):
                    act.wait_ge(shifted, n + 1)
                    nc.scalar.activation(e[:, :, :], e[:, :, :], ACT.Exp).then_inc(exp_done, 1)


def first_layer(env, l, dram, x, xt, cos, sin):
    nc = env.nc
    at = layer_of(dram, l)

    with ExitStack() as local:
        def tile(name, *shape):
            return local.enter_context(nc.sbuf_tensor(name, [P, *shape], F32))
        vec = tile("vec1", NV1)
        convw = tile("convw", CC, CONV + 1)
        load_small_stage(env, "small1", [(vec[:, :], at("vec1").to_broadcast([P, NV1])),
                                         (convw[:, :, :], at("conv1"))])
        with ExitStack() as mix:
            y = mix.enter_context(nc.sbuf_tensor("y1", [P, T, D], F32))
            proj = mix.enter_context(nc.sbuf_tensor("proj1", [P, T, IN1], F32))
            w_in = at("w_in")
            lhs = [xt[:, k, :] for k in range(KD)]
            jobs = []
            for c in range(0, IN1, BANK):
                w = min(BANK, IN1 - c)
                jobs.append((lhs, w_in[:, c:c + w], [(lambda b, w=w: b[:, 0:w], lambda t, c=c, w=w: proj[:, t, c:c + w])]))
            project_stage(env, "proj1", jobs)

            with ExitStack() as mla:
                def mtile(name, *shape):
                    return mla.enter_context(nc.sbuf_tensor(name, [P, *shape], F32))
                q_t, k_t = mtile("q_t", MLA_H, S), mtile("k_t", MLA_H, S)
                v = mtile("v_mla", T, MLA_H, MLA_V)
                with ExitStack() as pre:
                    def ptile(name, *shape):
                        return pre.enter_context(nc.sbuf_tensor(name, [P, *shape], F32))
                    qn, kn = ptile("qn", T, MLA_H, QK), ptile("kn", T, MLA_H, QK)
                    NC = (Q_RANK + KV_RANK) // P
                    cqn = k_t[:, 0:NC, :].rearrange("p a c -> p (a c)").rearrange("p (t c) -> p t c", t=T)
                    cqt = k_t[:, 3:3 + NC, :]
                    latent_norm_stage(env, proj, vec, cqn)
                    transpose_stage(env, "latent_t", [([cqn[:, t, k * P:(k + 1) * P] for t in range(T)],
                                                       cqt[:, k, :], None) for k in range(NC)])
                    jobs = []
                    for n in range(2):
                        hs = slice(n * 4, n * 4 + 4)
                        jobs.append(([cqt[:, 0, :], cqt[:, 1, :]], at("mla_w_uq")[:, n * 4 * QK:(n + 1) * 4 * QK],
                                     [(lambda b: by_head(b[:, 0:4 * QK], 4), lambda t, hs=hs: qn[:, t, hs, :])]))
                    for n in range(2):
                        hs = slice(n * 4, n * 4 + 4)
                        jobs.append(([cqt[:, 2, :]], at("mla_w_ukv")[:, n * BANK:(n + 1) * BANK],
                                     [(lambda b: by_head(b, 4)[:, :, 0:NOPE], lambda t, hs=hs: kn[:, t, hs, 0:NOPE]),
                                      (lambda b: by_head(b, 4)[:, :, NOPE:], lambda t, hs=hs: v[:, t, hs, :])]))
                    project_stage(env, "mla_proj", jobs)
                    mla_rope_stage(env, proj, qn, kn, cos, sin)
                    transpose_stage(env, "mla_t", [([src[:, t, h, :] for t in range(T)], dst[0:QK, h, :], None)
                                                   for h in range(MLA_H) for src, dst in ((qn, q_t), (kn, k_t))])
                units = [dict(q=q_t[0:QK, h, t * P:(t + 1) * P], k=k_t[0:QK, h, :], nk=S, mask=None,
                              v=[v[:, b, h, :] for b in range(T)],
                              dst=y[:, t, h * MLA_V:(h + 1) * MLA_V])
                         for h in range(MLA_H) for t in range(T)]
                attention_stage(env, "mla", units, QK ** -0.5)

            with ExitStack() as rec:
                def rtile(name, *shape):
                    return rec.enter_context(nc.sbuf_tensor(name, [P, *shape], F32))
                conv_out = rtile("conv_out", CC, S)
                xs = rtile("xs", T, SSD_H * SSD_P)
                with ExitStack() as pre:
                    xc = pre.enter_context(nc.sbuf_tensor("xc", [P, CC, S + 2 * PAD], F32))
                    pad_stage(env, xc)
                    transpose_stage(env, "conv_t", [([proj[:, t, XBC + c * P:XBC + (c + 1) * P] for t in range(T)],
                                                     xc[:, c, PAD:PAD + S], None) for c in range(CC)])
                    conv_stage(env, xc, convw, conv_out)
                mqk_t = rtile("mqk_t", 4, S)
                jobs = [([proj[:, t, MQ + c * P:MQ + (c + 1) * P] for t in range(T)], mqk_t[:, c, :], None)
                        for c in range(4)]
                for t in range(T):
                    jobs.append(([conv_out[:, c, t * P:(t + 1) * P] for c in range(2)], xs[:, t, :], None))
                transpose_stage(env, "rec_t", jobs)
                gates, dt = rtile("gates", T, 24), rtile("dt", T, 8)
                vx, cols = rtile("vx", T, ML_H, ML_D + 1), rtile("cols", T, 32)
                h_sum, y_ssd = rtile("h_sum", T, ML_H * ML_D), rtile("y_ssd", T, SSD_H * SSD_P)
                gates_stage(env, proj, vec, gates, dt[:, :, :], vx)
                scan_stage(env, gates, cols)
                exp_m_stage(env, cols)
                decay_stage(env, decay_units(proj, mqk_t, conv_out, cols, dt, vx, xs, h_sum, y_ssd), cols)
                mixer_end_stage(env, proj, vec, h_sum, y_ssd, xs, y)

            transpose_stage(env, "y_t", x_transposes(env, y, xt))
            w_out = at("w_out")
            jobs = [([xt[:, k, :] for k in range(KD)], w_out[:, n * BANK:(n + 1) * BANK],
                     [(lambda b: b, lambda t, n=n: x[:, t, n * BANK:(n + 1) * BANK])]) for n in range(2)]
            project_stage(env, "out1", jobs, alpha_x=ALPHA)
        layernorm_stage(env, "ln1", at("ln1"), x)
        transpose_stage(env, "x1_t", x_transposes(env, x, xt))
        with ExitStack() as moe:
            combine = moe.enter_context(nc.sbuf_tensor("combine", [P, T, EXPERTS], F32))
            router_stage(env, xt, at("router"), vec, combine)
            hidden = moe.enter_context(nc.sbuf_tensor("hidden1", [P, EXPERTS * F_CH // P, S], F32))

            def expert(name):
                return lambda c: at(name)[c:c + 1, :, :].rearrange("e (k p) f -> p (e k) f", p=P)

            hidden_stage(env, "moe", xt, expert("expert_w_gate"), expert("expert_w_up"), EXPERTS, hidden,
                         lambda t, c: combine[:, t, c:c + 1].to_broadcast([P, P]))
            down_stage(env, "moe_down", hidden, EXPERTS * F_CH // P,
                       at("expert_w_down").rearrange("e f d -> (e f) d"), x, ALPHA)
        layernorm_stage(env, "ln2", at("ln2"), x)
        transpose_stage(env, "x2_t", x_transposes(env, x, xt))


def layer_of(dram, l):
    def at(name):
        ap = dram[name]
        ap = ap[tuple([bass.ds(l, 1)] + [slice(None)] * (len(ap.shape) - 1))]
        if len(ap.shape) == 2:
            return ap
        dims = [f"d{i}" for i in range(1, len(ap.shape))]
        return ap.rearrange(f"a {' '.join(dims)} -> (a {dims[0]}) {' '.join(dims[1:])}")
    return at


def load_small_stage(env, stage, pairs):
    nc = env.nc
    loaded = env.sem(stage, "loaded")
    with nc.Block() as block:
        @block.sync
        def _(sp):
            for dst, src in pairs:
                sp.dma_start(dst, src).then_inc(loaded, 16)
            sp.wait_ge(loaded, 16 * len(pairs))


def pad_stage(env, xc):
    nc = env.nc
    with nc.Block() as block:
        @block.gpsimd
        def _(pool):
            nc.gpsimd.memset(xc[:, :, 0:PAD], 0.0)
            nc.gpsimd.memset(xc[:, :, PAD + S:], 0.0)



def rms_stage(env, stage, x, out):
    nc = env.nc
    squares, roots, step = (env.sem(stage, n) for n in ("squares_summed", "roots", "vector_step"))
    with nc.sbuf_tensor(f"{stage}_ss", [P, T], F32) as ss:
        with nc.Block() as block:
            @block.scalar
            def _(act):
                for t in range(T):
                    nc.scalar.activation(out[:, t, :], x[:, t, :], ACT.Square, accum_out=ss[:, t:t + 1]
                                         ).then_inc(squares, 1)
                act.wait_ge(squares, T)
                nc.scalar.activation(ss[:, :], ss[:, :], ACT.Sqrt, scale=1.0 / D, bias=env.eps6).then_inc(roots, 1)

            @block.vector
            def _(dve):
                link = Link(dve, step)
                dve.wait_ge(roots, 1)
                link(nc.vector.reciprocal(ss[:, :], ss[:, :]))
                for t in range(T):
                    nc.vector.tensor_scalar(out[:, t, :], x[:, t, :], ss[:, t:t + 1], None, ALU.mult)


def head_norm_stage(env, proj, vec2, scratch, ik2, iw, lam):
    nc = env.nc
    squares, roots, step = (env.sem("head_norm", n) for n in ("squares_summed", "roots", "vector_step"))
    dots, exps = env.sem("head_norm", "lambda_dots"), env.sem("head_norm", "lambda_exps")
    segs = [(B_MQ, 4, 0), (B_DQ, 8, 1), (B_SQ, 4, 2)]
    with ExitStack() as local:
        ss = local.enter_context(nc.sbuf_tensor("head_ss", [P, T, 32], F32))
        lt = local.enter_context(nc.sbuf_tensor("lam_tmp", [P, 128], F32))
        dot = local.enter_context(nc.sbuf_tensor("lam_dot", [P, 2], F32))
        with nc.Block() as block:
            @block.vector
            def _(dve):
                link = Link(dve, step)
                v = nc.vector
                for t in range(T):
                    o = 0
                    for c, nh, _ in segs:
                        w = 2 * nh * HD
                        x = proj[:, t, c:c + w]
                        link(v.tensor_tensor(scratch[:, t, 0:w], x, x, ALU.mult))
                        last = v.reduce_sum(ss[:, t, o:o + 2 * nh], by_head(scratch[:, t, 0:w], 2 * nh), AX)
                        link(last)
                        o += 2 * nh
                v.tensor_scalar(ss[:, :, :], ss[:, :, :], 1.0 / HD, 1e-6, ALU.mult, ALU.add).then_inc(squares, 1)
                for n in range(2):
                    a = V2_L + 2 * n * HD
                    link(v.tensor_tensor(lt[:, 0:HD], vec2[:, a:a + HD], vec2[:, a + HD:a + 2 * HD], ALU.mult))
                    link(v.reduce_sum(dot[:, n:n + 1], lt[:, 0:HD], AX))
                v.tensor_scalar(dot[:, :], dot[:, :], 1.0, None, ALU.mult).then_inc(dots, 1)
                dve.wait_ge(roots, 1)
                link(v.reciprocal(ss[:, :, :], ss[:, :, :]))
                for t in range(T):
                    o = 0
                    for c, nh, g in segs:
                        x = by_head(proj[:, t, c:c + 2 * nh * HD], 2 * nh)
                        link(v.tensor_tensor(x, x, per_tile(ss[:, t, o:o + 2 * nh], HD), ALU.mult))
                        o += 2 * nh
                        for side, gains in ((0, V2_Q), (1, V2_K)):
                            xs = x[:, side * nh:(side + 1) * nh, :]
                            gain = vec2[:, gains + g * HD:gains + (g + 1) * HD].unsqueeze(1).to_broadcast([P, nh, HD])
                            link(v.tensor_tensor(xs, xs, gain, ALU.mult))
                    for c, nh in ((B_MQ, 8), (B_DQ, 16), (B_SQ, 8), (B_IQ, 9)):
                        x = by_head(proj[:, t, c:c + nh * HD], nh)
                        a = scratch[:, t, 0:nh * HALF].rearrange("p (h c) -> p h c", h=nh)
                        b = scratch[:, t, 512:512 + nh * HALF].rearrange("p (h c) -> p h c", h=nh)
                        cos = env.cos2[:, t, :].unsqueeze(1)
                        sin = env.sin2[:, t, :].unsqueeze(1)
                        rope(nc, link, x[:, :, 0:HALF], x[:, :, HALF:HD], cos, sin, a, b, [P, nh, HALF])
                for n in range(2):
                    v.tensor_copy(ik2[:, :, n * HD:(n + 1) * HD], proj[:, :, B_IK:B_IK + HD])
                v.tensor_scalar(iw, proj[:, :, B_IW:B_IW + IDX_H], IDX_H ** -0.5, None, ALU.mult)
                dve.wait_ge(exps, 1)
                link(v.tensor_tensor(lam, dot[:, 1:2], dot[:, 0:1], ALU.subtract))
                v.tensor_tensor(lam, lam, env.lam_c[:, 0:1], ALU.subtract)

            @block.scalar
            def _(act):
                act.wait_ge(squares, 1)
                nc.scalar.activation(ss[:, :, :], ss[:, :, :], ACT.Sqrt).then_inc(roots, 1)
                act.wait_ge(dots, 1)
                nc.scalar.activation(dot[:, :], dot[:, :], ACT.Exp).then_inc(exps, 1)


def index_stage(env, qk_t, ik_t, iw, score):
    nc, ps, causal = env.nc, env.ps, env.causal
    names = ("logits_ready", "relu_done", "added", "vector_step")
    logits_ready, relu_done, added, step = (env.sem("index", n) for n in names)
    TAKEN = -3e38
    tiles = list(range(N_TOP // P, T))
    units = [(t, h) for t in tiles for h in range(IDX_H)]
    with ExitStack() as local:
        relu = local.enter_context(nc.sbuf_tensor("index_relu", [P, 2, S], F32))
        top = local.enter_context(nc.sbuf_tensor("index_top", [P, T, 8], F32))
        with nc.Block() as block:
            @block.tensor
            def _(pe):
                for i, (t, h) in enumerate(units):
                    nk = (t + 1) * P
                    base = (h % 2) * HD
                    if i >= 4:
                        pe.wait_ge(relu_done, i - 3)
                    nc.tensor.matmul(ps[:, i % 4, 0:nk], qk_t[base:base + HD, 16 + h // 2, t * P:(t + 1) * P],
                                     ik_t[base:base + HD, 0:nk], start=True, stop=True).then_inc(logits_ready, 1)

            @block.scalar
            def _(act):
                for i, (t, h) in enumerate(units):
                    nk = (t + 1) * P
                    act.wait_ge(logits_ready, i + 1)
                    if i >= 2:
                        act.wait_ge(added, i - 1)
                    nc.scalar.activation(relu[:, i % 2, 0:nk], ps[:, i % 4, 0:nk], ACT.Relu, scale=HD ** -0.5
                                         ).then_inc(relu_done, 1)

            @block.vector
            def _(dve):
                link = Link(dve, step)
                v = nc.vector
                for i, (t, h) in enumerate(units):
                    nk = (t + 1) * P
                    dve.wait_ge(relu_done, i + 1)
                    sc, w = score(t), iw[:, t, h:h + 1]
                    if h == 0:
                        ins = v.tensor_scalar(sc, relu[:, i % 2, 0:nk], w, None, ALU.mult)
                    else:
                        ins = v.scalar_tensor_tensor(out=sc, in0=relu[:, i % 2, 0:nk], scalar=w, in1=sc,
                                                     op0=ALU.mult, op1=ALU.add)
                    ins.then_inc(added, 1)
                    dve.wait_ge(added, i + 1)
                for t in tiles:
                    diag = score(t)[:, t * P:(t + 1) * P]
                    link(v.tensor_tensor(diag, diag, causal, ALU.add))
                for r in range(N_TOP // 8):
                    for t in tiles:
                        last = v.max(top[:, t, :], score(t))
                    link(last)
                    for t in tiles:
                        last = v.match_replace(score(t), top[:, t, :], score(t), TAKEN)
                    link(last)
                for t in tiles:
                    last = v.tensor_scalar(score(t), score(t), TAKEN, MASKED, ALU.not_equal, ALU.mult)


def diff_end_stage(env, y2, d2, vec2, lam):
    nc = env.nc
    squares, roots, step = (env.sem("diff_end", n) for n in ("squares_summed", "roots", "vector_step"))
    NH, W = 4, 128
    with ExitStack() as local:
        sq = local.enter_context(nc.sbuf_tensor("diff_sq", [P, NH * W], F32))
        ss = local.enter_context(nc.sbuf_tensor("diff_ss", [P, T * NH], F32))
        gain = local.enter_context(nc.sbuf_tensor("diff_gain", [P, W], F32))
        with nc.Block() as block:
            @block.vector
            def _(dve):
                link = Link(dve, step)
                v = nc.vector
                link(v.tensor_scalar(gain[:, :], vec2[:, V2_S:V2_S + W], env.lam_c[:, 1:2], None, ALU.mult))
                for t in range(T):
                    y = y2[:, t, 256:768]
                    link(v.scalar_tensor_tensor(out=y, in0=d2[:, t, :], scalar=lam, in1=y, op0=ALU.mult, op1=ALU.add))
                    link(v.tensor_tensor(sq[:, :], y, y, ALU.mult))
                    link(v.reduce_sum(ss[:, t * NH:(t + 1) * NH], by_head(sq[:, :], NH), AX))
                v.tensor_scalar(ss[:, :], ss[:, :], 1.0 / W, 1e-6, ALU.mult, ALU.add).then_inc(squares, 1)
                dve.wait_ge(roots, 1)
                link(v.reciprocal(ss[:, :], ss[:, :]))
                for t in range(T):
                    y = by_head(y2[:, t, 256:768], NH)
                    link(v.tensor_tensor(y, y, per_tile(ss[:, t * NH:(t + 1) * NH], W), ALU.mult))
                    v.tensor_tensor(y, y, gain[:, :].unsqueeze(1).to_broadcast([P, NH, W]), ALU.mult)

            @block.scalar
            def _(act):
                act.wait_ge(squares, 1)
                nc.scalar.activation(ss[:, :], ss[:, :], ACT.Sqrt).then_inc(roots, 1)


def second_layer(env, l, dram, x, xt):
    nc = env.nc
    at = layer_of(dram, l)
    with ExitStack() as local:
        def tile(name, *shape):
            return local.enter_context(nc.sbuf_tensor(name, [P, *shape], F32))
        vec2, gains = tile("vec2", NV2), tile("gains2", 2 * KD)
        env.lam_c = tile("lam_c", 2)
        load_small_stage(env, "small2", [(vec2[:, :], at("vec2").to_broadcast([P, NV2])),
                                         (gains[:, :], at("gains2")),
                                         (env.lam_c[:, :], at("lam_init").to_broadcast([P, 2]))])
        with ExitStack() as mix:
            def mtile(name, *shape):
                return mix.enter_context(nc.sbuf_tensor(name, [P, *shape], F32))
            y2 = mtile("y2", T, D)
            rms_stage(env, "rms_attn", x, y2)
            transpose_stage(env, "h_t", x_transposes(env, y2, xt, gains[:, 0:KD]))
            proj = mtile("proj2", T, IN2)
            w_in = at("w_in_2")
            lhs = [xt[:, k, :] for k in range(KD)]
            jobs = []
            for c in range(0, IN2, BANK):
                w = min(BANK, IN2 - c)
                jobs.append((lhs, w_in[:, c:c + w], [(lambda b, w=w: b[:, 0:w], lambda t, c=c, w=w: proj[:, t, c:c + w])]))
            project_stage(env, "proj2", jobs)
            ik2, iw, lam = mtile("ik2", T, P), mtile("iw", T, IDX_H), mtile("lam", 1)
            head_norm_stage(env, proj, vec2, y2, ik2, iw[:, :, :], lam[:, 0:1])
            qk_t = mtile("qk_t", 21, S)
            cols = ([B_MQ + c * P for c in range(4)] + [B_DQ + c * P for c in range(8)]
                    + [B_SQ + c * P for c in range(4)] + [B_IQ + c * P for c in range(4)])
            jobs = [([proj[:, t, c:c + P] for t in range(T)], qk_t[:, n, :], None) for n, c in enumerate(cols)]
            jobs.append(([ik2[:, t, :] for t in range(T)], qk_t[:, 20, :], None))
            transpose_stage(env, "qk_t", jobs)

            def score(t):
                return proj[:, t, B_DK:B_DK + (t + 1) * P]
            index_stage(env, qk_t, qk_t[:, 20, :], iw, score)
            d2 = proj[:, :, B_DQ:B_DQ + 512]

            def half(chunk, h):
                base = (h % 2) * HD
                return qk_t[base:base + HD, chunk + h // 2, :]

            units = []
            for name, nh, q0, k0 in (("moba", 4, 0, 2), ("diff", 8, 4, 8), ("dsa", 4, 12, 14)):
                for h in range(nh):
                    for t in range(T):
                        nk = (t + 1) * P
                        u = dict(q=half(q0, h)[:, t * P:nk], k=half(k0, h)[:, 0:nk], nk=nk, mask="diag")
                        if name == "moba":
                            u["v"] = [proj[:, b, B_MV + h * HD:B_MV + (h + 1) * HD] for b in range(t + 1)]
                            u["dst"] = y2[:, t, h * HD:(h + 1) * HD]
                        elif name == "dsa":
                            u["v"] = [proj[:, b, B_SV + h * HD:B_SV + (h + 1) * HD] for b in range(t + 1)]
                            u["dst"] = y2[:, t, 768 + h * HD:768 + (h + 1) * HD]
                            if t >= N_TOP // P:
                                u["mask"] = score(t)
                        else:
                            g = h // 2
                            u["v"] = [proj[:, b, B_DV + g * P:B_DV + (g + 1) * P] for b in range(t + 1)]
                            u["dst"] = d2[:, t, g * P:(g + 1) * P] if h % 2 else y2[:, t, 256 + g * P:256 + (g + 1) * P]
                        units.append(u)
            attention_stage(env, "attn2", units, HD ** -0.5)
            diff_end_stage(env, y2, d2, vec2, lam[:, 0:1])
            transpose_stage(env, "y2_t", x_transposes(env, y2, xt))
            w_out = at("w_out_2")
            jobs = [([xt[:, k, :] for k in range(KD)], w_out[:, n * BANK:(n + 1) * BANK],
                     [(lambda b: b, lambda t, n=n: x[:, t, n * BANK:(n + 1) * BANK])]) for n in range(2)]
            project_stage(env, "out2", jobs, alpha_x=1.0)
            rms_stage(env, "rms_ffn", x, y2)
            transpose_stage(env, "h2_t", x_transposes(env, y2, xt, gains[:, KD:2 * KD]))
        with ExitStack() as ffn:
            hidden = ffn.enter_context(nc.sbuf_tensor("hidden2", [P, D_FF // P, S], F32))

            def chunk(name):
                return lambda c: at(name).rearrange("(k p) f -> p k f", p=P)[:, :, c * F_CH:(c + 1) * F_CH]

            hidden_stage(env, "ffn", xt, chunk("w_gate_2"), chunk("w_up_2"), FF_CH, hidden)
            down_stage(env, "ffn_down", hidden, D_FF // P, at("w_down_2"), x, 1.0)


def build(nc, dram, out, debug=None):
    with ExitStack() as ctx:
        env = Env(nc)

        def tile(name, *shape):
            return ctx.enter_context(nc.sbuf_tensor(name, [P, *shape], F32))
        x, xt = tile("x", T, D), tile("xt", KD, S)
        env.slots = 2
        env.ring = tile("ring", env.slots, KD * BANK)
        env.consts = tile("consts", NK)
        eps = tile("eps", 2)
        cos1, sin1 = tile("cos1", T, ROPE // 2), tile("sin1", T, ROPE // 2)
        env.ps = ctx.enter_context(nc.psum_tensor("ps", [P, NBANK, BANK], F32))
        env.ident = env.consts[:, K_ID:K_ID + P]
        env.keep_ge = env.consts[:, K_GE:K_GE + P]
        env.keep_le = env.consts[:, K_LE:K_LE + P]
        env.causal = env.consts[:, K_CAUSAL:K_CAUSAL + P]
        env.cos2 = env.consts[:, K_COS:K_COS + T * HALF].rearrange("p (t c) -> p t c", t=T)
        env.sin2 = env.consts[:, K_SIN:K_SIN + T * HALF].rearrange("p (t c) -> p t c", t=T)
        env.eps5, env.eps6 = eps[:, 0:1], eps[:, 1:2]
        saved = ctx.enter_context(nc.semaphore("output_saved"))
        start_loaded = ctx.enter_context(nc.semaphore("start_loaded"))

        with nc.Block() as block:
            @block.sync
            def _(sp):
                sp.dma_start(x[:, :, :], dram["x"].rearrange("a (t p) d -> p (a t) d", p=P)).then_inc(start_loaded, 16)
                sp.dma_start(env.consts[:, :], dram["consts"]).then_inc(start_loaded, 16)
                sp.wait_ge(start_loaded, 32)

            @block.vector
            def _(dve):
                nc.vector.memset(eps[:, 0:1], 1e-5)
                nc.vector.memset(eps[:, 1:2], 1e-6)
        with env.semaphores():
            rope_table_stage(env, dram["positions"], cos1[:, :, :], sin1[:, :, :])
            transpose_stage(env, "x_t", x_transposes(env, x, xt))
            env.end_layer()
        with env.semaphores(), nc.Fori(0, DEPTH) as l:
            first_layer(env, l, dram, x, xt, cos1[:, :, :], sin1[:, :, :])
            env.end_layer()
        with env.semaphores(), nc.Fori(0, DEPTH) as l:
            second_layer(env, l, dram, x, xt)
            env.end_layer()
        with nc.Block() as block:
            @block.sync
            def _(sp):
                sp.dma_start(out.rearrange("a (t p) d -> p (a t) d", p=P), x[:, :, :]).then_inc(saved, 16)
                sp.wait_ge(saved, 16)


def constants():
    c = np.zeros((P, NK), np.float32)
    i = np.arange(P)
    c[:, K_ID:K_ID + P] = np.eye(P)
    c[:, K_GE:K_GE + P] = i[None, :] >= i[:, None]
    c[:, K_LE:K_LE + P] = i[None, :] <= i[:, None]
    c[:, K_CAUSAL:K_CAUSAL + P] = np.where(i[None, :] <= i[:, None], 0.0, MASKED)
    f = np.float32
    inv = f(1.0) / f(10000.0) ** (np.arange(0, HD, 2, dtype=f) / f(HD))
    ang = (np.arange(S, dtype=f)[:, None] * inv[None, :]).reshape(T, P, HALF).transpose(1, 0, 2)
    c[:, K_COS:K_COS + T * HALF] = np.cos(ang).reshape(P, -1)
    c[:, K_SIN:K_SIN + T * HALF] = np.sin(ang).reshape(P, -1)
    c[:, K_INV:K_INV + ROPE // 2] = f(10000.0) ** (-np.arange(0, ROPE, 2, dtype=f) / f(ROPE))
    return c


def packed(i):
    n = DEPTH

    def rows(*names):
        return np.concatenate([np.asarray(i[k]).reshape(n, -1) for k in names], 1)

    def by_partition(a):
        return np.asarray(a).reshape(n, KD, P).transpose(0, 2, 1)

    conv = np.concatenate([np.asarray(i["ssd_conv_w"]), np.asarray(i["ssd_conv_b"])[:, None]], 1)
    lam0 = [0.8 - 0.6 * float(np.exp(-0.3 * l)) for l in range(n)]
    arrays = {
        "consts": constants(),
        "vec1": rows("mla_q_norm", "mla_kv_norm", "mlstm_gate_bias", "mlstm_norm", "ssd_dt_bias", "ssd_a_log",
                     "ssd_d", "ssd_norm", "router_group_b", "router_expert_b"),
        "conv1": conv.transpose(0, 2, 1).reshape(n, CC, P, CONV + 1).transpose(0, 2, 1, 3),
        "ln1": rows("ln1_g", "ln1_b"), "ln2": rows("ln2_g", "ln2_b"),
        "router": np.concatenate([np.asarray(i["router_group_w"]),
                                  np.asarray(i["router_expert_w"]).transpose(0, 2, 1, 3).reshape(n, D, EXPERTS)], 2),
        "vec2": rows("q_norm_g_2", "k_norm_g_2", "diff_lambda_2", "diff_subln_g_2"),
        "gains2": np.concatenate([by_partition(i["attn_norm_g_2"]), by_partition(i["ffn_norm_g_2"])], 2),
        "lam_init": np.array([[a, 1.0 - a] for a in lam0], np.float32),
    }
    for k in ("x", "positions", "w_in", "mla_w_uq", "mla_w_ukv", "w_out", "expert_w_gate", "expert_w_up",
              "expert_w_down", "w_in_2", "w_out_2", "w_gate_2", "w_up_2", "w_down_2"):
        arrays[k] = np.asarray(i[k])
    return {k: np.ascontiguousarray(v) for k, v in arrays.items()}


def kernel(**inputs):
    import concourse.bacc as bacc
    from concourse.bass_utils import run_bass_kernel_spmd

    nc = bacc.Bacc("TRN2", target_bir_lowering=False, num_devices=1)
    arrays = packed(inputs)
    dram = {k: nc.dram_tensor(f"in_{k}", list(a.shape), mybir.dt.from_np(a.dtype), kind="ExternalInput").ap()
            for k, a in arrays.items()}
    out = nc.dram_tensor("out_x", [1, S, D], F32, kind="ExternalOutput").ap()
    build(nc, dram, out)
    r = run_bass_kernel_spmd(nc, [{f"in_{k}": a for k, a in arrays.items()}], core_ids=[0])
    return r.results[0]["out_x"]
```

```python
from contextlib import ExitStack, contextmanager

import numpy as np

import concourse.bass as bass
from concourse import mybir

F32 = mybir.dt.float32
F32R = mybir.dt.float32r
I32 = mybir.dt.int32
ALU = mybir.AluOpType
ACT = mybir.ActivationFunctionType
AX = mybir.AxisListType.X

P = 128
S = 512
T = S // P
D = 1024
KD = D // P
DEPTH = 2
BANK = 512
NBANK = 8
MASKED = -1e30
ALPHA = (2 * DEPTH) ** 0.25

MLA_H, NOPE, ROPE, MLA_V = 8, 64, 32, 64
QK = NOPE + ROPE
Q_RANK, KV_RANK = 256, 128
ML_H, ML_D = 4, 64
SSD_H, SSD_P, SSD_G, SSD_N, CONV = 4, 64, 2, 128, 5
PAD = CONV // 2
CQ = 0
CKV = CQ + Q_RANK
KR = CKV + KV_RANK
MQ = KR + ROPE
MK = MQ + ML_H * ML_D
MV = MK + ML_H * ML_D
MO = MV + ML_H * ML_D
MG = MO + ML_H * ML_D
SZ = MG + 4 * ML_H
XBC = SZ + SSD_H * SSD_P
NXBC = SSD_H * SSD_P + 2 * SSD_G * SSD_N
SDT = XBC + NXBC
IN1 = SDT + 2 * SSD_H
CC = NXBC // P
GROUPS, PER_GROUP = 4, 4
EXPERTS = GROUPS * PER_GROUP
NR = GROUPS + EXPERTS
SLOTS = 192
F_CH = 256

V_Q, V_KV, V_GB, V_MN, V_DTB, V_AL, V_SD, V_SN, V_RB = np.cumsum(
    [0, Q_RANK, KV_RANK, 4 * ML_H, ML_H * ML_D, 2 * SSD_H, 2 * SSD_H, SSD_H, SSD_H * SSD_P]).tolist()
NV1 = V_RB + NR

HD = 64
HALF = HD // 2
B_MQ, B_MK, B_MV, B_DQ, B_DK, B_DV, B_SQ, B_SK, B_SV, B_IQ, B_IK, B_IW, IN2 = np.cumsum(
    [0, 256, 256, 256, 512, 512, 512, 256, 256, 256, 512, 64, 8]).tolist()
IDX_H = 8
N_TOP = min(256, S // 4)
D_FF = 2816
FF_CH = D_FF // F_CH
V2_Q, V2_K, V2_L, V2_S = 0, 192, 384, 640
NV2 = 768

K_ID, K_GE, K_LE, K_ONES, K_CAUSAL, K_COS, K_SIN, K_INV, K_SLOT, NK = np.cumsum(
    [0, P, P, P, P, P, T * HALF, T * HALF, ROPE // 2, SLOTS]).tolist()


class Env:

    def __init__(self, nc):
        self.nc, self.ctx, self.sems = nc, None, {}

    def sem(self, stage, name):
        key = f"{stage}_{name}"
        if key not in self.sems:
            self.sems[key] = self.ctx.enter_context(self.nc.semaphore(key))
        return self.sems[key]

    @contextmanager
    def semaphores(self):
        with ExitStack() as ctx:
            self.ctx, self.sems = ctx, {}
            yield

    def end_layer(self):
        nums = [s.num for s in self.sems.values()]
        self.nc.all_engine_barrier(sems_to_clear=range(min(nums), max(nums) + 1))


class Link:

    def __init__(self, eng, sem):
        self.eng, self.sem, self.n = eng, sem, 0

    def __call__(self, ins):
        ins.then_inc(self.sem, 1)
        self.n += 1
        self.eng.wait_ge(self.sem, self.n)


def per_tile(ap, width):
    return ap.unsqueeze(2).to_broadcast([ap.shape[0], ap.shape[1], width])



class WeightStream:
    RAW, SPLIT, UNIT = 3, 2, 2048

    def __init__(self, env, sources):
        self.nc, self.env, self.sources, self.sent = env.nc, env, sources, 0
        self.loaded = [env.sem("stream", f"loaded{s}") for s in range(self.RAW)]
        self.hi_ready, self.lo_ready = env.sem("stream", "hi_ready"), env.sem("stream", "lo_ready")
        self.used = env.sem("stream", "used")

    def views(self, u, tile):
        a, b = self.sources[u].shape[1:]
        return tile[:, 0:a * b].rearrange("p (a b) -> p a b", a=a)

    def load(self, sp, upto):
        for u in range(self.sent, min(upto, len(self.sources))):
            if u >= self.RAW:
                sp.wait_ge(self.lo_ready, u - self.RAW + 1)
            sp.dma_start(self.views(u, self.env.raw[:, u % self.RAW]), self.sources[u]
                         ).then_inc(self.loaded[u % self.RAW], 16)
            self.sent = u + 1

    def split_hi(self, act, u):
        act.wait_ge(self.loaded[u % self.RAW], 16 * (u // self.RAW + 1))
        if u >= self.SPLIT:
            act.wait_ge(self.used, u - self.SPLIT + 1)
        n = int(np.prod(self.sources[u].shape[1:]))
        self.nc.scalar.activation(self.env.w_hi[:, u % self.SPLIT, 0:n], self.env.raw[:, u % self.RAW, 0:n], ACT.Copy
                                  ).then_inc(self.hi_ready, 1)

    def split_lo(self, eng, u):
        eng.wait_ge(self.hi_ready, u + 1)
        n = int(np.prod(self.sources[u].shape[1:]))
        eng.tensor_tensor(self.env.w_lo[:, u % self.SPLIT, 0:n], self.env.raw[:, u % self.RAW, 0:n],
                                     self.env.w_hi[:, u % self.SPLIT, 0:n].bitcast(F32), ALU.subtract
                                     ).then_inc(self.lo_ready, 1)

    def ready(self, pe, u):
        pe.wait_ge(self.lo_ready, u + 1)
        return self.views(u, self.env.w_hi[:, u % self.SPLIT]), self.views(u, self.env.w_lo[:, u % self.SPLIT])


def product(nc, out, a, b, start, stop, **more):
    nc.tensor.matmul(out, a[0], b[0], start=start, stop=False, **more)
    nc.tensor.matmul(out, a[0], b[1], start=False, stop=False, **more)
    return nc.tensor.matmul(out, a[1], b[0], start=False, stop=stop, **more)


def exact_product(nc, out, a, b, start, stop, **more):
    if isinstance(a, tuple):
        nc.tensor.matmul(out, a[0], b, start=start, stop=False, **more)
        return nc.tensor.matmul(out, a[1], b, start=False, stop=stop, **more)
    nc.tensor.matmul(out, a, b[0], start=start, stop=False, **more)
    return nc.tensor.matmul(out, a, b[1], start=False, stop=stop, **more)


def transpose_stage(env, stage, jobs):
    nc, ps, ident = env.nc, env.ps, env.ident
    pairs = isinstance(jobs[0][1], tuple)
    turned = env.sem(stage, "turned")
    act_copied, dve_copied = env.sem(stage, "act_copied"), env.sem(stage, "dve_copied")

    with nc.Block() as block:
        @block.tensor
        def _(pe):
            for i, (srcs, dst, scale) in enumerate(jobs):
                if i >= NBANK:
                    if pairs:
                        pe.wait_ge(dve_copied, i - NBANK + 1)
                    else:
                        pe.wait_ge(dve_copied if i % 2 else act_copied, (i - NBANK) // 2 + 1)
                for j, src in enumerate(srcs):
                    w = src.shape[1]
                    last = nc.tensor.transpose(ps[0:w, i % NBANK, j * P:(j + 1) * P], src, ident)
                last.then_inc(turned, 1)

        def bank(eng, i):
            srcs, dst, scale = jobs[i]
            eng.wait_ge(turned, i + 1)
            return ps[0:srcs[0].shape[1], i % NBANK, 0:len(srcs) * P], dst, scale

        @block.scalar
        def _(act):
            for i in range(0, len(jobs), 1 if pairs else 2):
                src, dst, scale = bank(act, i)
                nc.scalar.activation(dst[0] if pairs else dst, src, ACT.Copy if scale is None else ACT.Identity,
                                     scale=1.0 if scale is None else scale).then_inc(act_copied, 1)

        @block.vector
        def _(dve):
            for i in range(0 if pairs else 1, len(jobs), 1 if pairs else 2):
                src, dst, scale = bank(dve, i)
                if pairs:
                    dve.wait_ge(act_copied, i + 1)
                    hi = dst[0].bitcast(F32)
                    if scale is None:
                        ins = nc.vector.tensor_tensor(dst[1], src, hi, ALU.subtract)
                    else:
                        ins = nc.vector.scalar_tensor_tensor(out=dst[1], in0=src, scalar=scale, in1=hi,
                                                             op0=ALU.mult, op1=ALU.subtract)
                elif scale is None:
                    ins = nc.vector.tensor_copy(dst, src)
                else:
                    ins = nc.vector.tensor_scalar(dst, src, scale, None, ALU.mult)
                ins.then_inc(dve_copied, 1)


def weight_units(weights, width=BANK, rows=4 * P):
    K, N = weights.shape
    return [weights[r:min(r + rows, K), c:min(c + width, N)].rearrange("(k p) w -> p k w", p=P)
            for c in range(0, N, width) for r in range(0, K, rows)]


def project_stage(env, stage, first, jobs, alpha_x=None, prefetch=0):
    nc, ps, stream = env.nc, env.ps, env.stream
    act_done, dve_done = env.sem(stage, "act_stored"), env.sem(stage, "dve_stored")
    ends, units = [], []
    for c, (lhs, parts, w, pieces) in enumerate(jobs):
        for n, ks in enumerate(parts):
            units.append((c, ks, n == 0, n == len(parts) - 1))
        ends.append(len(units) - 1)
    N = len(units)

    def bank(c, t):
        return ps[:, (c % 2) * T + t, :]

    with nc.Block() as block:
        @block.sync
        def _(sp):
            stream.load(sp, first + N + prefetch)

        @block.tensor
        def _(pe):
            for n, (c, ks, is_first, is_last) in enumerate(units):
                lhs, parts, w, pieces = jobs[c]
                if is_first and c >= 2:
                    pe.wait_ge(dve_done, c - 1)
                    if alpha_x is None:
                        pe.wait_ge(act_done, c - 1)
                w_hi, w_lo = stream.ready(pe, first + n)
                for t in range(T):
                    for j, k in enumerate(ks):
                        a = tuple(x[:, t * P:(t + 1) * P] for x in lhs[k])
                        last = product(nc, bank(c, t)[:, 0:w], a, (w_hi[:, j], w_lo[:, j]),
                                       is_first and j == 0, is_last and j == len(ks) - 1)
                last.then_inc(stream.used, 1)

        @block.scalar
        def _(act):
            def store(c):
                act.wait_ge(stream.used, first + ends[c] + 1)
                for t in (0, 2):
                    for view, dst in jobs[c][3]:
                        last = nc.scalar.activation(dst(t), view(bank(c, t)), ACT.Copy)
                last.then_inc(act_done, 1)

            for n in range(N + 2):
                if n < N:
                    stream.split_hi(act, first + n)
                if alpha_x is None and n - 2 in ends:
                    store(ends.index(n - 2))

        @block.vector
        def _(dve):
            def store(c):
                dve.wait_ge(stream.used, first + ends[c] + 1)
                for t in (1, 3) if alpha_x is None else range(T):
                    for view, dst in jobs[c][3]:
                        d, src = dst(t), view(bank(c, t))
                        if alpha_x is None:
                            last = nc.vector.tensor_copy(d, src)
                        else:
                            last = nc.vector.scalar_tensor_tensor(out=d, in0=d, scalar=alpha_x, in1=src,
                                                                  op0=ALU.mult, op1=ALU.add)
                last.then_inc(dve_done, 1)

            for n in range(N + 2):
                if n < N:
                    stream.split_lo(dve, first + n)
                if n - 2 in ends:
                    store(ends.index(n - 2))


def attention_stage(env, stage, units, scale, prob=None, prob_t=None, prefetch=0):
    nc, ps, ident, causal = env.nc, env.ps, env.ident, env.causal
    N = len(units)
    scores_ready, max_ready = env.sem(stage, "scores_ready"), env.sem(stage, "max_ready")
    exp_done, turned = env.sem(stage, "exp_done"), env.sem(stage, "turned")
    turned_copied, out_ready = env.sem(stage, "turned_copied"), env.sem(stage, "out_ready")
    out_stored, step = env.sem(stage, "out_stored"), env.sem(stage, "vector_step")

    with ExitStack() as local:
        if prob is None:
            prob = local.enter_context(nc.sbuf_tensor(f"{stage}_prob", [P, 4, S], F32))
            prob_t = local.enter_context(nc.sbuf_tensor(f"{stage}_prob_t", [P, 2, S], F32))
        top = local.enter_context(nc.sbuf_tensor(f"{stage}_top", [P, N], F32))
        total = local.enter_context(nc.sbuf_tensor(f"{stage}_total", [P, N], F32))
        recip = local.enter_context(nc.sbuf_tensor(f"{stage}_recip", [P, N], F32))

        def score_bank(i, nk):
            return ps[:, i % 4, 0:nk]

        with nc.Block() as block:
            @block.sync
            def _(sp):
                env.stream.load(sp, prefetch)

            @block.tensor
            def _(pe):
                for i in range(N + 4):
                    if i < N:
                        u = units[i]
                        if i >= 4:
                            pe.wait_ge(exp_done, i - 3)
                        nc.tensor.matmul(score_bank(i, u["nk"]), u["q"], u["k"], start=True, stop=True
                                         ).then_inc(scores_ready, 1)
                    if 3 <= i < N + 3:
                        j = i - 3
                        pe.wait_ge(exp_done, j + 1)
                        if j >= 2:
                            pe.wait_ge(turned_copied, j - 1)
                        for b in range(units[j]["nk"] // P):
                            last = nc.tensor.transpose(ps[:, 4 + j % 2, b * P:(b + 1) * P],
                                                       prob[:, j % 4, b * P:(b + 1) * P], ident)
                        last.then_inc(turned, 1)
                    if i >= 4:
                        j = i - 4
                        u = units[j]
                        nb = u["nk"] // P
                        pe.wait_ge(turned_copied, j + 1)
                        if j >= 2:
                            pe.wait_ge(out_stored, j - 1)
                        for b in range(nb):
                            w = u["v"][b].shape[1]
                            last = nc.tensor.matmul(ps[:, 6 + j % 2, 0:w], prob_t[:, j % 2, b * P:(b + 1) * P],
                                                    u["v"][b], start=(b == 0), stop=(b == nb - 1))
                        last.then_inc(out_ready, 1)

            @block.vector
            def _(dve):
                link = Link(dve, step)
                for i in range(N + 4):
                    if i < N:
                        u = units[i]
                        dve.wait_ge(scores_ready, i + 1)
                        sc = score_bank(i, u["nk"])
                        if u["mask"] == "diag":
                            last = ps[:, i % 4, u["nk"] - P:u["nk"]]
                            link(nc.vector.tensor_tensor(last, last, causal, ALU.add))
                        elif u["mask"] is not None:
                            link(nc.vector.tensor_tensor(sc, sc, u["mask"], ALU.add))
                        link(nc.vector.reduce_max(top[:, i:i + 1], sc, AX))
                        nc.vector.tensor_scalar(top[:, i:i + 1], top[:, i:i + 1], -scale, None, ALU.mult
                                                ).then_inc(max_ready, 1)
                    if i >= 4:
                        j = i - 4
                        u = units[j]
                        dve.wait_ge(exp_done, j + 1)
                        link(nc.vector.reciprocal(recip[:, j:j + 1], total[:, j:j + 1]))
                        dve.wait_ge(out_ready, j + 1)
                        nc.vector.tensor_scalar(u["dst"], ps[:, 6 + j % 2, 0:u["dst"].shape[1]], recip[:, j:j + 1],
                                                None, ALU.mult).then_inc(out_stored, 1)

            @block.scalar
            def _(act):
                for i in range(N + 3):
                    if i >= 3:
                        j = i - 3
                        nk = units[j]["nk"]
                        act.wait_ge(turned, j + 1)
                        if j >= 2:
                            act.wait_ge(out_ready, j - 1)
                        nc.scalar.activation(prob_t[:, j % 2, 0:nk], ps[:, 4 + j % 2, 0:nk], ACT.Copy
                                             ).then_inc(turned_copied, 1)
                    if i < N:
                        u = units[i]
                        act.wait_ge(max_ready, i + 1)
                        if i >= 4:
                            act.wait_ge(turned, i - 3)
                        nc.scalar.activation(prob[:, i % 4, 0:u["nk"]], score_bank(i, u["nk"]), ACT.Exp,
                                             bias=top[:, i:i + 1], scale=scale,
                                             accum_out=total[:, i:i + 1]).then_inc(exp_done, 1)


def layernorm_stage(env, stage, gains, x):
    nc = env.nc
    names = ("gains_loaded", "var_ready", "root_ready", "shift_ready", "centred", "times_g", "vector_step")
    gains_loaded, var_ready, root_ready, shift_ready, centred, times_g, step = (env.sem(stage, n) for n in names)
    with ExitStack() as local:
        gb = local.enter_context(nc.sbuf_tensor(f"{stage}_gb", [P, 2 * D], F32))
        st = local.enter_context(nc.sbuf_tensor(f"{stage}_stats", [P, T, 2, 6], F32))
        mv = local.enter_context(nc.sbuf_tensor(f"{stage}_mv", [P, T, 2], F32))
        rs = local.enter_context(nc.sbuf_tensor(f"{stage}_rs", [P, T], F32))
        shift = local.enter_context(nc.sbuf_tensor(f"{stage}_shift", [P, T], F32))
        with nc.Block() as block:
            @block.sync
            def _(sp):
                sp.dma_start(gb[:, :], gains.to_broadcast([P, 2 * D])).then_inc(gains_loaded, 16)

            @block.vector
            def _(dve):
                link = Link(dve, step)
                v = nc.vector
                for t in range(T):
                    for h in range(2):
                        last = v.bn_stats(st[:, t, h, :], x[:, t, h * BANK:(h + 1) * BANK])
                link(last)
                for t in range(T):
                    last = v.bn_aggr(mv[:, t, :], st[:, t, :, :])
                last.then_inc(var_ready, 1)
                dve.wait_ge(root_ready, 1)
                link(v.reciprocal(rs[:, :], rs[:, :]))
                v.scalar_tensor_tensor(out=shift[:, :], in0=mv[:, :, 0], scalar=-1.0, in1=rs[:, :],
                                       op0=ALU.mult, op1=ALU.mult).then_inc(shift_ready, 1)
                dve.wait_ge(gains_loaded, 16)
                for t in range(T):
                    dve.wait_ge(centred, t + 1)
                    v.tensor_tensor(x[:, t, :], x[:, t, :], gb[:, 0:D], ALU.mult).then_inc(times_g, 1)
                for t in range(2, T):
                    dve.wait_ge(times_g, t + 1)
                    v.tensor_tensor(x[:, t, :], x[:, t, :], gb[:, D:2 * D], ALU.add)

            @block.scalar
            def _(act):
                act.wait_ge(var_ready, 1)
                nc.scalar.activation(rs[:, :], mv[:, :, 1], ACT.Sqrt, bias=env.eps5).then_inc(root_ready, 1)
                act.wait_ge(shift_ready, 1)
                for t in range(T):
                    nc.scalar.activation(x[:, t, :], x[:, t, :], ACT.Identity, scale=rs[:, t:t + 1],
                                         bias=shift[:, t:t + 1]).then_inc(centred, 1)

            @block.gpsimd
            def _(pool):
                pool.wait_ge(gains_loaded, 16)
                for t in range(2):
                    pool.wait_ge(times_g, t + 1)
                    nc.gpsimd.tensor_tensor(x[:, t, :], x[:, t, :], gb[:, D:2 * D], ALU.add)


def ffn_stage(env, stage, first, xt, chunks, x, prefetch=0):
    nc, ps, stream = env.nc, env.ps, env.stream
    FC = F_CH // P
    nf = chunks * FC
    names = ("silu_done", "times_up_done", "hidden_hi", "hidden_lo", "stored")
    gated, sized, hidden_hi, hidden_lo, stored = (env.sem(stage, n) for n in names)
    downs = [(half, list(range(f, min(f + 4, nf)))) for half in range(2) for f in range(0, nf, 4)]
    first_down = 2 * chunks
    N = first_down + len(downs)

    with ExitStack() as local:
        h_hi = local.enter_context(nc.sbuf_tensor(f"{stage}_h_hi", [P, nf, S], F32R))
        h_lo = local.enter_context(nc.sbuf_tensor(f"{stage}_h_lo", [P, nf, S], F32R))
        gate = local.enter_context(nc.sbuf_tensor(f"{stage}_gate", [P, 2, S], F32))

        def bank(c, up, f):
            return ps[:, (c % 2) * 4 + 2 * up + f, :]

        def out_bank(half, t):
            return ps[:, (chunks + half) % 2 * T + t, :]

        with nc.Block() as block:
            @block.sync
            def _(sp):
                stream.load(sp, first + N + prefetch)

            @block.tensor
            def _(pe):
                for n in range(first_down):
                    c, up = n // 2, n % 2
                    if c >= 2 and up == 0:
                        pe.wait_ge(sized, FC * (c - 1))
                    w_hi, w_lo = stream.ready(pe, first + n)
                    for f in range(FC):
                        cols = slice(f * P, (f + 1) * P)
                        for k in range(KD):
                            last = product(nc, bank(c, up, f), (w_hi[:, k, cols], w_lo[:, k, cols]),
                                           (xt[0][:, k, :], xt[1][:, k, :]), k == 0, k == KD - 1)
                    last.then_inc(stream.used, 1)
                for m, (half, fs) in enumerate(downs):
                    if m == 0:
                        pe.wait_ge(sized, nf - FC)
                    if half and not downs[m - 1][0]:
                        pe.wait_ge(sized, nf)
                    pe.wait_ge(hidden_lo, min(nf, fs[-1] + 1))
                    w_hi, w_lo = stream.ready(pe, first + first_down + m)
                    for t in range(T):
                        for j, f in enumerate(fs):
                            a = tuple(h[:, f, t * P:(t + 1) * P] for h in (h_hi, h_lo))
                            last = product(nc, out_bank(half, t), a, (w_hi[:, j], w_lo[:, j]),
                                           f == 0, f == nf - 1)
                    last.then_inc(stream.used, 1)

            @block.scalar
            def _(act):
                for n in range(N + 2):
                    if n < N:
                        stream.split_hi(act, first + n)
                    m = n - 2
                    if not 0 <= m < first_down:
                        continue
                    act.wait_ge(stream.used, first + m + 1)
                    c, up = m // 2, m % 2
                    for f in range(FC):
                        i = c * FC + f
                        if not up:
                            if c:
                                act.wait_ge(hidden_lo, i - FC + 1)
                            nc.scalar.activation(gate[:, f, :], bank(c, 0, f), ACT.Silu).then_inc(gated, 1)
                        else:
                            act.wait_ge(sized, i + 1)
                            nc.scalar.activation(h_hi[:, i, :], gate[:, f, :], ACT.Copy).then_inc(hidden_hi, 1)

            @block.vector
            def _(dve):
                for n in range(N + 2):
                    if n < N:
                        stream.split_lo(dve, first + n)
                    m = n - 2
                    if 0 <= m < first_down and m % 2:
                        c = m // 2
                        dve.wait_ge(stream.used, first + m + 1)
                        for f in range(FC):
                            dve.wait_ge(gated, c * FC + f + 1)
                            nc.vector.tensor_tensor(gate[:, f, :], gate[:, f, :], bank(c, 1, f), ALU.mult
                                                    ).then_inc(sized, 1)
                        for f in range(FC):
                            i = c * FC + f
                            dve.wait_ge(hidden_hi, i + 1)
                            nc.vector.tensor_tensor(h_lo[:, i, :], gate[:, f, :], h_hi[:, i, :].bitcast(F32),
                                                    ALU.subtract).then_inc(hidden_lo, 1)
                    if m - first_down in (len(downs) // 2 - 1, len(downs) - 1):
                        half = downs[m - first_down][0]
                        dve.wait_ge(stream.used, first + m + 1)
                        for t in range(T):
                            d = x[:, t, half * BANK:(half + 1) * BANK]
                            nc.vector.tensor_tensor(d, d, out_bank(half, t), ALU.add).then_inc(stored, 1)


def by_head(ap, heads):
    return ap.rearrange("p (h c) -> p h c", h=heads)


def x_transposes(env, src, dst, scale=None):
    return [([src[:, t, k * P:(k + 1) * P] for t in range(T)], dst[:, k, :],
             None if scale is None else scale[:, k:k + 1]) for k in range(KD)]


def pair_transposes(src, pair, scale=None):
    return [([src(t, k) for t in range(T)], (pair[0][:, k, :], pair[1][:, k, :]),
             None if scale is None else scale[:, k:k + 1]) for k in range(KD)]



def rope_table_stage(env, positions, cos, sin):
    nc = env.nc
    TWO_PI = 2 * np.pi
    C1 = 6.28125
    C2 = float(np.float32(np.floor((TWO_PI - C1) * 2 ** 21) / 2 ** 21))
    C3 = float(np.float32(TWO_PI - C1 - C2))
    ROUND = 1.5 * 2 ** 23
    pos_loaded, reduced, sines = (env.sem("rope_table", n) for n in ("pos_loaded", "reduced", "sines"))
    step = env.sem("rope_table", "vector_step")
    n = T * ROPE // 2
    with ExitStack() as local:
        pos_i = local.enter_context(nc.sbuf_tensor("rope_pos_i", [P, T], I32))
        pos = local.enter_context(nc.sbuf_tensor("rope_pos", [P, T], F32))
        ang = local.enter_context(nc.sbuf_tensor("rope_ang", [P, T, ROPE // 2], F32))
        turns = local.enter_context(nc.sbuf_tensor("rope_turns", [P, T, ROPE // 2], F32))
        half = local.enter_context(nc.sbuf_tensor("rope_half", [P, T, ROPE // 2], F32))
        with nc.Block() as block:
            @block.sync
            def _(sp):
                sp.dma_start(pos_i[:, :], positions.rearrange("a (t p) -> p (a t)", p=P),
                             allow_slow_non_contiguous=True).then_inc(pos_loaded, 16)

            @block.vector
            def _(dve):
                link = Link(dve, step)
                dve.wait_ge(pos_loaded, 16)
                link(nc.vector.tensor_copy(pos[:, :], pos_i[:, :]))
                inv = env.consts[:, K_INV:K_INV + ROPE // 2].unsqueeze(1).to_broadcast([P, T, ROPE // 2])
                link(nc.vector.tensor_tensor(ang[:, :, :], per_tile(pos[:, :], ROPE // 2), inv, ALU.mult))
                link(nc.vector.tensor_scalar(turns[:, :, :], ang[:, :, :], 1 / TWO_PI, ROUND, ALU.mult, ALU.add))
                link(nc.vector.tensor_scalar(turns[:, :, :], turns[:, :, :], -ROUND, None, ALU.add))
                for c in (C1, C2, C3):
                    link(nc.vector.scalar_tensor_tensor(out=ang[:, :, :], in0=turns[:, :, :], scalar=-c,
                                                        in1=ang[:, :, :], op0=ALU.mult, op1=ALU.add))
                nc.vector.tensor_scalar(ang[:, :, :], ang[:, :, :], float(np.float32(3.1415925)),
                                        float(np.float32(-3.1415925)), ALU.min, ALU.max).then_inc(reduced, 1)
                dve.wait_ge(sines, 2)
                link(nc.vector.tensor_tensor(half[:, :, :], half[:, :, :], half[:, :, :], ALU.mult))
                nc.vector.tensor_scalar(cos, half[:, :, :], -2.0, 1.0, ALU.mult, ALU.add)

            @block.scalar
            def _(act):
                act.wait_ge(reduced, 1)
                nc.scalar.activation(sin, ang[:, :, :], ACT.Sin).then_inc(sines, 1)
                nc.scalar.activation(half[:, :, :], ang[:, :, :], ACT.Sin, scale=0.5).then_inc(sines, 1)


def rope(nc, link, x1, x2, cos, sin, a, b, shape):
    c, s = (t.to_broadcast(shape) for t in (cos, sin))
    nc_v = nc.vector
    link(nc_v.tensor_tensor(a, x1, s, ALU.mult))
    link(nc_v.tensor_tensor(b, x2, s, ALU.mult))
    link(nc_v.tensor_tensor(x1, x1, c, ALU.mult))
    link(nc_v.tensor_tensor(x2, x2, c, ALU.mult))
    link(nc_v.tensor_tensor(x1, x1, b, ALU.subtract))
    link(nc_v.tensor_tensor(x2, x2, a, ALU.add))


def latent_norm_stage(env, proj, vec, cqn):
    nc = env.nc
    squares, roots, step = (env.sem("latent_norm", n) for n in ("squares_summed", "roots", "vector_step"))
    parts = ((CQ, Q_RANK, V_Q, 0), (CKV, KV_RANK, V_KV, Q_RANK))
    with ExitStack() as local:
        ss = local.enter_context(nc.sbuf_tensor("latent_ss", [P, 2, T], F32))
        with nc.Block() as block:
            @block.vector
            def _(dve):
                link = Link(dve, step)
                for n, (c, w, g, o) in enumerate(parts):
                    for t in range(T):
                        src = proj[:, t, c:c + w]
                        last = nc.vector.tensor_tensor_reduce(out=cqn[:, t, o:o + w], in0=src, in1=src, scale=1.0,
                                                              scalar=0.0, op0=ALU.mult, op1=ALU.add,
                                                              accum_out=ss[:, n, t:t + 1])
                last.then_inc(squares, 1)
                dve.wait_ge(roots, 2)
                link(nc.vector.reciprocal(ss[:, :, :], ss[:, :, :]))
                for n, (c, w, g, o) in enumerate(parts):
                    for t in range(T):
                        nc.vector.scalar_tensor_tensor(out=cqn[:, t, o:o + w], in0=proj[:, t, c:c + w],
                                                       scalar=ss[:, n, t:t + 1], in1=vec[:, g:g + w],
                                                       op0=ALU.mult, op1=ALU.mult)

            @block.scalar
            def _(act):
                act.wait_ge(squares, 1)
                for n, (c, w, g, o) in enumerate(parts):
                    nc.scalar.activation(ss[:, n, :], ss[:, n, :], ACT.Sqrt, scale=1.0 / w, bias=env.eps6
                                         ).then_inc(roots, 1)


def mla_rope_stage(env, proj, qn, kn, cos, sin):
    nc = env.nc
    step = env.sem("mla_rope", "vector_step")
    H2 = ROPE // 2
    with ExitStack() as local:
        a = local.enter_context(nc.sbuf_tensor("mla_rope_a", [P, T, MLA_H, H2], F32))
        b = local.enter_context(nc.sbuf_tensor("mla_rope_b", [P, T, MLA_H, H2], F32))
        with nc.Block() as block:
            @block.vector
            def _(dve):
                link = Link(dve, step)
                rope(nc, link, qn[:, :, :, NOPE:NOPE + H2], qn[:, :, :, NOPE + H2:QK], cos.unsqueeze(2), sin.unsqueeze(2),
                     a[:, :, :, :], b[:, :, :, :], [P, T, MLA_H, H2])
                rope(nc, link, proj[:, :, KR:KR + H2], proj[:, :, KR + H2:KR + ROPE], cos, sin,
                     a[:, :, 0, :], b[:, :, 0, :], [P, T, H2])
                src = proj[:, :, KR:KR + ROPE].unsqueeze(2).to_broadcast([P, T, MLA_H, ROPE])
                nc.vector.tensor_copy(kn[:, :, :, NOPE:QK], src)


def gates_stage(env, proj, vec, gates, dt, vx):
    nc = env.nc
    ready, exp_done, ln_done = (env.sem("gates", n) for n in ("abs_ready", "exp_done", "ln_done"))
    a_exp, step, pool_step = (env.sem("gates", n) for n in ("a_exp", "vector_step", "pool_step"))
    with ExitStack() as local:
        pre = local.enter_context(nc.sbuf_tensor("gates_pre", [P, T, 16], F32))
        e = local.enter_context(nc.sbuf_tensor("gates_e", [P, T, 16], F32))
        u = local.enter_context(nc.sbuf_tensor("gates_u", [P, T, 16], F32))
        one = local.enter_context(nc.sbuf_tensor("gates_one", [P, T, 16], F32))
        ln = local.enter_context(nc.sbuf_tensor("gates_ln", [P, T, 16], F32))
        na = local.enter_context(nc.sbuf_tensor("gates_na", [P, 8], F32))
        with nc.Block() as block:
            @block.vector
            def _(dve):
                link = Link(dve, step)
                v = nc.vector
                for kind, dst in ((0, gates[:, :, 0:4]), (2, gates[:, :, 4:8]), (1, pre[:, :, 0:4]), (3, pre[:, :, 4:8])):
                    c = MG + kind * ML_H
                    bias = vec[:, V_GB + kind * ML_H:V_GB + (kind + 1) * ML_H].unsqueeze(1).to_broadcast([P, T, ML_H])
                    link(v.tensor_tensor(dst, proj[:, :, c:c + ML_H], bias, ALU.add))
                bias = vec[:, V_DTB:V_DTB + 8].unsqueeze(1).to_broadcast([P, T, 8])
                link(v.tensor_tensor(pre[:, :, 8:16], proj[:, :, SDT:SDT + 8], bias, ALU.add))
                v.scalar_tensor_tensor(out=e[:, :, :], in0=pre[:, :, :], scalar=-1.0, in1=pre[:, :, :],
                                       op0=ALU.mult, op1=ALU.max).then_inc(ready, 1)
                dve.wait_ge(exp_done, 1)
                link(v.tensor_scalar(u[:, :, :], e[:, :, :], 1.0, None, ALU.add))
                link(v.tensor_scalar(u[:, :, :], u[:, :, :], -1.0, None, ALU.add))
                link(v.tensor_scalar(one[:, :, :], u[:, :, :], 0.0, None, ALU.is_equal))
                link(v.tensor_tensor(one[:, :, :], one[:, :, :], e[:, :, :], ALU.mult))
                link(v.tensor_scalar(u[:, :, :], u[:, :, :], 1e-30, None, ALU.max))
                link(v.reciprocal(u[:, :, :], u[:, :, :]))
                link(v.tensor_tensor(u[:, :, :], u[:, :, :], e[:, :, :], ALU.mult))
                dve.wait_ge(ln_done, 1)
                link(v.tensor_tensor(ln[:, :, :], ln[:, :, :], u[:, :, :], ALU.mult))
                link(v.tensor_tensor(ln[:, :, :], ln[:, :, :], one[:, :, :], ALU.add))
                link(v.scalar_tensor_tensor(out=gates[:, :, 8:16], in0=pre[:, :, 0:8], scalar=0.0,
                                            in1=ln[:, :, 0:8], op0=ALU.min, op1=ALU.subtract))
                link(v.scalar_tensor_tensor(out=dt, in0=pre[:, :, 8:16], scalar=0.0,
                                            in1=ln[:, :, 8:16], op0=ALU.max, op1=ALU.add))
                dve.wait_ge(a_exp, 1)
                a = na[:, :].unsqueeze(1).to_broadcast([P, T, 8])
                link(v.tensor_tensor(gates[:, :, 16:24], dt, a, ALU.mult))
                v.tensor_scalar(gates[:, :, 16:24], gates[:, :, 16:24], -1.0, None, ALU.mult)

            @block.scalar
            def _(act):
                nc.scalar.activation(na[:, :], vec[:, V_AL:V_AL + 8], ACT.Exp).then_inc(a_exp, 1)
                act.wait_ge(ready, 1)
                nc.scalar.activation(e[:, :, :], e[:, :, :], ACT.Exp, scale=-1.0).then_inc(exp_done, 1)
                act.wait_ge(exp_done, 1)
                nc.scalar.activation(ln[:, :, :], e[:, :, :], ACT.Ln, bias=1.0).then_inc(ln_done, 1)

            @block.gpsimd
            def _(pool):
                for t in range(T):
                    nc.gpsimd.tensor_copy(vx[:, t, :, 0:ML_D],
                                          proj[:, t, MV:MV + ML_H * ML_D].rearrange("p (h c) -> p h c", h=ML_H))
                nc.gpsimd.memset(vx[:, :, :, ML_D:ML_D + 1], 1.0)


def scan_stage(env, gates, cols):
    nc, ps, ident = env.nc, env.ps, env.ident
    turned, copied, scanned, back = (env.sem("scan", n) for n in ("turned", "copied", "scanned", "turned_back"))
    step = env.sem("scan", "vector_step")
    R = slice(None, None, -1)
    with ExitStack() as local:
        def tile(name, rows):
            return local.enter_context(nc.sbuf_tensor(f"scan_{name}", [rows, S], F32))
        ig, lf = tile("ig", 8), tile("lf", 16)
        sums = [tile("sum_f", 16), tile("sum_b", 16)]
        c = [tile("c_f", 8), tile("c_b", 8)]
        mx = [tile("max_f", 8), tile("max_b", 8)]
        m = [tile("m_f", 8), tile("m_b", 8)]
        with nc.Block() as block:
            @block.tensor
            def _(pe):
                for t in range(T):
                    nc.tensor.transpose(ps[0:8, 0, t * P:(t + 1) * P], gates[:, t, 0:8], ident)
                    last = nc.tensor.transpose(ps[0:16, 1, t * P:(t + 1) * P], gates[:, t, 8:24], ident)
                last.then_inc(turned, 1)
                pe.wait_ge(scanned, 1)
                for t in range(T):
                    for q, (src, rows, first) in enumerate(((c, 8, 0), (mx, 8, 0), (m, 8, 0), (sums, 16, 8))):
                        for d in range(2):
                            o = q * 8 + d * 4
                            last = nc.tensor.matmul(ps[:, 2, t * 32 + o:t * 32 + o + 4],
                                                    src[d][0:rows, t * P:(t + 1) * P],
                                                    ident[0:rows, first + d * 4:first + d * 4 + 4],
                                                    start=True, stop=True)
                last.then_inc(back, 1)

            @block.vector
            def _(dve):
                link = Link(dve, step)
                v = nc.vector
                dve.wait_ge(turned, 1)
                link(v.tensor_copy(ig[:, :], ps[0:8, 0, :]))
                link(v.tensor_copy(lf[:, :], ps[0:16, 1, :]))
                for d, w in ((0, slice(None)), (1, R)):
                    link(v.tensor_tensor_scan(sums[d][:, w], lf[:, w], lf[:, w], 0.0, ALU.add, ALU.bypass))
                    link(v.tensor_tensor(c[d][:, :], ig[:, :], sums[d][0:8, :], ALU.subtract))
                    link(v.tensor_tensor_scan(mx[d][:, w], c[d][:, w], c[d][:, w], -3e38, ALU.max, ALU.bypass))
                    last = v.tensor_tensor(m[d][:, :], mx[d][:, :], sums[d][0:8, :], ALU.add)
                last.then_inc(scanned, 1)
                dve.wait_ge(back, 1)
                src = ps[:, 2, 0:T * 32].rearrange("p (t c) -> p t c", t=T)
                v.tensor_copy(cols[:, :, 0:24], src[:, :, 0:24])
                v.tensor_scalar(cols[:, :, 24:32], src[:, :, 24:32], -1.0, None, ALU.mult)


def conv_stage(env, xc, convw, conv_out):
    nc = env.nc
    step, ready = env.sem("conv", "vector_step"), env.sem("conv", "conv_ready")
    with nc.Block() as block:
        @block.vector
        def _(dve):
            link = Link(dve, step)
            for j in range(CONV):
                for c in range(CC):
                    src, dst, w = xc[:, c, j:j + S], conv_out[:, c, :], convw[:, c, j:j + 1]
                    if j == 0:
                        ins = nc.vector.tensor_scalar(dst, src, w, convw[:, c, CONV:CONV + 1], ALU.mult, ALU.add)
                    else:
                        dve.wait_ge(step, (j - 1) * CC + c + 1)
                        ins = nc.vector.scalar_tensor_tensor(out=dst, in0=src, scalar=w, in1=dst,
                                                             op0=ALU.mult, op1=ALU.add)
                    ins.then_inc(step, 1)

        @block.scalar
        def _(act):
            for c in range(CC):
                act.wait_ge(step, (CONV - 1) * CC + c + 1)
                nc.scalar.activation(conv_out[:, c, :], conv_out[:, c, :], ACT.Silu)


def decay_stage(env, units, cols):
    nc, ps, ident = env.nc, env.ps, env.ident
    N = len(units)
    names = ("products_ready", "row_ready", "gap_ready", "exp_done", "weighted", "masked", "out_ready",
             "out_stored", "vector_step")
    products_ready, row_ready, gap_ready, exp_done, weighted, masked, out_ready, out_stored, step = (
        env.sem("decay", n) for n in names)
    new_group = [i == 0 or units[i]["group"] != units[i - 1]["group"] for i in range(N)]

    def span(u, i):
        return (0, (i + 1) * P) if u["back"] else (i * P, S)

    with ExitStack() as local:
        gap = local.enter_context(nc.sbuf_tensor("decay_gap", [P, 2, T, S], F32))
        wq = local.enter_context(nc.sbuf_tensor("decay_weighted", [P, 2, T, S], F32))
        tmp = local.enter_context(nc.sbuf_tensor("decay_tmp", [P, T, 4], F32))
        with nc.Block() as block:
            @block.tensor
            def _(pe):
                for i in range(N + 1):
                    if i < N:
                        u = units[i]
                        if i >= 2:
                            pe.wait_ge(gap_ready, T * (i - 1))
                        for t in range(T):
                            r = cols[:, t, u["row"]:u["row"] + 1].to_broadcast([P, P])
                            last = nc.tensor.matmul(ps[:, 4 + i % 2, t * P:(t + 1) * P], r, ident, start=True, stop=True)
                        last.then_inc(row_ready, 1)
                        if new_group[i]:
                            if i:
                                pe.wait_ge(weighted, T * i)
                            for s in range(T):
                                last = nc.tensor.matmul(ps[:, s, :], u["k"][:, s * P:(s + 1) * P], u["q"],
                                                        start=True, stop=True)
                            last.then_inc(products_ready, 1)
                    if i >= 1:
                        j = i - 1
                        u = units[j]
                        pe.wait_ge(masked, T * (j + 1))
                        if j >= 2:
                            pe.wait_ge(out_stored, j - 1)
                        for t in range(T):
                            keys = range(t, T) if u["back"] else range(0, t + 1)
                            for s in keys:
                                last = nc.tensor.matmul(ps[:, 6 + j % 2, t * u["w"]:(t + 1) * u["w"]],
                                                        wq[:, j % 2, s, t * P:(t + 1) * P], u["v"](s),
                                                        start=(s == keys[0]), stop=(s == keys[-1]))
                        last.then_inc(out_ready, 1)

            @block.vector
            def _(dve):
                link = Link(dve, step)
                groups = 0
                for i in range(N + 1):
                    if i < N:
                        u = units[i]
                        groups += new_group[i]
                        dve.wait_ge(row_ready, i + 1)
                        for s in range(T):
                            a, b = span(u, s)
                            if i >= 2 and s == 0:
                                dve.wait_ge(weighted, T * (i - 1))
                            nc.vector.tensor_scalar(gap[:, i % 2, s, a:b], ps[:, 4 + i % 2, a:b],
                                                    cols[:, s, u["col"]:u["col"] + 1], 0.0, ALU.subtract, ALU.max
                                                    ).then_inc(gap_ready, 1)
                        dve.wait_ge(products_ready, groups)
                        if i >= 2:
                            dve.wait_ge(out_ready, i - 1)
                        for s in range(T):
                            a, b = span(u, s)
                            dve.wait_ge(exp_done, T * i + s + 1)
                            nc.vector.scalar_tensor_tensor(out=wq[:, i % 2, s, a:b], in0=ps[:, s, a:b],
                                                           scalar=u["weight"](s), in1=gap[:, i % 2, s, a:b],
                                                           op0=ALU.mult, op1=ALU.mult).then_inc(weighted, 1)
                    if i >= 1:
                        j = i - 1
                        dve.wait_ge(out_ready, j + 1)
                        out = ps[:, 6 + j % 2, 0:T * units[j]["w"]].rearrange("p (t c) -> p t c", t=T)
                        units[j]["store"](nc, link, out, tmp).then_inc(out_stored, 1)
                        dve.wait_ge(out_stored, j + 1)

            @block.scalar
            def _(act):
                for i in range(N):
                    for s in range(T):
                        a, b = span(units[i], s)
                        act.wait_ge(gap_ready, T * i + s + 1)
                        nc.scalar.activation(gap[:, i % 2, s, a:b], gap[:, i % 2, s, a:b], ACT.Exp, scale=-1.0
                                             ).then_inc(exp_done, 1)

            @block.gpsimd
            def _(pool):
                for i in range(N):
                    for s in range(T):
                        pool.wait_ge(weighted, T * i + s + 1)
                        d = wq[:, i % 2, s, s * P:(s + 1) * P]
                        nc.gpsimd.tensor_tensor(d, d, env.keep_le if units[i]["back"] else env.keep_ge, ALU.mult
                                                ).then_inc(masked, 1)


def decay_units(proj, mqk_t, conv_out, cols, dt, vx, xs, h_sum, y_ssd):
    units = []
    for h in range(ML_H):
        base, chunk = (h % 2) * ML_D, h // 2
        for d in range(2):
            k = d * ML_H + h

            def store(nc, link, out, tmp, h=h, d=d, k=k):
                v = nc.vector
                den = out[:, :, ML_D]
                link(v.tensor_scalar(tmp[:, :, 0], den, -1.0, None, ALU.mult))
                link(v.tensor_tensor(tmp[:, :, 0], tmp[:, :, 0], den, ALU.max))
                link(v.tensor_tensor(tmp[:, :, 0], tmp[:, :, 0], cols[:, :, 16 + k], ALU.max))
                link(v.reciprocal(tmp[:, :, 0], tmp[:, :, 0]))
                for t in range(T):
                    dst = h_sum[:, t, h * ML_D:(h + 1) * ML_D]
                    if d == 0:
                        last = v.tensor_scalar(dst, out[:, t, 0:ML_D], tmp[:, t, 0:1], None, ALU.mult)
                    else:
                        last = v.scalar_tensor_tensor(out=dst, in0=out[:, t, 0:ML_D], scalar=tmp[:, t, 0:1],
                                                      in1=dst, op0=ALU.mult, op1=ALU.add)
                return last

            units.append(dict(group=("m", h), k=mqk_t[base:base + ML_D, 2 + chunk, :], q=mqk_t[base:base + ML_D, chunk, :],
                              weight=lambda s: ML_D ** -0.5, row=8 + k, col=k, back=d == 1,
                              v=lambda s, h=h: vx[:, s, h, :], w=ML_D + 1, store=store))
    for h in range(SSD_H):
        g = h // (SSD_H // SSD_G)
        for d in range(2):
            k = d * SSD_H + h

            def store(nc, link, out, tmp, h=h, d=d):
                dst = y_ssd[:, :, h * SSD_P:(h + 1) * SSD_P]
                if d == 0:
                    return nc.vector.tensor_copy(dst, out)
                return nc.vector.tensor_tensor(dst, out, dst, ALU.add)

            units.append(dict(group=("s", g), k=conv_out[:, 2 + g, :], q=conv_out[:, 4 + g, :],
                              weight=lambda s, k=k: dt[:, s, k:k + 1], row=24 + k, col=24 + k, back=d == 1,
                              v=lambda s, h=h: xs[:, s, h * SSD_P:(h + 1) * SSD_P], w=SSD_P, store=store))
    return units


def exp_m_stage(env, cols):
    with env.nc.Block() as block:
        @block.scalar
        def _(act):
            env.nc.scalar.activation(cols[:, :, 16:24], cols[:, :, 16:24], ACT.Exp, scale=-1.0)


def mixer_end_stage(env, proj, vec, h_sum, y_ssd, xs):
    nc = env.nc
    names = ("vector_step", "variances", "roots", "sigmoid_done", "silu_done")
    step, variances, roots, sig, silu = (env.sem("mixer_end", n) for n in names)
    ME, GE = ML_H, SSD_G
    W = ML_H * ML_D
    with ExitStack() as local:
        sq = local.enter_context(nc.sbuf_tensor("end_sq", [P, T, W], F32))
        mean = local.enter_context(nc.sbuf_tensor("end_mean", [P, T * ME], F32))
        var = local.enter_context(nc.sbuf_tensor("end_var", [P, T * ME], F32))
        ss = local.enter_context(nc.sbuf_tensor("end_ss", [P, T * GE], F32))
        o = local.enter_context(nc.sbuf_tensor("end_o", [P, T, W], F32))
        z = local.enter_context(nc.sbuf_tensor("end_z", [P, T, W], F32))

        def flat(x, w):
            return x[:, :, :].rearrange("p t (h c) -> p t h c", c=w)

        def stat(a, w):
            a = a[:, :].rearrange("p (t h) -> p t h", t=T)
            return a if w is None else a.unsqueeze(3).to_broadcast([P, T, a.shape[2], w])

        def row(c):
            return vec[:, c:c + W].unsqueeze(1).to_broadcast([P, T, W])

        with nc.Block() as block:
            @block.scalar
            def _(act):
                nc.scalar.activation(o[:, :, :], proj[:, :, MO:MO + W], ACT.Sigmoid).then_inc(sig, 1)
                nc.scalar.activation(z[:, :, :], proj[:, :, SZ:SZ + W], ACT.Silu).then_inc(silu, 1)
                act.wait_ge(variances, 1)
                nc.scalar.activation(var[:, :], var[:, :], ACT.Sqrt, scale=1.0 / ML_D, bias=env.eps5).then_inc(roots, 1)
                act.wait_ge(variances, 2)
                nc.scalar.activation(ss[:, :], ss[:, :], ACT.Sqrt, scale=SSD_G / W, bias=env.eps6).then_inc(roots, 1)

            @block.vector
            def _(dve):
                link = Link(dve, step)
                v = nc.vector
                hf, sf = flat(h_sum, ML_D), flat(sq, ML_D)
                link(v.reduce_sum(stat(mean, None), hf, AX))
                link(v.tensor_scalar(mean[:, :], mean[:, :], 1.0 / ML_D, None, ALU.mult))
                link(v.tensor_tensor(hf, hf, stat(mean, ML_D), ALU.subtract))
                link(v.tensor_tensor(sf, hf, hf, ALU.mult))
                v.reduce_sum(stat(var, None), sf, AX).then_inc(variances, 1)
                for h in range(SSD_H):
                    c = slice(h * SSD_P, (h + 1) * SSD_P)
                    last = v.scalar_tensor_tensor(out=y_ssd[:, :, c], in0=xs[:, :, c], scalar=vec[:, V_SD + h:V_SD + h + 1],
                                                  in1=y_ssd[:, :, c], op0=ALU.mult, op1=ALU.add)
                link(last)
                dve.wait_ge(silu, 1)
                link(v.tensor_tensor(y_ssd[:, :, :], y_ssd[:, :, :], z[:, :, :], ALU.mult))
                dve.wait_ge(variances, 1)
                link(v.tensor_tensor(sq[:, :, :], y_ssd[:, :, :], y_ssd[:, :, :], ALU.mult))
                v.reduce_sum(stat(ss, None), flat(sq, W // GE), AX).then_inc(variances, 1)
                dve.wait_ge(roots, 2)
                link(v.reciprocal(var[:, :], var[:, :]))
                link(v.reciprocal(ss[:, :], ss[:, :]))
                link(v.tensor_tensor(hf, hf, stat(var, ML_D), ALU.mult))
                link(v.tensor_tensor(h_sum[:, :, :], h_sum[:, :, :], row(V_MN), ALU.mult))
                dve.wait_ge(sig, 1)
                v.tensor_tensor(h_sum[:, :, :], h_sum[:, :, :], o[:, :, :], ALU.mult)
                yf = flat(y_ssd, W // GE)
                link(v.tensor_tensor(yf, yf, stat(ss, W // GE), ALU.mult))
                v.tensor_tensor(y_ssd[:, :, :], y_ssd[:, :, :], row(V_SN), ALU.mult)


def router_stage(env, xt, router_w, vec, combine, oh, rank, passes):
    nc, ps = env.nc, env.ps
    names = ("weights_loaded", "logits_ready", "shifted", "exp_done", "groups_chosen", "ranked", "vector_step")
    loaded, logits_ready, shifted, exp_done, chosen, ranked, step = (env.sem("router", n) for n in names)
    with ExitStack() as local:
        def tile(name, *shape):
            return local.enter_context(nc.sbuf_tensor(f"router_{name}", [P, *shape], F32))
        wr = tile("w", KD, NR)
        lg, e, acc = tile("logits", T, NR), tile("e", T, GROUPS), tile("acc", T, PER_GROUP)
        top, eq, rem = tile("top", T, 1), tile("eq", T, 4), tile("rem", T, 1)
        most, more = tile("most", 1), tile("more", 1)
        first, second, gp, tmp = tile("first", T, 4), tile("second", T, 4), tile("gp", T, 1), tile("tmp", T, 4)
        with nc.Block() as block:
            @block.sync
            def _(sp):
                sp.dma_start(wr[:, :, :], router_w.rearrange("(k p) c -> p k c", p=P),
                             allow_slow_non_contiguous=True).then_inc(loaded, 16)

            @block.tensor
            def _(pe):
                pe.wait_ge(loaded, 16)
                for t in range(T):
                    for k in range(KD):
                        last = nc.tensor.matmul(ps[:, 0, t * NR:(t + 1) * NR], xt[:, k, t * P:(t + 1) * P],
                                                wr[:, k, :], start=(k == 0), stop=(k == KD - 1))
                last.then_inc(logits_ready, 1)
                pe.wait_ge(chosen, 1)
                for t in range(T):
                    for b in range(t + 1):
                        nc.tensor.matmul(ps[:, 1, t * 4:(t + 1) * 4], env.keep_ge if b == t else env.ones,
                                         oh[:, b, :], start=(b == 0), stop=(b == t))
                for b in range(T):
                    last = nc.tensor.matmul(ps[:, 1, T * 4:T * 4 + 4], env.ones, oh[:, b, :],
                                            start=(b == 0), stop=(b == T - 1))
                last.then_inc(ranked, 1)

            @block.vector
            def _(dve):
                link = Link(dve, step)
                v = nc.vector

                def wide(x):
                    return x[:, :, :].to_broadcast([P, T, 4])

                def first_of_max(x, out):
                    link(v.reduce_max(top[:, :, 0], x, AX))
                    link(v.tensor_tensor(eq[:, :, :], x, wide(top), ALU.is_equal))
                    link(v.tensor_scalar(rem[:, :, :], top[:, :, :], 0.0, 1.0, ALU.mult, ALU.add))
                    for j in range(4):
                        link(v.tensor_tensor(out[:, :, j:j + 1], eq[:, :, j:j + 1], rem[:, :, :], ALU.mult))
                        if j < 3:
                            link(v.tensor_tensor(rem[:, :, :], rem[:, :, :], out[:, :, j:j + 1], ALU.subtract))

                dve.wait_ge(logits_ready, 1)
                src = ps[:, 0, 0:T * NR].rearrange("p (t c) -> p t c", t=T)
                bias = vec[:, V_RB:V_RB + NR].unsqueeze(1).to_broadcast([P, T, NR])
                link(v.tensor_tensor(lg[:, :, :], src, bias, ALU.add))
                first_of_max(lg[:, :, 0:GROUPS], oh)
                v.tensor_copy(eq[:, :, :], oh[:, :, :]).then_inc(chosen, 1)
                v.tensor_tensor(e[:, :, :], lg[:, :, 0:GROUPS], wide(top), ALU.subtract).then_inc(shifted, 1)
                dve.wait_ge(exp_done, 1)
                link(v.reduce_sum(gp[:, :, 0], e[:, :, :], AX))
                link(v.reciprocal(gp[:, :, :], gp[:, :, :]))
                for g in range(GROUPS):
                    c = GROUPS + g * PER_GROUP
                    dst = acc if g == 0 else tmp
                    link(v.tensor_tensor(dst[:, :, :], lg[:, :, c:c + PER_GROUP], oh[:, :, g:g + 1].to_broadcast([P, T, 4]),
                                         ALU.mult))
                    if g:
                        link(v.tensor_tensor(acc[:, :, :], acc[:, :, :], tmp[:, :, :], ALU.add))
                first_of_max(acc[:, :, :], first)
                v.tensor_tensor(e[:, :, :], acc[:, :, :], wide(top), ALU.subtract).then_inc(shifted, 1)
                link(v.scalar_tensor_tensor(out=tmp[:, :, :], in0=first[:, :, :], scalar=-3e38, in1=acc[:, :, :],
                                            op0=ALU.mult, op1=ALU.add))
                dve.wait_ge(shifted, 2)
                first_of_max(tmp[:, :, :], second)
                dve.wait_ge(exp_done, 2)
                link(v.tensor_tensor(first[:, :, :], first[:, :, :], second[:, :, :], ALU.add))
                link(v.tensor_tensor(e[:, :, :], e[:, :, :], first[:, :, :], ALU.mult))
                link(v.reduce_sum(rem[:, :, 0], e[:, :, :], AX))
                link(v.reciprocal(rem[:, :, :], rem[:, :, :]))
                link(v.tensor_tensor(rem[:, :, :], rem[:, :, :], gp[:, :, :], ALU.mult))
                link(v.tensor_tensor(e[:, :, :], e[:, :, :], wide(rem), ALU.mult))
                for g in range(GROUPS):
                    last = v.tensor_tensor(lg[:, :, g * PER_GROUP:(g + 1) * PER_GROUP], e[:, :, :],
                                           oh[:, :, g:g + 1].to_broadcast([P, T, 4]), ALU.mult)
                link(last)
                link(v.tensor_copy(combine[0][:, :, :], lg[:, :, 0:EXPERTS]))
                v.tensor_tensor(combine[1][:, :, :], lg[:, :, 0:EXPERTS], combine[0][:, :, :].bitcast(F32), ALU.subtract)
                dve.wait_ge(ranked, 1)
                v.tensor_copy(rank[:, :, :], ps[:, 1, 0:T * 4].rearrange("p (t g) -> p t g", t=T))
                link(v.reduce_max(most[:, :], ps[:, 1, T * 4:T * 4 + 4], AX))
                link(v.tensor_scalar(more[:, :], most[:, :], float(2 * SLOTS), None, ALU.is_gt))
                link(v.tensor_scalar(most[:, :], most[:, :], float(SLOTS), 1.0, ALU.is_gt, ALU.add))
                v.tensor_tensor(passes[:, :], most[:, :], more[:, :], ALU.add)

            @block.scalar
            def _(act):
                for n in range(2):
                    act.wait_ge(shifted, n + 1)
                    nc.scalar.activation(e[:, :, :], e[:, :, :], ACT.Exp).then_inc(exp_done, 1)


def split_x_stage(env, x, xp):
    nc = env.nc
    hi, lo = env.sem("split_x", "hi"), env.sem("split_x", "lo")
    with nc.Block() as block:
        @block.scalar
        def _(act):
            for t in range(T):
                nc.scalar.activation(xp[0][:, t, :], x[:, t, :], ACT.Copy).then_inc(hi, 1)
            for t in range(T):
                act.wait_ge(lo, t + 1)
                nc.scalar.activation(x[:, t, :], x[:, t, :], ACT.Copy, scale=ALPHA)

        @block.vector
        def _(dve):
            for t in range(T):
                dve.wait_ge(hi, t + 1)
                nc.vector.tensor_tensor(xp[1][:, t, :], x[:, t, :], xp[0][:, t, :].bitcast(F32), ALU.subtract
                                        ).then_inc(lo, 1)


def places_stage(env, oh, rank, take, put):
    nc, ps, ident = env.nc, env.ps, env.ident
    placed, turned = env.sem("places", "placed"), env.sem("places", "turned")
    step = env.sem("places", "vector_step")
    jobs = [(g, st) for g in range(GROUPS) for st in range(2)]
    with nc.Block() as block:
        @block.sync
        def _(sp):
            env.stream.load(sp, env.stream.RAW)

        @block.vector
        def _(dve):
            for g in range(GROUPS):
                for t in range(T):
                    last = nc.vector.tensor_scalar(take[:, g, t, :], env.slot_numbers, rank[:, t, g:g + 1],
                                                   oh[:, t, g:g + 1], ALU.is_equal, ALU.mult)
                last.then_inc(placed, 1)
            dve.wait_ge(placed, GROUPS)
            nc.vector.tensor_scalar(rank[:, :, :], rank[:, :, :], -float(SLOTS), None, ALU.add)

        @block.tensor
        def _(pe):
            for i, (g, st) in enumerate(jobs):
                pe.wait_ge(placed, g + 1)
                w = min(P, SLOTS - st * P)
                for t in range(T):
                    src = take[:, g, t, st * P:st * P + w].bitcast(F32)
                    last = nc.tensor.transpose(ps[0:w, i, t * P:(t + 1) * P], src, ident)
                last.then_inc(turned, 1)

        @block.scalar
        def _(act):
            for i, (g, st) in enumerate(jobs):
                w = min(P, SLOTS - st * P)
                act.wait_ge(turned, i + 1)
                nc.scalar.activation(put[0:w, g, st, :], ps[0:w, i, :], ACT.Copy)


def expert_units(at):
    units, kinds = [], []
    for g in range(GROUPS):
        for kind, e in (("gate", 0), ("up", 0), ("gate", 1), ("up", 1), ("down", 0), ("gate", 2), ("up", 2),
                        ("down", 1), ("gate", 3), ("up", 3), ("down", 2), ("down", 3)):
            w = at(f"expert_w_{kind}")[g * PER_GROUP + e]
            units.append(w.rearrange("(k p) f -> p k f", p=P))
            kinds.append((kind, g, e))
    return units, kinds


def expert_stage(env, x, xp, take, put, combine, kinds):
    nc, ps, stream = env.nc, env.ps, env.stream
    names = ("gathered", "xg_hi", "xg_lo", "row_ready", "silu_done", "times_up", "times_combine", "hidden_hi",
             "hidden_lo", "out_hi", "out_lo", "scattered", "added", "pad_zero")
    (gathered, xg_hi_done, xg_lo_done, row_ready, silu_done, times_up, times_combine, hidden_hi, hidden_lo,
     out_hi, out_lo, scattered, added, pad_zero) = (env.sem("experts", n) for n in names)
    FC = F_CH // P
    E, N = PER_GROUP, len(kinds)
    per = N // GROUPS
    outs = [(st, half) for st in range(2) for half in range(2)]
    sums = [(tt, half) for tt in range(T) for half in range(2)]
    with ExitStack() as local:
        def pair(name, *shape):
            return tuple(local.enter_context(nc.sbuf_tensor(f"expert_{name}_{n}", [P, *shape], F32R)) for n in ("hi", "lo"))
        xg, hidden, og = pair("xg", KD, SLOTS), pair("hidden", E * FC, 2 * P), pair("out", 2, D)
        gate = local.enter_context(nc.sbuf_tensor("expert_gate", [P, FC, SLOTS], F32))

        def two(b):
            return ps[:, b, 0:2 * SLOTS].rearrange("p (k s) -> p k s", k=2)

        with nc.Block() as block:
            @block.sync
            def _(sp):
                stream.load(sp, N)

            @block.gpsimd
            def _(pool):
                for h in hidden:
                    nc.gpsimd.memset(h[:, :, SLOTS:2 * P].bitcast(F32), 0.0).then_inc(pad_zero, 1)

            @block.tensor
            def _(pe):
                def gather(g):
                    if g:
                        pe.wait_ge(silu_done, FC * E * g)
                        pe.wait_ge(times_combine, FC * E * g)
                    if g > 1:
                        pe.wait_ge(added, len(sums) * (g - 1))
                    for b in range(4):
                        for k in range(2 * b, 2 * b + 2):
                            for t in range(T):
                                a = tuple(h[:, t, k * P:(k + 1) * P] for h in xp)
                                last = exact_product(nc, two(b)[:, k % 2, :], a, take[:, g, t, :], t == 0, t == T - 1)
                        last.then_inc(gathered, 1)

                def scatter(g):
                    pe.wait_ge(out_lo, 4 * (g + 1))
                    for i, (tt, half) in enumerate(sums):
                        b = i % 4
                        if i >= 4:
                            pe.wait_ge(added, len(sums) * g + i - 3)
                        elif g < GROUPS - 1:
                            pe.wait_ge(xg_lo_done, 4 * (g + 1) + b + 1)
                        elif i == 0:
                            pe.wait_ge(added, len(sums) * g)
                        for st in range(2):
                            w = min(P, SLOTS - st * P)
                            a = put[0:w, g, st, tt * P:(tt + 1) * P]
                            o = tuple(h[0:w, st, half * BANK:(half + 1) * BANK] for h in og)
                            last = exact_product(nc, ps[:, b, :], a, o, st == 0, st == 1)
                        last.then_inc(scattered, 1)

                gather(0)
                pe.wait_ge(pad_zero, 2)
                for n, (kind, g, e) in enumerate(kinds):
                    ex = g * E + e
                    if kind == "gate":
                        if e == 0:
                            pe.wait_ge(xg_lo_done, 4 * (g + 1))
                            if g:
                                pe.wait_ge(added, len(sums) * g)
                        if ex:
                            pe.wait_ge(silu_done, FC * ex)
                    if kind == "up":
                        if ex:
                            pe.wait_ge(times_combine, FC * ex)
                        for t in range(T):
                            c = tuple(h[:, t, ex:ex + 1].to_broadcast([P, P]) for h in combine)
                            last = exact_product(nc, ps[:, 2, 0:SLOTS], c, take[:, g, t, :], t == 0, t == T - 1)
                        last.then_inc(row_ready, 1)
                    w_hi, w_lo = stream.ready(pe, n)
                    if kind == "down":
                        pe.wait_ge(hidden_lo, FC * (ex + 1))
                        if e == 0 and g:
                            pe.wait_ge(out_lo, 4 * g)
                        for i, (st, half) in enumerate(outs):
                            cols = slice(half * BANK, (half + 1) * BANK)
                            for f in range(FC):
                                a = tuple(h[:, e * FC + f, st * P:(st + 1) * P] for h in hidden)
                                last = product(nc, ps[:, 4 + i, :], a, (w_hi[:, f, cols], w_lo[:, f, cols]),
                                               e == 0 and f == 0, e == E - 1 and f == FC - 1)
                    else:
                        if kind == "up" and ex:
                            pe.wait_ge(times_up, FC * ex)
                        for f in range(FC):
                            cols = slice(f * P, (f + 1) * P)
                            for k in range(KD):
                                last = product(nc, two(kind == "up")[:, f, :], (w_hi[:, k, cols], w_lo[:, k, cols]),
                                               (xg[0][:, k, :], xg[1][:, k, :]), k == 0, k == KD - 1)
                    last.then_inc(stream.used, 1)
                    if (kind, e) == ("down", E - 1):
                        if g < GROUPS - 1:
                            gather(g + 1)
                        scatter(g)

            @block.scalar
            def _(act):
                def gathered_hi(g):
                    for b in range(4):
                        act.wait_ge(gathered, 4 * g + b + 1)
                        nc.scalar.activation(xg[0][:, 2 * b:2 * b + 2, :], two(b), ACT.Copy).then_inc(xg_hi_done, 1)

                for n in range(N + 1):
                    if n < N:
                        stream.split_hi(act, n)
                    if n == 1:
                        gathered_hi(0)
                    if n >= 2 and kinds[n - 2][0] != "down":
                        kind, g, e = kinds[n - 2]
                        ex = g * E + e
                        if kind == "gate":
                            act.wait_ge(stream.used, n - 1)
                            if ex:
                                act.wait_ge(hidden_lo, FC * ex)
                            for f in range(FC):
                                last = nc.scalar.activation(gate[:, f, :], two(0)[:, f, :], ACT.Silu).then_inc(silu_done, 1)
                        else:
                            for f in range(FC):
                                act.wait_ge(times_combine, FC * ex + f + 1)
                                nc.scalar.activation(hidden[0][:, e * FC + f, 0:SLOTS], gate[:, f, :], ACT.Copy
                                                     ).then_inc(hidden_hi, 1)
                    if n and n % per == 0:
                        g = n // per - 1
                        act.wait_ge(stream.used, n)
                        if g:
                            act.wait_ge(scattered, len(sums) * g)
                        for i, (st, half) in enumerate(outs):
                            nc.scalar.activation(og[0][:, st, half * BANK:(half + 1) * BANK], ps[:, 4 + i, :], ACT.Copy
                                                 ).then_inc(out_hi, 1)
                        if g < GROUPS - 1:
                            gathered_hi(g + 1)

            @block.vector
            def _(dve):
                v = nc.vector

                def gathered_lo(g):
                    for b in range(4):
                        dve.wait_ge(xg_hi_done, 4 * g + b + 1)
                        ks = slice(2 * b, 2 * b + 2)
                        v.tensor_tensor(xg[1][:, ks, :], two(b), xg[0][:, ks, :].bitcast(F32), ALU.subtract
                                        ).then_inc(xg_lo_done, 1)

                for n in range(N + 1):
                    after_up = n >= 2 and kinds[n - 2][0] == "up"
                    if after_up:
                        kind, g, e = kinds[n - 2]
                        ex = g * E + e
                        dve.wait_ge(stream.used, n - 1)
                        for f in range(FC):
                            dve.wait_ge(silu_done, FC * ex + f + 1)
                            v.tensor_tensor(gate[:, f, :], gate[:, f, :], two(1)[:, f, :], ALU.mult).then_inc(times_up, 1)
                        dve.wait_ge(row_ready, ex + 1)
                        for f in range(FC):
                            dve.wait_ge(times_up, FC * ex + f + 1)
                            v.tensor_tensor(gate[:, f, :], gate[:, f, :], ps[:, 2, 0:SLOTS], ALU.mult
                                            ).then_inc(times_combine, 1)
                    if n < N:
                        stream.split_lo(dve, n)
                    if n == 1:
                        gathered_lo(0)
                    if after_up:
                        for f in range(FC):
                            dve.wait_ge(hidden_hi, FC * ex + f + 1)
                            v.tensor_tensor(hidden[1][:, e * FC + f, 0:SLOTS], gate[:, f, :],
                                            hidden[0][:, e * FC + f, 0:SLOTS].bitcast(F32), ALU.subtract
                                            ).then_inc(hidden_lo, 1)
                    if n and n % per == 0:
                        g = n // per - 1
                        for i, (st, half) in enumerate(outs):
                            cols = slice(half * BANK, (half + 1) * BANK)
                            dve.wait_ge(out_hi, 4 * g + i + 1)
                            v.tensor_tensor(og[1][:, st, cols], ps[:, 4 + i, :], og[0][:, st, cols].bitcast(F32),
                                            ALU.subtract).then_inc(out_lo, 1)
                        if g < GROUPS - 1:
                            gathered_lo(g + 1)
                        for i, (tt, half) in enumerate(sums):
                            d = x[:, tt, half * BANK:(half + 1) * BANK]
                            dve.wait_ge(scattered, len(sums) * g + i + 1)
                            v.tensor_tensor(d, d, ps[:, i % 4, :], ALU.add).then_inc(added, 1)


def pair_tile(nc, ctx, name, *shape):
    return tuple(ctx.enter_context(nc.sbuf_tensor(f"{name}_{n}", [P, *shape], F32R)) for n in ("hi", "lo"))


def chunks_of(pair, n=KD):
    return [(pair[0][:, k, :], pair[1][:, k, :]) for k in range(n)]


def first_mixers(env, l, dram, x, vec, convw, cos, sin):
    nc = env.nc
    at = layer_of(dram, l)
    KP = [range(0, 4), range(4, 8)]
    NIN = -(-IN1 // BANK)
    units = weight_units(at("w_in")) + weight_units(at("mla_w_uq"), width=4 * QK) + weight_units(at("mla_w_ukv"))
    first_uq, first_out = 2 * NIN, 2 * NIN + 4
    env.stream = WeightStream(env, units + weight_units(at("w_out")))

    with ExitStack() as mix:
        def tile(ctx, name, *shape):
            return ctx.enter_context(nc.sbuf_tensor(name, [P, *shape], F32))
        y = tile(mix, "y1", T, D)
        proj = tile(mix, "proj1", T, IN1)
        load_small_stage(env, "small1", [(vec[:, :], at("vec1").to_broadcast([P, NV1])),
                                         (convw[:, :, :], at("conv1"))], env.stream.RAW)
        with ExitStack() as local:
            xt = pair_tile(nc, local, "xt", KD, S)
            transpose_stage(env, "x_t", pair_transposes(lambda t, k: x[:, t, k * P:(k + 1) * P], xt))
            jobs = []
            for c in range(0, IN1, BANK):
                w = min(BANK, IN1 - c)
                jobs.append((chunks_of(xt), KP, w, [(lambda b, w=w: b[:, 0:w], lambda t, c=c, w=w: proj[:, t, c:c + w])]))
            project_stage(env, "proj1", 0, jobs, prefetch=3)

        with ExitStack() as mla:
            v = tile(mla, "v_mla", T, MLA_H, MLA_V)
            qn, kn = tile(mla, "qn", T, MLA_H, QK), tile(mla, "kn", T, MLA_H, QK)
            with ExitStack() as pre:
                NC = (Q_RANK + KV_RANK) // P
                cqn = tile(pre, "cqn", T, NC * P)
                cqt = pair_tile(nc, pre, "cqt", NC, S)
                latent_norm_stage(env, proj, vec, cqn)
                transpose_stage(env, "latent_t", [([cqn[:, t, k * P:(k + 1) * P] for t in range(T)],
                                                   (cqt[0][:, k, :], cqt[1][:, k, :]), None) for k in range(NC)])
                jobs = []
                for n in range(2):
                    hs = slice(n * 4, n * 4 + 4)
                    jobs.append((chunks_of(cqt, NC), [range(0, 2)], 4 * QK,
                                 [(lambda b: by_head(b[:, 0:4 * QK], 4), lambda t, hs=hs: qn[:, t, hs, :])]))
                for n in range(2):
                    hs = slice(n * 4, n * 4 + 4)
                    jobs.append((chunks_of(cqt, NC)[2:], [range(0, 1)], BANK,
                                 [(lambda b: by_head(b, 4)[:, :, 0:NOPE], lambda t, hs=hs: kn[:, t, hs, 0:NOPE]),
                                  (lambda b: by_head(b, 4)[:, :, NOPE:], lambda t, hs=hs: v[:, t, hs, :])]))
                project_stage(env, "mla_proj", first_uq, jobs)
                mla_rope_stage(env, proj, qn, kn, cos, sin)
            q_t, k_t = tile(mla, "q_t", MLA_H, S), tile(mla, "k_t", MLA_H, S)
            transpose_stage(env, "mla_t", [([src[:, t, h, :] for t in range(T)], dst[0:QK, h, :], None)
                                           for h in range(MLA_H) for src, dst in ((qn, q_t), (kn, k_t))])
            attn = [dict(q=q_t[0:QK, h, t * P:(t + 1) * P], k=k_t[0:QK, h, :], nk=S, mask=None,
                         v=[v[:, b, h, :] for b in range(T)], dst=y[:, t, h * MLA_V:(h + 1) * MLA_V])
                    for h in range(MLA_H) for t in range(T)]

            def slots(tile_, n):
                flat = tile_[:, :, :, :].rearrange("p t h c -> p (t h c)")
                return flat[:, 0:n * S].rearrange("p (n s) -> p n s", n=n)
            attention_stage(env, "mla", attn, QK ** -0.5, slots(qn, 4), slots(kn, 2), prefetch=first_out + 3)

        with ExitStack() as rec:
            conv_out = tile(rec, "conv_out", CC, S)
            xs = tile(rec, "xs", T, SSD_H * SSD_P)
            with ExitStack() as pre:
                xc = tile(pre, "xc", CC, S + 2 * PAD)
                pad_stage(env, xc)
                transpose_stage(env, "conv_t", [([proj[:, t, XBC + c * P:XBC + (c + 1) * P] for t in range(T)],
                                                 xc[:, c, PAD:PAD + S], None) for c in range(CC)])
                conv_stage(env, xc, convw, conv_out)
            mqk_t = tile(rec, "mqk_t", 4, S)
            jobs = [([proj[:, t, MQ + c * P:MQ + (c + 1) * P] for t in range(T)], mqk_t[:, c, :], None)
                    for c in range(4)]
            for t in range(T):
                jobs.append(([conv_out[:, c, t * P:(t + 1) * P] for c in range(2)], xs[:, t, :], None))
            transpose_stage(env, "rec_t", jobs)
            gates, dt = tile(rec, "gates", T, 24), tile(rec, "dt", T, 8)
            vx, cols = tile(rec, "vx", T, ML_H, ML_D + 1), tile(rec, "cols", T, 32)
            h_sum, y_ssd = y[:, :, 512:768], y[:, :, 768:1024]
            gates_stage(env, proj, vec, gates, dt[:, :, :], vx)
            scan_stage(env, gates, cols)
            exp_m_stage(env, cols)
            decay_stage(env, decay_units(proj, mqk_t, conv_out, cols, dt, vx, xs, h_sum, y_ssd), cols)
            mixer_end_stage(env, proj, vec, h_sum, y_ssd, xs)

        with ExitStack() as local:
            yt = pair_tile(nc, local, "yt", KD, S)
            transpose_stage(env, "y_t", pair_transposes(lambda t, k: y[:, t, k * P:(k + 1) * P], yt))
            jobs = [(chunks_of(yt), KP, BANK, [(lambda b: b, lambda t, n=n: x[:, t, n * BANK:(n + 1) * BANK])])
                    for n in range(2)]
            project_stage(env, "out1", first_out, jobs, alpha_x=ALPHA)


def first_experts(env, l, dram, x, vec):
    nc = env.nc
    at = layer_of(dram, l)
    layernorm_stage(env, "ln1", at("ln1"), x)
    with ExitStack() as local:
        def tile(name, *shape):
            return local.enter_context(nc.sbuf_tensor(name, [P, *shape], F32))
        oh, rank = tile("group_choice", T, GROUPS), tile("group_rank", T, GROUPS)
        combine = pair_tile(nc, local, "combine", T, EXPERTS)
        passes = local.enter_context(nc.sbuf_tensor("passes", [P, 1], I32))
        with nc.sbuf_tensor("router_xt", [P, KD, S], F32) as xt:
            transpose_stage(env, "x1_t", x_transposes(env, x, xt))
            router_stage(env, xt, at("router"), vec, combine, oh, rank, passes)
        xp = pair_tile(nc, local, "x_pair", T, D)
        split_x_stage(env, x, xp)
        env.end_layer()
        take = local.enter_context(nc.sbuf_tensor("take", [P, GROUPS, T, SLOTS], F32R))
        put = local.enter_context(nc.sbuf_tensor("put", [P, GROUPS, 2, S], F32R))
        units, kinds = expert_units(at)
        env.stream = WeightStream(env, units)
        n = nc.values_load(passes[0:1, 0:1], min_val=1, max_val=-(-S // SLOTS))
        with nc.Fori(0, n):
            places_stage(env, oh, rank, take, put)
            expert_stage(env, x, xp, take, put, combine, kinds)
            env.end_layer()
    layernorm_stage(env, "ln2", at("ln2"), x)


def layer_of(dram, l):
    def at(name):
        ap = dram[name]
        ap = ap[tuple([bass.ds(l, 1)] + [slice(None)] * (len(ap.shape) - 1))]
        if len(ap.shape) == 2:
            return ap
        dims = [f"d{i}" for i in range(1, len(ap.shape))]
        return ap.rearrange(f"a {' '.join(dims)} -> (a {dims[0]}) {' '.join(dims[1:])}")
    return at


def load_small_stage(env, stage, pairs, prefetch):
    nc = env.nc
    loaded = env.sem(stage, "loaded")
    with nc.Block() as block:
        @block.sync
        def _(sp):
            for dst, src in pairs:
                sp.dma_start(dst, src).then_inc(loaded, 16)
            env.stream.load(sp, prefetch)
            sp.wait_ge(loaded, 16 * len(pairs))


def pad_stage(env, xc):
    nc = env.nc
    with nc.Block() as block:
        @block.gpsimd
        def _(pool):
            nc.gpsimd.memset(xc[:, :, 0:PAD], 0.0)
            nc.gpsimd.memset(xc[:, :, PAD + S:], 0.0)



def rms_stage(env, stage, x, out):
    nc = env.nc
    squares, roots, step = (env.sem(stage, n) for n in ("squares_summed", "roots", "vector_step"))
    with nc.sbuf_tensor(f"{stage}_ss", [P, T], F32) as ss:
        with nc.Block() as block:
            @block.scalar
            def _(act):
                for t in range(T):
                    nc.scalar.activation(out[:, t, :], x[:, t, :], ACT.Square, accum_out=ss[:, t:t + 1]
                                         ).then_inc(squares, 1)
                act.wait_ge(squares, T)
                nc.scalar.activation(ss[:, :], ss[:, :], ACT.Sqrt, scale=1.0 / D, bias=env.eps6).then_inc(roots, 1)

            @block.vector
            def _(dve):
                link = Link(dve, step)
                dve.wait_ge(roots, 1)
                link(nc.vector.reciprocal(ss[:, :], ss[:, :]))
                for t in range(T):
                    nc.vector.tensor_scalar(out[:, t, :], x[:, t, :], ss[:, t:t + 1], None, ALU.mult)


def index_score(proj, t):
    return proj[:, t, B_IQ:B_IQ + (t + 1) * P]


def second_projection_units(w_in):
    units, jobs = [], []
    for c, w, heads in ((B_IK, B_IW + IDX_H - B_IK, None), (B_IQ, BANK, None), (B_MQ, BANK, (0, (0, 1))),
                        (B_DQ, BANK, (1, (0, 0))), (B_DK, BANK, (1, (1, 1))), (B_SQ, BANK, (2, (0, 1))),
                        (B_MV, 256, None), (B_SV, 256, None), (B_DV, BANK, None)):
        rows = P * min(KD, WeightStream.UNIT // w)
        jobs.append((len(units), D // rows, c, w, heads))
        units += weight_units(w_in[:, c:c + w], rows=rows)
    return units, jobs


def second_projection_stage(env, ht, jobs, proj, vec2, iw, lam):
    nc, ps, ident, causal, stream = env.nc, env.ps, env.ident, env.causal, env.stream
    names = ("tile_done", "tile_stored", "squared", "roots", "inverses", "scaled", "lambda_dots", "lambda_exps", "rotated",
             "turned", "turned_copied", "logits_ready", "relu_done", "added", "vector_step")
    (tile_done, tile_stored, squared, roots, inverses, scaled, dots, exps, rotated, turned, turned_copied, logits_ready,
     relu_done, added, step) = (env.sem("proj2", n) for n in names)
    TAKEN = -3e38
    NH = BANK // HD
    N = jobs[-1][0] + jobs[-1][1]
    job_of = [c for c, j in enumerate(jobs) for _ in range(j[1])]
    normed = [c for c, j in enumerate(jobs) if j[4]]
    ends = {c: jobs[c][0] + jobs[c][1] - 1 for c in range(len(jobs))}
    index_done = 2
    tiles = list(range(N_TOP // P, T))
    logits = [(t, h) for t in tiles for h in range(IDX_H)]
    NTURN = IDX_H // 2 + 1
    first = jobs[index_done][0] + 1
    slots = [(u, t) for u in range(first, N) for t in range(T)]
    turns_at = {slots[i // 2]: range(i, min(i + 2, NTURN)) for i in range(0, NTURN, 2)}
    after = (NTURN + 1) // 2
    logits_at = {slots[after + i // 3]: range(i, min(i + 3, len(logits))) for i in range(0, len(logits), 3)}

    with ExitStack() as local:
        def tile(name, *shape):
            return local.enter_context(nc.sbuf_tensor(name, [P, *shape], F32))
        ss = tile("head_ss", len(normed), T, NH)
        squares = tile("head_squares", NH, HD)
        ik2 = tile("ik2", T, P)
        iqk_t = tile("iqk_t", NTURN, S)
        relu = tile("index_relu", 2, S)
        top = tile("index_top", T, 8)
        a, b = tile("rope_a", T, NH + 1, HALF), tile("rope_b", T, NH + 1, HALF)
        tables = tile("rope_tables", 2, 4, T, HALF)
        lt, dot = tile("lam_tmp", HD), tile("lam_dot", 2)
        iq = proj[:, :, B_IQ:B_IK + HD].rearrange("p t (h c) -> p t h c", h=IDX_H + 1)

        with nc.Block() as block:
            @block.sync
            def _(sp):
                stream.load(sp, N + stream.RAW)

            @block.tensor
            def _(pe):
                for n in range(N):
                    c = job_of[n]
                    u0, nu, col, w, _ = jobs[c]
                    w_hi, w_lo = stream.ready(pe, n)
                    ks = KD // nu
                    for t in range(T):
                        if n == u0 and c:
                            pe.wait_ge(tile_stored, (c - 1) * T + t + 1)
                        for j in range(ks):
                            k = (n - u0) * ks + j
                            lhs = tuple(x[:, k, t * P:(t + 1) * P] for x in ht)
                            last = product(nc, ps[:, t, 0:w], lhs, (w_hi[:, j], w_lo[:, j]), k == 0, k == KD - 1)
                        if t == T - 1:
                            last.then_inc(stream.used, 1)
                        elif n == ends[c]:
                            last.then_inc(tile_done, 1)
                        for i in turns_at.get((n, t), ()):
                            pe.wait_ge(rotated, 1)
                            if i >= 4:
                                pe.wait_ge(turned_copied, i - 3)
                            for s in range(T):
                                src = ik2[:, s, :] if i == NTURN - 1 else proj[:, s, B_IQ + i * P:B_IQ + (i + 1) * P]
                                last = nc.tensor.transpose(ps[:, T + i % 4, s * P:(s + 1) * P], src, ident)
                            last.then_inc(turned, 1)
                        for i in logits_at.get((n, t), ()):
                            s, h = logits[i]
                            base = (h % 2) * HD
                            pe.wait_ge(turned_copied, NTURN)
                            if i >= 4:
                                pe.wait_ge(relu_done, i - 3)
                            nc.tensor.matmul(ps[:, T + i % 4, 0:(s + 1) * P],
                                             iqk_t[base:base + HD, h // 2, s * P:(s + 1) * P],
                                             iqk_t[base:base + HD, NTURN - 1, 0:(s + 1) * P], start=True, stop=True
                                             ).then_inc(logits_ready, 1)

            @block.scalar
            def _(act):
                act.wait_ge(dots, 1)
                nc.scalar.activation(dot[:, :], dot[:, :], ACT.Exp).then_inc(exps, 1)
                for n in range(-1, N):
                    if n + 1 < N:
                        stream.split_hi(act, n + 1)
                    if n < 0:
                        continue
                    c = job_of[n]
                    _, _, col, w, heads = jobs[c]
                    for t in range(T):
                        if n == ends[c]:
                            if t < T - 1:
                                act.wait_ge(tile_done, c * (T - 1) + t + 1)
                            else:
                                act.wait_ge(stream.used, n + 1)
                            nc.scalar.activation(proj[:, t, col:col + w], ps[:, t, 0:w], ACT.Copy
                                                 ).then_inc(tile_stored, 1)
                            i = normed.index(c) if heads else 0
                            if heads:
                                act.wait_ge(tile_stored, c * T + t + 1)
                            if heads and i * T + t:
                                act.wait_ge(squared, (i * T + t) * NH)
                            for h in range(NH if heads else 0):
                                nc.scalar.activation(squares[:, h, :], proj[:, t, col + h * HD:col + (h + 1) * HD],
                                                     ACT.Square, accum_out=ss[:, i, t, h:h + 1]
                                                     ).then_inc(squared, 1)
                        for i in turns_at.get((n, t), ()):
                            act.wait_ge(turned, i + 1)
                            nc.scalar.activation(iqk_t[:, i, :], ps[:, T + i % 4, :], ACT.Copy
                                                 ).then_inc(turned_copied, 1)
                        for i in logits_at.get((n, t), ()):
                            s, h = logits[i]
                            act.wait_ge(logits_ready, i + 1)
                            if i >= 2:
                                act.wait_ge(added, i - 1)
                            nc.scalar.activation(relu[:, i % 2, 0:(s + 1) * P], ps[:, T + i % 4, 0:(s + 1) * P],
                                                 ACT.Relu, scale=HD ** -0.5).then_inc(relu_done, 1)
                    if heads and n == ends[c]:
                        i = normed.index(c)
                        act.wait_ge(squared, (i + 1) * T * NH)
                        nc.scalar.activation(ss[:, i, :, :], ss[:, i, :, :], ACT.Sqrt, scale=1.0 / HD, bias=env.eps6
                                             ).then_inc(roots, 1)

            @block.gpsimd
            def _(pool):
                for n in range(N):
                    stream.split_lo(pool, n)
                    for i, c in enumerate(normed):
                        if n == ends[c] + 3:
                            pool.wait_ge(inverses, i + 1)
                            x = proj[:, :, jobs[c][2]:jobs[c][2] + BANK]
                            for t in range(T):
                                last = nc.gpsimd.tensor_tensor(by_head(x[:, t], NH), by_head(x[:, t], NH),
                                                               per_tile(ss[:, i, t, :], HD), ALU.mult)
                            last.then_inc(scaled, 1)

            @block.vector
            def _(dve):
                link = Link(dve, step)
                v = nc.vector
                cos2, sin2 = env.cos2, env.sin2

                def make_tables(g):
                    for side, gains in enumerate((V2_Q, V2_K)):
                        for half in range(2):
                            o = gains + g * HD + half * HALF
                            gain = vec2[:, o:o + HALF].unsqueeze(1).to_broadcast([P, T, HALF])
                            v.tensor_tensor(tables[:, side, 2 * half], cos2, gain, ALU.mult)
                            last = v.tensor_tensor(tables[:, side, 2 * half + 1], sin2, gain, ALU.mult)
                    link(last)

                def rotate(x1, x2, c1, s1, c2, s2, nh):
                    shape = [P, T, nh, HALF]
                    c1, s1, c2, s2 = (m.unsqueeze(2).to_broadcast(shape) for m in (c1, s1, c2, s2))
                    p, q = a[:, :, 0:nh, :], b[:, :, 0:nh, :]
                    v.tensor_tensor(p, x1, s1, ALU.mult)
                    v.tensor_tensor(q, x2, s2, ALU.mult)
                    v.tensor_tensor(x1, x1, c1, ALU.mult)
                    link(v.tensor_tensor(x2, x2, c2, ALU.mult))
                    v.tensor_tensor(x1, x1, q, ALU.subtract)
                    return v.tensor_tensor(x2, x2, p, ALU.add)

                def invert(i):
                    dve.wait_ge(roots, i + 1)
                    v.reciprocal(ss[:, i, :, :], ss[:, i, :, :]).then_inc(inverses, 1)

                def rotate_job(i):
                    _, _, col, w, (g, sides) = jobs[normed[i]]
                    if i == 0 or jobs[normed[i - 1]][4][0] != g:
                        make_tables(g)
                    dve.wait_ge(scaled, i + 1)
                    x = proj[:, :, col:col + BANK].rearrange("p t (h c) -> p t h c", h=NH)
                    for part, side in enumerate(sides):
                        xs = x[:, :, part * NH // 2:(part + 1) * NH // 2, :]
                        last = rotate(xs[:, :, :, 0:HALF], xs[:, :, :, HALF:HD], *(tables[:, side, m] for m in range(4)),
                                      NH // 2)
                        link(last)

                def add_up(which):
                    for i in which:
                        t, h = logits[i]
                        dve.wait_ge(relu_done, i + 1)
                        sc, w = index_score(proj, t), iw[:, t, h:h + 1]
                        r = relu[:, i % 2, 0:(t + 1) * P]
                        if h == 0:
                            ins = v.tensor_scalar(sc, r, w, None, ALU.mult)
                        else:
                            ins = v.scalar_tensor_tensor(out=sc, in0=r, scalar=w, in1=sc, op0=ALU.mult, op1=ALU.add)
                        ins.then_inc(added, 1)
                        dve.wait_ge(added, i + 1)

                def find_top(rounds):
                    for r in rounds:
                        for t in tiles:
                            last = v.max(top[:, t, :], index_score(proj, t))
                        link(last)
                        for t in tiles:
                            last = v.match_replace(index_score(proj, t), top[:, t, :], index_score(proj, t), TAKEN)
                        link(last)

                for n in range(2):
                    o = V2_L + 2 * n * HD
                    link(v.tensor_tensor(lt[:, :], vec2[:, o:o + HD], vec2[:, o + HD:o + 2 * HD], ALU.mult))
                    link(v.reduce_sum(dot[:, n:n + 1], lt[:, :], AX))
                v.tensor_scalar(dot[:, :], dot[:, :], 1.0, None, ALU.mult).then_inc(dots, 1)
                dve.wait_ge(exps, 1)
                link(v.tensor_tensor(lam, dot[:, 1:2], dot[:, 0:1], ALU.subtract))
                link(v.tensor_tensor(lam, lam, env.lam_c[:, 0:1], ALU.subtract))
                dve.wait_ge(tile_stored, index_done * T)
                link(rotate(iq[:, :, :, 0:HALF], iq[:, :, :, HALF:HD], cos2, sin2, cos2, sin2, IDX_H + 1))
                link(v.tensor_scalar(iw[:, :, :], proj[:, :, B_IW:B_IW + IDX_H], IDX_H ** -0.5, None, ALU.mult))
                for n in range(2):
                    last = v.tensor_copy(ik2[:, :, n * HD:(n + 1) * HD], proj[:, :, B_IK:B_IK + HD])
                last.then_inc(rotated, 1)
                add_up(range(0, IDX_H))
                invert(0)
                add_up(range(IDX_H, len(logits)))
                for t in tiles:
                    diag = index_score(proj, t)[:, t * P:(t + 1) * P]
                    last = v.tensor_tensor(diag, diag, causal, ALU.add)
                link(last)
                ROUNDS = N_TOP // 8
                share = ROUNDS // len(normed)
                for i in range(len(normed)):
                    rotate_job(i)
                    if i + 1 < len(normed):
                        invert(i + 1)
                    find_top(range(i * share, (i + 1) * share if i + 1 < len(normed) else ROUNDS))
                for t in tiles:
                    v.tensor_scalar(index_score(proj, t), index_score(proj, t), TAKEN, MASKED, ALU.not_equal, ALU.mult)


def diff_end_stage(env, d1, d2, vec2, lam):
    nc = env.nc
    squares, roots, step = (env.sem("diff_end", n) for n in ("squares_summed", "roots", "vector_step"))
    NH, W = 4, 128
    with ExitStack() as local:
        sq = local.enter_context(nc.sbuf_tensor("diff_sq", [P, NH * W], F32))
        ss = local.enter_context(nc.sbuf_tensor("diff_ss", [P, T * NH], F32))
        gain = local.enter_context(nc.sbuf_tensor("diff_gain", [P, W], F32))
        with nc.Block() as block:
            @block.vector
            def _(dve):
                link = Link(dve, step)
                v = nc.vector
                link(v.tensor_scalar(gain[:, :], vec2[:, V2_S:V2_S + W], env.lam_c[:, 1:2], None, ALU.mult))
                for t in range(T):
                    y = d1[:, t, :]
                    link(v.scalar_tensor_tensor(out=y, in0=d2[:, t, :], scalar=lam, in1=y, op0=ALU.mult, op1=ALU.add))
                    link(v.tensor_tensor(sq[:, :], y, y, ALU.mult))
                    link(v.reduce_sum(ss[:, t * NH:(t + 1) * NH], by_head(sq[:, :], NH), AX))
                v.tensor_scalar(ss[:, :], ss[:, :], 1.0 / W, 1e-6, ALU.mult, ALU.add).then_inc(squares, 1)
                dve.wait_ge(roots, 1)
                link(v.reciprocal(ss[:, :], ss[:, :]))
                for t in range(T):
                    y = by_head(d1[:, t, :], NH)
                    link(v.tensor_tensor(y, y, per_tile(ss[:, t * NH:(t + 1) * NH], W), ALU.mult))
                    v.tensor_tensor(y, y, gain[:, :].unsqueeze(1).to_broadcast([P, NH, W]), ALU.mult)

            @block.scalar
            def _(act):
                act.wait_ge(squares, 1)
                nc.scalar.activation(ss[:, :], ss[:, :], ACT.Sqrt).then_inc(roots, 1)


def second_layer(env, l, dram, x):
    nc = env.nc
    at = layer_of(dram, l)
    KP = [range(0, 4), range(4, 8)]
    w_gate, w_up, w_down = at("w_gate_2"), at("w_up_2"), at("w_down_2")
    units, jobs = second_projection_units(at("w_in_2"))
    first_out = len(units)
    first_ffn = first_out + 4
    units += weight_units(at("w_out_2"))
    for c in range(0, D_FF, F_CH):
        for w in (w_gate, w_up):
            units.append(w[:, c:c + F_CH].rearrange("(k p) w -> p k w", p=P))
    env.stream = WeightStream(env, units + weight_units(w_down))

    with ExitStack() as local:
        def tile(ctx, name, *shape):
            return ctx.enter_context(nc.sbuf_tensor(name, [P, *shape], F32))
        vec2, gains = tile(local, "vec2", NV2), tile(local, "gains2", 2 * KD)
        env.lam_c = tile(local, "lam_c", 2)
        load_small_stage(env, "small2", [(vec2[:, :], at("vec2").to_broadcast([P, NV2])),
                                         (gains[:, :], at("gains2")),
                                         (env.lam_c[:, :], at("lam_init").to_broadcast([P, 2]))], env.stream.RAW)

        def normed_turned(ctx, stage, gain):
            ht = pair_tile(nc, ctx, f"{stage}_ht", KD, S)
            with nc.sbuf_tensor(f"{stage}_h", [P, T, D], F32) as h:
                rms_stage(env, f"{stage}_rms", x, h)
                transpose_stage(env, f"{stage}_t", pair_transposes(lambda t, k: h[:, t, k * P:(k + 1) * P], ht, gain))
            return ht

        with ExitStack() as mix:
            proj = tile(mix, "proj2", T, IN2)
            iw, lam = tile(mix, "iw", T, IDX_H), tile(mix, "lam", 1)
            with ExitStack() as pre:
                ht = normed_turned(pre, "attn", gains[:, 0:KD])
                second_projection_stage(env, ht, jobs, proj, vec2, iw, lam[:, 0:1])
            with ExitStack() as heads:
                qk_t = tile(heads, "qk_t", 16, S)
                cols = ([B_MQ + c * P for c in range(4)] + [B_DQ + c * P for c in range(8)]
                        + [B_SQ + c * P for c in range(4)])
                transpose_stage(env, "qk_t", [([proj[:, t, c:c + P] for t in range(T)], qk_t[:, n, :], None)
                                              for n, c in enumerate(cols)])

                second_of_pair = proj[:, :, B_DK:B_DK + 512]

                def half(chunk, h):
                    base = (h % 2) * HD
                    return qk_t[base:base + HD, chunk + h // 2, :]

                units = []
                for name, nh, q0, k0 in (("moba", 4, 0, 2), ("diff", 8, 4, 8), ("dsa", 4, 12, 14)):
                    for h in range(nh):
                        for t in range(T):
                            nk = (t + 1) * P
                            u = dict(q=half(q0, h)[:, t * P:nk], k=half(k0, h)[:, 0:nk], nk=nk, mask="diag")
                            if name == "moba":
                                u["v"] = [proj[:, b, B_MV + h * HD:B_MV + (h + 1) * HD] for b in range(t + 1)]
                                u["dst"] = proj[:, t, B_MQ + h * HD:B_MQ + (h + 1) * HD]
                            elif name == "dsa":
                                u["v"] = [proj[:, b, B_SV + h * HD:B_SV + (h + 1) * HD] for b in range(t + 1)]
                                u["dst"] = proj[:, t, B_SQ + h * HD:B_SQ + (h + 1) * HD]
                                if t >= N_TOP // P:
                                    u["mask"] = index_score(proj, t)
                            else:
                                g = slice((h // 2) * P, (h // 2 + 1) * P)
                                u["v"] = [proj[:, b, B_DV:B_DV + 512][:, g] for b in range(t + 1)]
                                u["dst"] = second_of_pair[:, t, g] if h % 2 else proj[:, t, B_DQ:B_DQ + 512][:, g]
                            units.append(u)
                attention_stage(env, "attn2", units, HD ** -0.5, prefetch=first_out + 3)
            diff_end_stage(env, proj[:, :, B_DQ:B_DQ + 512], second_of_pair, vec2, lam[:, 0:1])
            yt = pair_tile(nc, mix, "y2t", KD, S)
            place = [B_MQ, B_MQ + P] + [B_DQ + c * P for c in range(4)] + [B_SQ, B_SQ + P]
            transpose_stage(env, "y2_t", pair_transposes(lambda t, k: proj[:, t, place[k]:place[k] + P], yt))
            jobs = [(chunks_of(yt), KP, BANK, [(lambda b: b, lambda t, n=n: x[:, t, n * BANK:(n + 1) * BANK])])
                    for n in range(2)]
            project_stage(env, "out2", first_out, jobs, alpha_x=1.0, prefetch=3)
        ht = normed_turned(local, "ffn", gains[:, KD:2 * KD])
        ffn_stage(env, "ffn", first_ffn, ht, FF_CH, x)


def build(nc, dram, out, debug=None):
    with ExitStack() as ctx:
        env = Env(nc)

        def tile(name, *shape):
            return ctx.enter_context(nc.sbuf_tensor(name, [P, *shape], F32))
        x = tile("x", T, D)
        env.raw = tile("weights_raw", WeightStream.RAW, WeightStream.UNIT)
        env.w_hi, env.w_lo = pair_tile(nc, ctx, "weights", WeightStream.SPLIT, WeightStream.UNIT)
        env.consts = tile("consts", NK)
        eps = tile("eps", 2)
        cos1, sin1 = tile("cos1", T, ROPE // 2), tile("sin1", T, ROPE // 2)
        env.ps = ctx.enter_context(nc.psum_tensor("ps", [P, NBANK, BANK], F32))
        env.ident = env.consts[:, K_ID:K_ID + P]
        env.keep_ge = env.consts[:, K_GE:K_GE + P]
        env.ones = env.consts[:, K_ONES:K_ONES + P]
        env.slot_numbers = env.consts[:, K_SLOT:K_SLOT + SLOTS]
        env.keep_le = env.consts[:, K_LE:K_LE + P]
        env.causal = env.consts[:, K_CAUSAL:K_CAUSAL + P]
        env.cos2 = env.consts[:, K_COS:K_COS + T * HALF].rearrange("p (t c) -> p t c", t=T)
        env.sin2 = env.consts[:, K_SIN:K_SIN + T * HALF].rearrange("p (t c) -> p t c", t=T)
        env.eps5, env.eps6 = eps[:, 0:1], eps[:, 1:2]
        saved = ctx.enter_context(nc.semaphore("output_saved"))
        start_loaded = ctx.enter_context(nc.semaphore("start_loaded"))

        with nc.Block() as block:
            @block.sync
            def _(sp):
                sp.dma_start(x[:, :, :], dram["x"].rearrange("a (t p) d -> p (a t) d", p=P)).then_inc(start_loaded, 16)
                sp.dma_start(env.consts[:, :], dram["consts"]).then_inc(start_loaded, 16)
                sp.wait_ge(start_loaded, 32)

            @block.vector
            def _(dve):
                nc.vector.memset(eps[:, 0:1], 1e-5)
                nc.vector.memset(eps[:, 1:2], 1e-6)
        with env.semaphores():
            rope_table_stage(env, dram["positions"], cos1[:, :, :], sin1[:, :, :])
            env.end_layer()
        with env.semaphores(), nc.Fori(0, DEPTH) as l, ExitStack() as local:
            vec = local.enter_context(nc.sbuf_tensor("vec1", [P, NV1], F32))
            with nc.sbuf_tensor("convw", [P, CC, CONV + 1], F32) as convw:
                first_mixers(env, l, dram, x, vec, convw, cos1[:, :, :], sin1[:, :, :])
            env.end_layer()
            first_experts(env, l, dram, x, vec)
            env.end_layer()
        with env.semaphores(), nc.Fori(0, DEPTH) as l:
            second_layer(env, l, dram, x)
            env.end_layer()
        with nc.Block() as block:
            @block.sync
            def _(sp):
                sp.dma_start(out.rearrange("a (t p) d -> p (a t) d", p=P), x[:, :, :]).then_inc(saved, 16)
                sp.wait_ge(saved, 16)


def constants():
    c = np.zeros((P, NK), np.float32)
    i = np.arange(P)
    c[:, K_ID:K_ID + P] = np.eye(P)
    c[:, K_GE:K_GE + P] = i[None, :] >= i[:, None]
    c[:, K_LE:K_LE + P] = i[None, :] <= i[:, None]
    c[:, K_CAUSAL:K_CAUSAL + P] = np.where(i[None, :] <= i[:, None], 0.0, MASKED)
    c[:, K_ONES:K_ONES + P] = 1.0
    c[:, K_SLOT:K_SLOT + SLOTS] = np.arange(1, SLOTS + 1)
    f = np.float32
    inv = f(1.0) / f(10000.0) ** (np.arange(0, HD, 2, dtype=f) / f(HD))
    ang = (np.arange(S, dtype=f)[:, None] * inv[None, :]).reshape(T, P, HALF).transpose(1, 0, 2)
    c[:, K_COS:K_COS + T * HALF] = np.cos(ang).reshape(P, -1)
    c[:, K_SIN:K_SIN + T * HALF] = np.sin(ang).reshape(P, -1)
    c[:, K_INV:K_INV + ROPE // 2] = f(10000.0) ** (-np.arange(0, ROPE, 2, dtype=f) / f(ROPE))
    return c


def packed(i):
    n = DEPTH

    def rows(*names):
        return np.concatenate([np.asarray(i[k]).reshape(n, -1) for k in names], 1)

    def by_partition(a):
        return np.asarray(a).reshape(n, KD, P).transpose(0, 2, 1)

    conv = np.concatenate([np.asarray(i["ssd_conv_w"]), np.asarray(i["ssd_conv_b"])[:, None]], 1)
    lam0 = [0.8 - 0.6 * float(np.exp(-0.3 * l)) for l in range(n)]
    arrays = {
        "consts": constants(),
        "vec1": rows("mla_q_norm", "mla_kv_norm", "mlstm_gate_bias", "mlstm_norm", "ssd_dt_bias", "ssd_a_log",
                     "ssd_d", "ssd_norm", "router_group_b", "router_expert_b"),
        "conv1": conv.transpose(0, 2, 1).reshape(n, CC, P, CONV + 1).transpose(0, 2, 1, 3),
        "ln1": rows("ln1_g", "ln1_b"), "ln2": rows("ln2_g", "ln2_b"),
        "router": np.concatenate([np.asarray(i["router_group_w"]),
                                  np.asarray(i["router_expert_w"]).transpose(0, 2, 1, 3).reshape(n, D, EXPERTS)], 2),
        "vec2": rows("q_norm_g_2", "k_norm_g_2", "diff_lambda_2", "diff_subln_g_2"),
        "gains2": np.concatenate([by_partition(i["attn_norm_g_2"]), by_partition(i["ffn_norm_g_2"])], 2),
        "lam_init": np.array([[a, 1.0 - a] for a in lam0], np.float32),
    }
    for k in ("x", "positions", "w_in", "mla_w_uq", "mla_w_ukv", "w_out", "expert_w_gate", "expert_w_up",
              "expert_w_down", "w_in_2", "w_out_2", "w_gate_2", "w_up_2", "w_down_2"):
        arrays[k] = np.asarray(i[k])
    return {k: np.ascontiguousarray(v) for k, v in arrays.items()}


def kernel(**inputs):
    import concourse.bacc as bacc
    from concourse.bass_utils import run_bass_kernel_spmd

    nc = bacc.Bacc("TRN2", target_bir_lowering=False, num_devices=1)
    arrays = packed(inputs)
    dram = {k: nc.dram_tensor(f"in_{k}", list(a.shape), mybir.dt.from_np(a.dtype), kind="ExternalInput").ap()
            for k, a in arrays.items()}
    out = nc.dram_tensor("out_x", [1, S, D], F32, kind="ExternalOutput").ap()
    build(nc, dram, out)
    r = run_bass_kernel_spmd(nc, [{f"in_{k}": a for k, a in arrays.items()}], core_ids=[0])
    return r.results[0]["out_x"]
```

```python
from contextlib import ExitStack, contextmanager

import numpy as np

import concourse.bass as bass
from concourse import mybir

F32 = mybir.dt.float32
F32R = mybir.dt.float32r
I32 = mybir.dt.int32
ALU = mybir.AluOpType
ACT = mybir.ActivationFunctionType
AX = mybir.AxisListType.X

P = 128
S = 512
T = S // P
D = 1024
KD = D // P
DEPTH = 2
BANK = 512
NBANK = 8
MASKED = -1e30
ALPHA = (2 * DEPTH) ** 0.25

MLA_H, NOPE, ROPE, MLA_V = 8, 64, 32, 64
QK = NOPE + ROPE
Q_RANK, KV_RANK = 256, 128
ML_H, ML_D = 4, 64
SSD_H, SSD_P, SSD_G, SSD_N, CONV = 4, 64, 2, 128, 5
PAD = CONV // 2
CQ = 0
CKV = CQ + Q_RANK
KR = CKV + KV_RANK
MQ = KR + ROPE
MK = MQ + ML_H * ML_D
MV = MK + ML_H * ML_D
MO = MV + ML_H * ML_D
MG = MO + ML_H * ML_D
SZ = MG + 4 * ML_H
XBC = SZ + SSD_H * SSD_P
NXBC = SSD_H * SSD_P + 2 * SSD_G * SSD_N
SDT = XBC + NXBC
IN1 = SDT + 2 * SSD_H
CC = NXBC // P
GROUPS, PER_GROUP = 4, 4
EXPERTS = GROUPS * PER_GROUP
NR = GROUPS + EXPERTS
SLOTS = 192
F_CH = 256

V_Q, V_KV, V_GB, V_MN, V_DTB, V_AL, V_SD, V_SN, V_RB = np.cumsum(
    [0, Q_RANK, KV_RANK, 4 * ML_H, ML_H * ML_D, 2 * SSD_H, 2 * SSD_H, SSD_H, SSD_H * SSD_P]).tolist()
NV1 = V_RB + NR

HD = 64
HALF = HD // 2
B_MQ, B_MK, B_MV, B_DQ, B_DK, B_DV, B_SQ, B_SK, B_SV, B_IQ, B_IK, B_IW, IN2 = np.cumsum(
    [0, 256, 256, 256, 512, 512, 512, 256, 256, 256, 512, 64, 8]).tolist()
IDX_H = 8
N_TOP = min(256, S // 4)
D_FF = 2816
FF_CH = D_FF // F_CH
V2_Q, V2_K, V2_L = 0, 192, 384
NV2 = 640

K_ID, K_GE, K_LE, K_ONES, K_CAUSAL, K_COS, K_SIN, K_INV, K_SLOT, NK = np.cumsum(
    [0, P, P, P, P, P, T * HALF, T * HALF, ROPE // 2, SLOTS]).tolist()


class Env:

    def __init__(self, nc):
        self.nc, self.ctx, self.sems = nc, None, {}

    def sem(self, stage, name):
        key = f"{stage}_{name}"
        if key not in self.sems:
            self.sems[key] = self.ctx.enter_context(self.nc.semaphore(key))
        return self.sems[key]

    @contextmanager
    def semaphores(self):
        with ExitStack() as ctx:
            self.ctx, self.sems = ctx, {}
            yield

    def end_layer(self):
        nums = [s.num for s in self.sems.values()]
        self.nc.all_engine_barrier(sems_to_clear=range(min(nums), max(nums) + 1))


class Link:

    def __init__(self, eng, sem):
        self.eng, self.sem, self.n = eng, sem, 0

    def __call__(self, ins):
        ins.then_inc(self.sem, 1)
        self.n += 1
        self.eng.wait_ge(self.sem, self.n)


def per_tile(ap, width):
    return ap.unsqueeze(2).to_broadcast([ap.shape[0], ap.shape[1], width])



class WeightStream:
    RAW, SPLIT, UNIT = 3, 2, 2048

    def __init__(self, env, sources):
        self.nc, self.env, self.sources, self.sent = env.nc, env, sources, 0
        self.hi_split = self.lo_split = 0
        self.loaded = [env.sem("stream", f"loaded{s}") for s in range(self.RAW)]
        self.hi_ready, self.lo_ready = env.sem("stream", "hi_ready"), env.sem("stream", "lo_ready")
        self.used = env.sem("stream", "used")

    def views(self, u, tile):
        a, b = self.sources[u].shape[1:]
        return tile[:, 0:a * b].rearrange("p (a b) -> p a b", a=a)

    def load(self, sp, upto):
        for u in range(self.sent, min(upto, len(self.sources))):
            if u >= self.RAW:
                sp.wait_ge(self.lo_ready, u - self.RAW + 1)
            sp.dma_start(self.views(u, self.env.raw[:, u % self.RAW]), self.sources[u]
                         ).then_inc(self.loaded[u % self.RAW], 16)
            self.sent = u + 1

    def split_hi(self, act, u):
        if not self.hi_split <= u < len(self.sources):
            return
        self.hi_split = u + 1
        act.wait_ge(self.loaded[u % self.RAW], 16 * (u // self.RAW + 1))
        if u >= self.SPLIT:
            act.wait_ge(self.used, u - self.SPLIT + 1)
        n = int(np.prod(self.sources[u].shape[1:]))
        self.nc.scalar.activation(self.env.w_hi[:, u % self.SPLIT, 0:n], self.env.raw[:, u % self.RAW, 0:n], ACT.Copy
                                  ).then_inc(self.hi_ready, 1)

    def split_lo(self, eng, u):
        if not self.lo_split <= u < len(self.sources):
            return
        self.lo_split = u + 1
        eng.wait_ge(self.hi_ready, u + 1)
        n = int(np.prod(self.sources[u].shape[1:]))
        eng.tensor_tensor(self.env.w_lo[:, u % self.SPLIT, 0:n], self.env.raw[:, u % self.RAW, 0:n],
                                     self.env.w_hi[:, u % self.SPLIT, 0:n].bitcast(F32), ALU.subtract
                                     ).then_inc(self.lo_ready, 1)

    def ready(self, pe, u):
        pe.wait_ge(self.lo_ready, u + 1)
        return self.views(u, self.env.w_hi[:, u % self.SPLIT]), self.views(u, self.env.w_lo[:, u % self.SPLIT])


def product(nc, out, a, b, start, stop, **more):
    nc.tensor.matmul(out, a[0], b[0], start=start, stop=False, **more)
    nc.tensor.matmul(out, a[0], b[1], start=False, stop=False, **more)
    return nc.tensor.matmul(out, a[1], b[0], start=False, stop=stop, **more)


def exact_product(nc, out, a, b, start, stop, **more):
    if isinstance(a, tuple):
        nc.tensor.matmul(out, a[0], b, start=start, stop=False, **more)
        return nc.tensor.matmul(out, a[1], b, start=False, stop=stop, **more)
    nc.tensor.matmul(out, a, b[0], start=start, stop=False, **more)
    return nc.tensor.matmul(out, a, b[1], start=False, stop=stop, **more)


def transpose_stage(env, stage, jobs, ahead=None):
    nc, ps, ident = env.nc, env.ps, env.ident
    pairs = isinstance(jobs[0][1], tuple)
    turned = env.sem(stage, "turned")
    act_copied, dve_copied = env.sem(stage, "act_copied"), env.sem(stage, "dve_copied")

    with nc.Block() as block:
        @block.tensor
        def _(pe):
            for i, (srcs, dst, scale) in enumerate(jobs):
                if i >= NBANK:
                    if pairs:
                        pe.wait_ge(dve_copied, i - NBANK + 1)
                    else:
                        pe.wait_ge(dve_copied if i % 2 else act_copied, (i - NBANK) // 2 + 1)
                for j, src in enumerate(srcs):
                    w = src.shape[1]
                    last = nc.tensor.transpose(ps[0:w, i % NBANK, j * P:(j + 1) * P], src, ident)
                last.then_inc(turned, 1)

        def bank(eng, i):
            srcs, dst, scale = jobs[i]
            eng.wait_ge(turned, i + 1)
            return ps[0:srcs[0].shape[1], i % NBANK, 0:len(srcs) * P], dst, scale

        @block.scalar
        def _(act):
            if ahead is not None:
                env.stream.split_hi(act, ahead)
            for i in range(0, len(jobs), 1 if pairs else 2):
                src, dst, scale = bank(act, i)
                nc.scalar.activation(dst[0] if pairs else dst, src, ACT.Copy if scale is None else ACT.Identity,
                                     scale=1.0 if scale is None else scale).then_inc(act_copied, 1)

        @block.vector
        def _(dve):
            for i in range(0 if pairs else 1, len(jobs), 1 if pairs else 2):
                src, dst, scale = bank(dve, i)
                if pairs:
                    dve.wait_ge(act_copied, i + 1)
                    hi = dst[0].bitcast(F32)
                    if scale is None:
                        ins = nc.vector.tensor_tensor(dst[1], src, hi, ALU.subtract)
                    else:
                        ins = nc.vector.scalar_tensor_tensor(out=dst[1], in0=src, scalar=scale, in1=hi,
                                                             op0=ALU.mult, op1=ALU.subtract)
                elif scale is None:
                    ins = nc.vector.tensor_copy(dst, src)
                else:
                    ins = nc.vector.tensor_scalar(dst, src, scale, None, ALU.mult)
                ins.then_inc(dve_copied, 1)

        if ahead is not None:
            @block.gpsimd
            def _(pool):
                env.stream.split_lo(pool, ahead)


def weight_units(weights, width=BANK, rows=4 * P):
    K, N = weights.shape
    return [weights[r:min(r + rows, K), c:min(c + width, N)].rearrange("(k p) w -> p k w", p=P)
            for c in range(0, N, width) for r in range(0, K, rows)]


def project_stage(env, stage, first, jobs, alpha_x=None, prefetch=0):
    nc, ps, stream = env.nc, env.ps, env.stream
    act_done, dve_done = env.sem(stage, "act_stored"), env.sem(stage, "dve_stored")
    ends, units = [], []
    for c, (lhs, parts, w, pieces) in enumerate(jobs):
        for n, ks in enumerate(parts):
            units.append((c, ks, n == 0, n == len(parts) - 1))
        ends.append(len(units) - 1)
    N = len(units)

    def bank(c, t):
        return ps[:, (c % 2) * T + t, :]

    with nc.Block() as block:
        @block.sync
        def _(sp):
            stream.load(sp, first + N + prefetch)

        @block.tensor
        def _(pe):
            for n, (c, ks, is_first, is_last) in enumerate(units):
                lhs, parts, w, pieces = jobs[c]
                if is_first and c >= 2:
                    pe.wait_ge(dve_done, c - 1)
                    if alpha_x is None:
                        pe.wait_ge(act_done, c - 1)
                w_hi, w_lo = stream.ready(pe, first + n)
                for t in range(T):
                    for j, k in enumerate(ks):
                        a = tuple(x[:, t * P:(t + 1) * P] for x in lhs[k])
                        last = product(nc, bank(c, t)[:, 0:w], a, (w_hi[:, j], w_lo[:, j]),
                                       is_first and j == 0, is_last and j == len(ks) - 1)
                last.then_inc(stream.used, 1)

        @block.scalar
        def _(act):
            def store(c):
                act.wait_ge(stream.used, first + ends[c] + 1)
                for t in (0, 2):
                    for view, dst in jobs[c][3]:
                        last = nc.scalar.activation(dst(t), view(bank(c, t)), ACT.Copy)
                last.then_inc(act_done, 1)

            for n in range(N + 2):
                if n < N:
                    stream.split_hi(act, first + n)
                if alpha_x is None and n - 2 in ends:
                    store(ends.index(n - 2))

        @block.vector
        def _(dve):
            def store(c):
                dve.wait_ge(stream.used, first + ends[c] + 1)
                for t in (1, 3) if alpha_x is None else range(T):
                    for view, dst in jobs[c][3]:
                        d, src = dst(t), view(bank(c, t))
                        if alpha_x is None:
                            last = nc.vector.tensor_copy(d, src)
                        else:
                            last = nc.vector.scalar_tensor_tensor(out=d, in0=d, scalar=alpha_x, in1=src,
                                                                  op0=ALU.mult, op1=ALU.add)
                last.then_inc(dve_done, 1)

            for n in range(N + 2):
                if n < N:
                    stream.split_lo(dve, first + n)
                if n - 2 in ends:
                    store(ends.index(n - 2))


def attention_stage(env, stage, units, scale, prob=None, prob_t=None, prefetch=0, meanwhile=None):
    nc, ps, ident, causal = env.nc, env.ps, env.ident, env.causal
    N = len(units)
    scores_ready, max_ready = env.sem(stage, "scores_ready"), env.sem(stage, "max_ready")
    exp_done, turned = env.sem(stage, "exp_done"), env.sem(stage, "turned")
    turned_copied, out_ready = env.sem(stage, "turned_copied"), env.sem(stage, "out_ready")
    out_stored, step = env.sem(stage, "out_stored"), env.sem(stage, "vector_step")

    with ExitStack() as local:
        if prob is None:
            prob = local.enter_context(nc.sbuf_tensor(f"{stage}_prob", [P, 4, S], F32))
            prob_t = local.enter_context(nc.sbuf_tensor(f"{stage}_prob_t", [P, 2, S], F32))
        top = local.enter_context(nc.sbuf_tensor(f"{stage}_top", [P, N], F32))
        total = local.enter_context(nc.sbuf_tensor(f"{stage}_total", [P, N], F32))
        recip = local.enter_context(nc.sbuf_tensor(f"{stage}_recip", [P, N], F32))

        def score_bank(i, nk):
            return ps[:, i % 4, 0:nk]

        with nc.Block() as block:
            @block.sync
            def _(sp):
                env.stream.load(sp, prefetch)

            @block.tensor
            def _(pe):
                for i in range(N + 4):
                    if i < N:
                        u = units[i]
                        if i >= 4:
                            pe.wait_ge(exp_done, i - 3)
                        nc.tensor.matmul(score_bank(i, u["nk"]), u["q"], u["k"], start=True, stop=True
                                         ).then_inc(scores_ready, 1)
                    if 3 <= i < N + 3:
                        j = i - 3
                        pe.wait_ge(exp_done, j + 1)
                        if j >= 2:
                            pe.wait_ge(turned_copied, j - 1)
                        for b in range(units[j]["nk"] // P):
                            last = nc.tensor.transpose(ps[:, 4 + j % 2, b * P:(b + 1) * P],
                                                       prob[:, j % 4, b * P:(b + 1) * P], ident)
                        last.then_inc(turned, 1)
                    if i >= 4:
                        j = i - 4
                        u = units[j]
                        nb = u["nk"] // P
                        pe.wait_ge(turned_copied, j + 1)
                        if j >= 2:
                            pe.wait_ge(out_stored, j - 1)
                        for b in range(nb):
                            w = u["v"][b].shape[1]
                            last = nc.tensor.matmul(ps[:, 6 + j % 2, 0:w], prob_t[:, j % 2, b * P:(b + 1) * P],
                                                    u["v"][b], start=(b == 0), stop=(b == nb - 1))
                        last.then_inc(out_ready, 1)

            @block.vector
            def _(dve):
                link = Link(dve, step)
                for i in range(N + 4):
                    if i < N:
                        u = units[i]
                        dve.wait_ge(scores_ready, i + 1)
                        sc = score_bank(i, u["nk"])
                        if u["mask"] == "diag":
                            last = ps[:, i % 4, u["nk"] - P:u["nk"]]
                            link(nc.vector.tensor_tensor(last, last, causal, ALU.add))
                        elif u["mask"] is not None:
                            link(nc.vector.tensor_tensor(sc, sc, u["mask"], ALU.add))
                        link(nc.vector.reduce_max(top[:, i:i + 1], sc, AX))
                        nc.vector.tensor_scalar(top[:, i:i + 1], top[:, i:i + 1], -scale, None, ALU.mult
                                                ).then_inc(max_ready, 1)
                    if i >= 4:
                        j = i - 4
                        u = units[j]
                        dve.wait_ge(exp_done, j + 1)
                        link(nc.vector.reciprocal(recip[:, j:j + 1], total[:, j:j + 1]))
                        dve.wait_ge(out_ready, j + 1)
                        nc.vector.tensor_scalar(u["dst"], ps[:, 6 + j % 2, 0:u["dst"].shape[1]], recip[:, j:j + 1],
                                                None, ALU.mult).then_inc(out_stored, 1)
                    if meanwhile:
                        meanwhile.vector(dve, i)

            @block.scalar
            def _(act):
                for i in range(N + 3):
                    if i >= 3:
                        j = i - 3
                        nk = units[j]["nk"]
                        act.wait_ge(turned, j + 1)
                        if j >= 2:
                            act.wait_ge(out_ready, j - 1)
                        nc.scalar.activation(prob_t[:, j % 2, 0:nk], ps[:, 4 + j % 2, 0:nk], ACT.Copy
                                             ).then_inc(turned_copied, 1)
                    if i < N:
                        u = units[i]
                        act.wait_ge(max_ready, i + 1)
                        if i >= 4:
                            act.wait_ge(turned, i - 3)
                        nc.scalar.activation(prob[:, i % 4, 0:u["nk"]], score_bank(i, u["nk"]), ACT.Exp,
                                             bias=top[:, i:i + 1], scale=scale,
                                             accum_out=total[:, i:i + 1]).then_inc(exp_done, 1)
                    if meanwhile:
                        meanwhile.scalar(act, i)

            if meanwhile:
                @block.gpsimd
                def _(pool):
                    meanwhile.pool(pool, out_stored)


def layernorm_stage(env, stage, gains, x):
    nc = env.nc
    names = ("gains_loaded", "var_ready", "root_ready", "shift_ready", "centred", "times_g", "vector_step")
    gains_loaded, var_ready, root_ready, shift_ready, centred, times_g, step = (env.sem(stage, n) for n in names)
    with ExitStack() as local:
        gb = local.enter_context(nc.sbuf_tensor(f"{stage}_gb", [P, 2 * D], F32))
        st = local.enter_context(nc.sbuf_tensor(f"{stage}_stats", [P, T, 2, 6], F32))
        mv = local.enter_context(nc.sbuf_tensor(f"{stage}_mv", [P, T, 2], F32))
        rs = local.enter_context(nc.sbuf_tensor(f"{stage}_rs", [P, T], F32))
        shift = local.enter_context(nc.sbuf_tensor(f"{stage}_shift", [P, T], F32))
        with nc.Block() as block:
            @block.sync
            def _(sp):
                sp.dma_start(gb[:, :], gains.to_broadcast([P, 2 * D])).then_inc(gains_loaded, 16)

            @block.vector
            def _(dve):
                link = Link(dve, step)
                v = nc.vector
                for t in range(T):
                    for h in range(2):
                        last = v.bn_stats(st[:, t, h, :], x[:, t, h * BANK:(h + 1) * BANK])
                link(last)
                for t in range(T):
                    last = v.bn_aggr(mv[:, t, :], st[:, t, :, :])
                last.then_inc(var_ready, 1)
                dve.wait_ge(root_ready, 1)
                link(v.reciprocal(rs[:, :], rs[:, :]))
                v.scalar_tensor_tensor(out=shift[:, :], in0=mv[:, :, 0], scalar=-1.0, in1=rs[:, :],
                                       op0=ALU.mult, op1=ALU.mult).then_inc(shift_ready, 1)
                dve.wait_ge(gains_loaded, 16)
                for t in range(T):
                    dve.wait_ge(centred, t + 1)
                    v.tensor_tensor(x[:, t, :], x[:, t, :], gb[:, 0:D], ALU.mult).then_inc(times_g, 1)
                for t in range(2, T):
                    dve.wait_ge(times_g, t + 1)
                    v.tensor_tensor(x[:, t, :], x[:, t, :], gb[:, D:2 * D], ALU.add)

            @block.scalar
            def _(act):
                act.wait_ge(var_ready, 1)
                nc.scalar.activation(rs[:, :], mv[:, :, 1], ACT.Sqrt, bias=env.eps5).then_inc(root_ready, 1)
                act.wait_ge(shift_ready, 1)
                for t in range(T):
                    nc.scalar.activation(x[:, t, :], x[:, t, :], ACT.Identity, scale=rs[:, t:t + 1],
                                         bias=shift[:, t:t + 1]).then_inc(centred, 1)

            @block.gpsimd
            def _(pool):
                pool.wait_ge(gains_loaded, 16)
                for t in range(2):
                    pool.wait_ge(times_g, t + 1)
                    nc.gpsimd.tensor_tensor(x[:, t, :], x[:, t, :], gb[:, D:2 * D], ALU.add)


def ffn_stage(env, stage, first, xt, chunks, x, prefetch=0):
    nc, ps, stream = env.nc, env.ps, env.stream
    FC = F_CH // P
    nf = chunks * FC
    names = ("silu_done", "times_up_done", "hidden_hi", "hidden_lo", "stored")
    gated, sized, hidden_hi, hidden_lo, stored = (env.sem(stage, n) for n in names)
    downs = [(half, list(range(f, min(f + 4, nf)))) for half in range(2) for f in range(0, nf, 4)]
    first_down = 2 * chunks
    N = first_down + len(downs)

    with ExitStack() as local:
        h_hi = local.enter_context(nc.sbuf_tensor(f"{stage}_h_hi", [P, nf, S], F32R))
        h_lo = local.enter_context(nc.sbuf_tensor(f"{stage}_h_lo", [P, nf, S], F32R))
        gate = local.enter_context(nc.sbuf_tensor(f"{stage}_gate", [P, 2, S], F32))

        def bank(c, up, f):
            return ps[:, (c % 2) * 4 + 2 * up + f, :]

        def out_bank(half, t):
            return ps[:, (chunks + half) % 2 * T + t, :]

        with nc.Block() as block:
            @block.sync
            def _(sp):
                stream.load(sp, first + N + prefetch)

            @block.tensor
            def _(pe):
                for n in range(first_down):
                    c, up = n // 2, n % 2
                    if c >= 2 and up == 0:
                        pe.wait_ge(sized, FC * (c - 1))
                    w_hi, w_lo = stream.ready(pe, first + n)
                    for f in range(FC):
                        cols = slice(f * P, (f + 1) * P)
                        for k in range(KD):
                            last = product(nc, bank(c, up, f), (w_hi[:, k, cols], w_lo[:, k, cols]),
                                           (xt[0][:, k, :], xt[1][:, k, :]), k == 0, k == KD - 1)
                    last.then_inc(stream.used, 1)
                for m, (half, fs) in enumerate(downs):
                    if m == 0:
                        pe.wait_ge(sized, nf - FC)
                    if half and not downs[m - 1][0]:
                        pe.wait_ge(sized, nf)
                    pe.wait_ge(hidden_lo, min(nf, fs[-1] + 1))
                    w_hi, w_lo = stream.ready(pe, first + first_down + m)
                    for t in range(T):
                        for j, f in enumerate(fs):
                            a = tuple(h[:, f, t * P:(t + 1) * P] for h in (h_hi, h_lo))
                            last = product(nc, out_bank(half, t), a, (w_hi[:, j], w_lo[:, j]),
                                           f == 0, f == nf - 1)
                    last.then_inc(stream.used, 1)

            @block.scalar
            def _(act):
                for n in range(N + 2):
                    if n < N:
                        stream.split_hi(act, first + n)
                    m = n - 2
                    if not 0 <= m < first_down:
                        continue
                    act.wait_ge(stream.used, first + m + 1)
                    c, up = m // 2, m % 2
                    for f in range(FC):
                        i = c * FC + f
                        if not up:
                            if c:
                                act.wait_ge(hidden_lo, i - FC + 1)
                            nc.scalar.activation(gate[:, f, :], bank(c, 0, f), ACT.Silu).then_inc(gated, 1)
                        else:
                            act.wait_ge(sized, i + 1)
                            nc.scalar.activation(h_hi[:, i, :], gate[:, f, :], ACT.Copy).then_inc(hidden_hi, 1)

            @block.vector
            def _(dve):
                for n in range(N + 2):
                    if n < N:
                        stream.split_lo(dve, first + n)
                    m = n - 2
                    if 0 <= m < first_down and m % 2:
                        c = m // 2
                        dve.wait_ge(stream.used, first + m + 1)
                        for f in range(FC):
                            dve.wait_ge(gated, c * FC + f + 1)
                            nc.vector.tensor_tensor(gate[:, f, :], gate[:, f, :], bank(c, 1, f), ALU.mult
                                                    ).then_inc(sized, 1)
                        for f in range(FC):
                            i = c * FC + f
                            dve.wait_ge(hidden_hi, i + 1)
                            nc.vector.tensor_tensor(h_lo[:, i, :], gate[:, f, :], h_hi[:, i, :].bitcast(F32),
                                                    ALU.subtract).then_inc(hidden_lo, 1)
                    if m - first_down in (len(downs) // 2 - 1, len(downs) - 1):
                        half = downs[m - first_down][0]
                        dve.wait_ge(stream.used, first + m + 1)
                        for t in range(T):
                            d = x[:, t, half * BANK:(half + 1) * BANK]
                            nc.vector.tensor_tensor(d, d, out_bank(half, t), ALU.add).then_inc(stored, 1)


def by_head(ap, heads):
    return ap.rearrange("p (h c) -> p h c", h=heads)


def x_transposes(src, dst, scale=None):
    return [([src[:, t, k * P:(k + 1) * P] for t in range(T)], dst[:, k, :],
             None if scale is None else scale[:, k:k + 1]) for k in range(KD)]


def pair_transposes(src, pair, scale=None):
    return [([src(t, k) for t in range(T)], (pair[0][:, k, :], pair[1][:, k, :]),
             None if scale is None else scale[:, k:k + 1]) for k in range(KD)]



def rope_table_stage(env, positions, cos, sin):
    nc = env.nc
    TWO_PI = 2 * np.pi
    C1 = 6.28125
    C2 = float(np.float32(np.floor((TWO_PI - C1) * 2 ** 21) / 2 ** 21))
    C3 = float(np.float32(TWO_PI - C1 - C2))
    ROUND = 1.5 * 2 ** 23
    pos_loaded, reduced, sines = (env.sem("rope_table", n) for n in ("pos_loaded", "reduced", "sines"))
    step = env.sem("rope_table", "vector_step")
    n = T * ROPE // 2
    with ExitStack() as local:
        pos_i = local.enter_context(nc.sbuf_tensor("rope_pos_i", [P, T], I32))
        pos = local.enter_context(nc.sbuf_tensor("rope_pos", [P, T], F32))
        ang = local.enter_context(nc.sbuf_tensor("rope_ang", [P, T, ROPE // 2], F32))
        turns = local.enter_context(nc.sbuf_tensor("rope_turns", [P, T, ROPE // 2], F32))
        half = local.enter_context(nc.sbuf_tensor("rope_half", [P, T, ROPE // 2], F32))
        with nc.Block() as block:
            @block.sync
            def _(sp):
                sp.dma_start(pos_i[:, :], positions.rearrange("a (t p) -> p (a t)", p=P),
                             allow_slow_non_contiguous=True).then_inc(pos_loaded, 16)

            @block.vector
            def _(dve):
                link = Link(dve, step)
                dve.wait_ge(pos_loaded, 16)
                link(nc.vector.tensor_copy(pos[:, :], pos_i[:, :]))
                inv = env.consts[:, K_INV:K_INV + ROPE // 2].unsqueeze(1).to_broadcast([P, T, ROPE // 2])
                link(nc.vector.tensor_tensor(ang[:, :, :], per_tile(pos[:, :], ROPE // 2), inv, ALU.mult))
                link(nc.vector.tensor_scalar(turns[:, :, :], ang[:, :, :], 1 / TWO_PI, ROUND, ALU.mult, ALU.add))
                link(nc.vector.tensor_scalar(turns[:, :, :], turns[:, :, :], -ROUND, None, ALU.add))
                for c in (C1, C2, C3):
                    link(nc.vector.scalar_tensor_tensor(out=ang[:, :, :], in0=turns[:, :, :], scalar=-c,
                                                        in1=ang[:, :, :], op0=ALU.mult, op1=ALU.add))
                nc.vector.tensor_scalar(ang[:, :, :], ang[:, :, :], float(np.float32(3.1415925)),
                                        float(np.float32(-3.1415925)), ALU.min, ALU.max).then_inc(reduced, 1)
                dve.wait_ge(sines, 2)
                link(nc.vector.tensor_tensor(half[:, :, :], half[:, :, :], half[:, :, :], ALU.mult))
                nc.vector.tensor_scalar(cos, half[:, :, :], -2.0, 1.0, ALU.mult, ALU.add)

            @block.scalar
            def _(act):
                act.wait_ge(reduced, 1)
                nc.scalar.activation(sin, ang[:, :, :], ACT.Sin).then_inc(sines, 1)
                nc.scalar.activation(half[:, :, :], ang[:, :, :], ACT.Sin, scale=0.5).then_inc(sines, 1)


def rope(nc, link, x1, x2, cos, sin, a, b, shape):
    c, s = (t.to_broadcast(shape) for t in (cos, sin))
    nc_v = nc.vector
    link(nc_v.tensor_tensor(a, x1, s, ALU.mult))
    link(nc_v.tensor_tensor(b, x2, s, ALU.mult))
    link(nc_v.tensor_tensor(x1, x1, c, ALU.mult))
    link(nc_v.tensor_tensor(x2, x2, c, ALU.mult))
    link(nc_v.tensor_tensor(x1, x1, b, ALU.subtract))
    link(nc_v.tensor_tensor(x2, x2, a, ALU.add))


def project_between(env, pe, jobs, ht, tile_done, tile_stored, between):
    ps, stream = env.ps, env.stream
    for c, (u0, nu, _, w, *_) in enumerate(jobs):
        for n in range(u0, u0 + nu):
            w_hi, w_lo = stream.ready(pe, n)
            ks = KD // nu
            for t in range(T):
                if n == u0 and c:
                    pe.wait_ge(tile_stored, (c - 1) * T + t + 1)
                for j in range(ks):
                    k = (n - u0) * ks + j
                    lhs = tuple(x[:, k, t * P:(t + 1) * P] for x in ht)
                    last = product(env.nc, ps[:, t, 0:w], lhs, (w_hi[:, j], w_lo[:, j]), k == 0, k == KD - 1)
                if t == T - 1:
                    last.then_inc(stream.used, 1)
                elif n == u0 + nu - 1:
                    last.then_inc(tile_done, 1)
                between(n, t)


def store_between(env, act, jobs, proj, tile_done, tile_stored, tile_work, between):
    nc, ps, stream = env.nc, env.ps, env.stream
    stream.split_hi(act, 0)
    for c, (u0, nu, col, w, *_) in enumerate(jobs):
        for n in range(u0, u0 + nu):
            stream.split_hi(act, n + 1)
            for t in range(T):
                if n == u0 + nu - 1:
                    if t < T - 1:
                        act.wait_ge(tile_done, c * (T - 1) + t + 1)
                    else:
                        act.wait_ge(stream.used, n + 1)
                    nc.scalar.activation(proj[:, t, col:col + w], ps[:, t, 0:w], ACT.Copy).then_inc(tile_stored, 1)
                    tile_work(c, t)
                between(n, t)


def first_projection_units(w_in):
    units, jobs = [], []
    for a, b in ((MG, IN1), (0, MG)):
        n = -(-(b - a) // BANK)
        step = -(-(b - a) // (2 * n)) * 2
        for c in range(a, b, step):
            w = min(step, b - c)
            jobs.append((len(units), 2, c, w))
            units += weight_units(w_in[:, c:c + w], width=w)
    return units, jobs


def first_projection_stage(env, xt, jobs, proj, vec, convw, gates, dt, cols, cqt, xc, scratch):
    nc, ps, ident, stream = env.nc, env.ps, env.ident, env.stream
    names = ("tile_done", "tile_stored", "padded", "a_exp", "abs_ready", "exp_done", "ln_done", "gates_ready",
             "xc_turned", "xc_copied", "gates_turned", "gates_copied", "convolved", "silu_done", "x_turned", "x_copied",
             "mqk_turned", "mqk_copied", "squares_summed", "roots", "latent_scaled", "latent_turned", "latent_hi",
             "scanned", "turned_back", "vector_step")
    (tile_done, tile_stored, padded, a_exp, abs_ready, exp_done, ln_done, gates_ready, xc_turned, xc_copied,
     gates_turned, gates_copied, convolved, silu_done, x_turned, x_copied, mqk_turned, mqk_copied, squares_summed,
     roots, latent_scaled, latent_turned, latent_hi, scanned, turned_back, step) = (env.sem("proj1", n) for n in names)
    N = jobs[-1][0] + jobs[-1][1]
    early = [j[2] for j in jobs].index(0)
    U = jobs[early][0]
    latents = ((CQ, Q_RANK, V_Q), (CKV, KV_RANK, V_KV))
    NC = (Q_RANK + KV_RANK) // P
    XCH = SSD_H * SSD_P // P
    taps = [(j, c) for cs in (range(XCH), range(XCH, CC)) for j in range(CONV) for c in cs]
    xc_at = {(U, i): (2 * i, 2 * i + 1) for i in range(CC // 2)}
    gates_at = (U, 3)
    silu_at = {(U + 1, 3): (0, 1), (U + 3, 1): (2, 3), (U + 3, 2): (4, 5)}
    x_at = {(U + 2, 0): (0, 1), (U + 2, 1): (2, 3)}
    mqk_at = {(U + 4, 0): (0, 1), (U + 4, 1): (2, 3)}
    roots_at = (U + 3, 3)
    latent_at = {(U + 4, 2): 0, (U + 4, 3): 1, (U + 5, 0): 2}
    latent_bank = (6, 7, 4)
    R = slice(None, None, -1)

    def block(c):
        return turned_block(proj, XBC + c * P)

    def window(c, j):
        return xc[:, c, j:j + S].rearrange("p (t c) -> p t c", t=T)

    with ExitStack() as local:
        def tile(name, *shape):
            return local.enter_context(nc.sbuf_tensor(f"gates_{name}", [P, *shape], F32))
        pre, e, u, one, ln = (tile(n, T, 16) for n in ("pre", "e", "u", "one", "ln"))
        na = tile("na", 8)
        ss = tile("latent_ss", 2, T)
        ig, lf = scratch(0)[0:8], scratch(1)
        sums, c_, mx, m = ([scratch(2 + 2 * i + d)[0:16 if i == 0 else 8] for d in range(2)] for i in range(4))

        with nc.Block() as blk:
            @blk.sync
            def _(sp):
                stream.load(sp, N + 3)

            @blk.tensor
            def _(pe):
                def between(n, t):
                    for i in xc_at.get((n, t), ()):
                        pe.wait_ge(tile_stored, early * T)
                        if i >= 4:
                            pe.wait_ge(xc_copied, i - 3)
                        for s in range(T):
                            last = nc.tensor.transpose(ps[:, 4 + i % 4, s * P:(s + 1) * P],
                                                       proj[:, s, XBC + i * P:XBC + (i + 1) * P], ident)
                        last.then_inc(xc_turned, 1)
                    if (n, t) == gates_at:
                        pe.wait_ge(gates_ready, 1)
                        pe.wait_ge(xc_copied, 4)
                        for s in range(T):
                            nc.tensor.transpose(ps[0:8, 6, s * P:(s + 1) * P], gates[:, s, 0:8], ident)
                            last = nc.tensor.transpose(ps[0:16, 7, s * P:(s + 1) * P], gates[:, s, 8:24], ident)
                        last.then_inc(gates_turned, 1)
                    for s in x_at.get((n, t), ()):
                        pe.wait_ge(silu_done, XCH)
                        pe.wait_ge(xc_copied, CC)
                        if s >= 2:
                            pe.wait_ge(x_copied, s - 1)
                        for i in range(XCH):
                            last = nc.tensor.transpose(ps[:, 4 + s % 2, i * P:(i + 1) * P], block(i)[:, s, :], ident)
                        last.then_inc(x_turned, 1)
                    for i in mqk_at.get((n, t), ()):
                        pe.wait_ge(tile_stored, (early + 2) * T)
                        pe.wait_ge(x_copied, T)
                        if i >= 2:
                            pe.wait_ge(mqk_copied, i - 1)
                        for s in range(T):
                            last = nc.tensor.transpose(ps[:, 4 + i % 2, s * P:(s + 1) * P],
                                                       proj[:, s, MQ + i * P:MQ + (i + 1) * P], ident)
                        last.then_inc(mqk_turned, 1)
                    if (n, t) in latent_at:
                        i = latent_at[n, t]
                        pe.wait_ge(latent_scaled, 1)
                        pe.wait_ge(gates_copied, 1)
                        pe.wait_ge(mqk_copied, 4)
                        for s in range(T):
                            last = nc.tensor.transpose(ps[:, latent_bank[i], s * P:(s + 1) * P],
                                                       proj[:, s, i * P:(i + 1) * P], ident)
                        last.then_inc(latent_turned, 1)

                project_between(env, pe, jobs, xt, tile_done, tile_stored, between)
                pe.wait_ge(scanned, 1)
                for t in range(T):
                    for q, (src, rows, first) in enumerate(((c_, 8, 0), (mx, 8, 0), (m, 8, 0), (sums, 16, 8))):
                        for d in range(2):
                            o = q * 8 + d * 4
                            last = nc.tensor.matmul(ps[:, 5, t * 32 + o:t * 32 + o + 4],
                                                    src[d][:, t * P:(t + 1) * P],
                                                    ident[0:rows, first + d * 4:first + d * 4 + 4],
                                                    start=True, stop=True)
                last.then_inc(turned_back, 1)

            @blk.scalar
            def _(act):
                nc.scalar.activation(na[:, :], vec[:, V_AL:V_AL + 8], ACT.Exp).then_inc(a_exp, 1)

                def tile_work(c, t):
                    pass

                def between(n, t):
                    if (n, t) == (U, 0):
                        act.wait_ge(abs_ready, 1)
                        nc.scalar.activation(e[:, :, :], e[:, :, :], ACT.Exp, scale=-1.0).then_inc(exp_done, 1)
                        act.wait_ge(exp_done, 1)
                        nc.scalar.activation(ln[:, :, :], e[:, :, :], ACT.Ln, bias=1.0).then_inc(ln_done, 1)
                    for i in xc_at.get((n, t), ()):
                        act.wait_ge(xc_turned, i + 1)
                        nc.scalar.activation(xc[:, i, PAD:PAD + S], ps[:, 4 + i % 4, :], ACT.Copy).then_inc(xc_copied, 1)
                    for i in silu_at.get((n, t), ()):
                        act.wait_ge(convolved, taps.index((CONV - 1, i)) + 1)
                        nc.scalar.activation(block(i), block(i), ACT.Silu).then_inc(silu_done, 1)
                    for s in x_at.get((n, t), ()):
                        act.wait_ge(x_turned, s + 1)
                        nc.scalar.activation(proj[:, s, XBC:XBC + XCH * P], ps[:, 4 + s % 2, 0:XCH * P], ACT.Copy
                                             ).then_inc(x_copied, 1)
                    for i in mqk_at.get((n, t), ()):
                        act.wait_ge(mqk_turned, i + 1)
                        nc.scalar.activation(turned_block(proj, MQ + i * P),
                                             ps[:, 4 + i % 2, :].rearrange("p (t c) -> p t c", t=T), ACT.Copy
                                             ).then_inc(mqk_copied, 1)
                    if (n, t) == roots_at:
                        act.wait_ge(squares_summed, 1)
                        for i, (c, w, _) in enumerate(latents):
                            nc.scalar.activation(ss[:, i, :], ss[:, i, :], ACT.Sqrt, scale=1.0 / w, bias=env.eps6
                                                 ).then_inc(roots, 1)
                    if (n, t) in latent_at:
                        i = latent_at[n, t]
                        act.wait_ge(latent_turned, i + 1)
                        nc.scalar.activation(cqt[0][:, i, :], ps[:, latent_bank[i], :], ACT.Copy).then_inc(latent_hi, 1)

                store_between(env, act, jobs, proj, tile_done, tile_stored, tile_work, between)

            @blk.gpsimd
            def _(pool):
                nc.gpsimd.memset(xc[:, :, 0:PAD], 0.0).then_inc(padded, 1)
                nc.gpsimd.memset(xc[:, :, PAD + S:], 0.0).then_inc(padded, 1)
                for n in range(N + 1):
                    stream.split_lo(pool, n)

            @blk.vector
            def _(dve):
                link = Link(dve, step)
                v = nc.vector
                dve.wait_ge(tile_stored, early * T)
                for kind, dst in ((0, gates[:, :, 0:4]), (2, gates[:, :, 4:8]), (1, pre[:, :, 0:4]), (3, pre[:, :, 4:8])):
                    c = MG + kind * ML_H
                    bias = vec[:, V_GB + kind * ML_H:V_GB + (kind + 1) * ML_H].unsqueeze(1).to_broadcast([P, T, ML_H])
                    v.tensor_tensor(dst, proj[:, :, c:c + ML_H], bias, ALU.add)
                bias = vec[:, V_DTB:V_DTB + 8].unsqueeze(1).to_broadcast([P, T, 8])
                link(v.tensor_tensor(pre[:, :, 8:16], proj[:, :, SDT:SDT + 8], bias, ALU.add))
                v.scalar_tensor_tensor(out=e[:, :, :], in0=pre[:, :, :], scalar=-1.0, in1=pre[:, :, :],
                                       op0=ALU.mult, op1=ALU.max).then_inc(abs_ready, 1)
                dve.wait_ge(exp_done, 1)
                link(v.tensor_scalar(u[:, :, :], e[:, :, :], 1.0, None, ALU.add))
                link(v.tensor_scalar(u[:, :, :], u[:, :, :], -1.0, None, ALU.add))
                link(v.tensor_scalar(one[:, :, :], u[:, :, :], 0.0, None, ALU.is_equal))
                link(v.tensor_tensor(one[:, :, :], one[:, :, :], e[:, :, :], ALU.mult))
                link(v.tensor_scalar(u[:, :, :], u[:, :, :], 1e-30, None, ALU.max))
                link(v.reciprocal(u[:, :, :], u[:, :, :]))
                link(v.tensor_tensor(u[:, :, :], u[:, :, :], e[:, :, :], ALU.mult))
                dve.wait_ge(ln_done, 1)
                link(v.tensor_tensor(ln[:, :, :], ln[:, :, :], u[:, :, :], ALU.mult))
                link(v.tensor_tensor(ln[:, :, :], ln[:, :, :], one[:, :, :], ALU.add))
                v.scalar_tensor_tensor(out=gates[:, :, 8:16], in0=pre[:, :, 0:8], scalar=0.0,
                                       in1=ln[:, :, 0:8], op0=ALU.min, op1=ALU.subtract)
                link(v.scalar_tensor_tensor(out=dt, in0=pre[:, :, 8:16], scalar=0.0,
                                            in1=ln[:, :, 8:16], op0=ALU.max, op1=ALU.add))
                dve.wait_ge(a_exp, 1)
                a = na[:, :].unsqueeze(1).to_broadcast([P, T, 8])
                v.scalar_tensor_tensor(out=gates[:, :, 16:24], in0=dt, scalar=-1.0, in1=a, op0=ALU.mult, op1=ALU.mult
                                       ).then_inc(gates_ready, 1)
                dve.wait_ge(padded, 2)
                dve.wait_ge(xc_copied, CC)
                for j, c in taps:
                    w = convw[:, c, j:j + 1]
                    if j == 0:
                        ins = v.tensor_scalar(block(c), window(c, j), w, convw[:, c, CONV:CONV + 1], ALU.mult, ALU.add)
                    else:
                        dve.wait_ge(convolved, taps.index((j - 1, c)) + 1)
                        ins = v.scalar_tensor_tensor(out=block(c), in0=window(c, j), scalar=w, in1=block(c),
                                                     op0=ALU.mult, op1=ALU.add)
                    ins.then_inc(convolved, 1)
                dve.wait_ge(convolved, len(taps))
                dve.wait_ge(tile_stored, (early + 1) * T)
                for i, (c, w, _) in enumerate(latents):
                    for t in range(T):
                        src = proj[:, t, c:c + w]
                        last = v.tensor_tensor_reduce(out=xc[:, t, c:c + w], in0=src, in1=src, scale=1.0, scalar=0.0,
                                                      op0=ALU.mult, op1=ALU.add, accum_out=ss[:, i, t:t + 1])
                last.then_inc(squares_summed, 1)
                dve.wait_ge(gates_turned, 1)
                v.tensor_copy(ig, ps[0:8, 6, :])
                v.tensor_copy(lf, ps[0:16, 7, :]).then_inc(gates_copied, 1)
                dve.wait_ge(roots, 2)
                link(v.reciprocal(ss[:, :, :], ss[:, :, :]))
                for i, (c, w, g) in enumerate(latents):
                    for t in range(T):
                        x = proj[:, t, c:c + w]
                        last = v.scalar_tensor_tensor(out=x, in0=x, scalar=ss[:, i, t:t + 1], in1=vec[:, g:g + w],
                                                      op0=ALU.mult, op1=ALU.mult)
                last.then_inc(latent_scaled, 1)
                dve.wait_ge(gates_copied, 1)
                for d, w in ((0, slice(None)), (1, R)):
                    link(v.tensor_tensor_scan(sums[d][:, w], lf[:, w], lf[:, w], 0.0, ALU.add, ALU.bypass))
                    link(v.tensor_tensor(c_[d][:, :], ig[:, :], sums[d][0:8, :], ALU.subtract))
                    link(v.tensor_tensor_scan(mx[d][:, w], c_[d][:, w], c_[d][:, w], -3e38, ALU.max, ALU.bypass))
                    last = v.tensor_tensor(m[d][:, :], mx[d][:, :], sums[d][0:8, :], ALU.add)
                last.then_inc(scanned, 1)
                for i in range(NC):
                    dve.wait_ge(latent_hi, i + 1)
                    v.tensor_tensor(cqt[1][:, i, :], ps[:, latent_bank[i], :], cqt[0][:, i, :].bitcast(F32), ALU.subtract)
                dve.wait_ge(turned_back, 1)
                src = ps[:, 5, 0:T * 32].rearrange("p (t c) -> p t c", t=T)
                v.tensor_copy(cols[:, :, 0:24], src[:, :, 0:24])
                v.tensor_scalar(cols[:, :, 24:32], src[:, :, 24:32], -1.0, None, ALU.mult)


def turned_block(proj, col):
    return proj[:, :, col:col + P]


def mla_rope_stage(env, proj, qn, kn, cos, sin, a, b):
    nc = env.nc
    step = env.sem("mla_rope", "vector_step")
    H2 = ROPE // 2
    with nc.Block() as block:
        @block.vector
        def _(dve):
            link = Link(dve, step)
            rope(nc, link, qn[:, :, :, NOPE:NOPE + H2], qn[:, :, :, NOPE + H2:QK], cos.unsqueeze(2), sin.unsqueeze(2),
                 a, b, [P, T, MLA_H, H2])
            rope(nc, link, proj[:, :, KR:KR + H2], proj[:, :, KR + H2:KR + ROPE], cos, sin,
                 a[:, :, 0, :], b[:, :, 0, :], [P, T, H2])
            src = proj[:, :, KR:KR + ROPE].unsqueeze(2).to_broadcast([P, T, MLA_H, ROPE])
            nc.vector.tensor_copy(kn[:, :, :, NOPE:QK], src)


def decay_stage(env, units, cols, minus_cols):
    nc, ps, ident = env.nc, env.ps, env.ident
    N = len(units)
    names = ("products_ready", "row_ready", "gap_ready", "exp_done", "weighted", "masked", "out_ready",
             "out_stored", "vector_step")
    products_ready, row_ready, gap_ready, exp_done, weighted, masked, out_ready, out_stored, step = (
        env.sem("decay", n) for n in names)
    new_group = [i == 0 or units[i]["group"] != units[i - 1]["group"] for i in range(N)]

    def span(u, i):
        return (0, (i + 1) * P) if u["back"] else (i * P, S)

    with ExitStack() as local:
        gap = local.enter_context(nc.sbuf_tensor("decay_gap", [P, 2, T, S], F32))
        wq = local.enter_context(nc.sbuf_tensor("decay_weighted", [P, 2, T, S], F32))
        tmp = local.enter_context(nc.sbuf_tensor("decay_tmp", [P, T, 4], F32))
        with nc.Block() as block:
            @block.tensor
            def _(pe):
                for i in range(N + 2):
                    if i < N:
                        if i >= 2:
                            pe.wait_ge(gap_ready, T * (i - 1))
                        for t in range(T):
                            r = cols[:, t, units[i]["row"]:units[i]["row"] + 1].to_broadcast([P, P])
                            last = nc.tensor.matmul(ps[:, 4 + i % 2, t * P:(t + 1) * P], r, ident, start=True, stop=True)
                        last.then_inc(row_ready, 1)
                    if 1 <= i <= N and new_group[i - 1]:
                        u = units[i - 1]
                        for s in range(T):
                            if i > 1:
                                pe.wait_ge(weighted, T * (i - 2) + s + 1)
                            last = nc.tensor.matmul(ps[:, s, :].rearrange("p (t c) -> p t c", t=T), u["k"][:, s, :],
                                                    u["q"], start=True, stop=True)
                            last.then_inc(products_ready, 1)
                    if i >= 2:
                        j = i - 2
                        u = units[j]
                        pe.wait_ge(masked, T * (j + 1))
                        if j >= 2:
                            pe.wait_ge(out_stored, j - 1)
                        for t in range(T):
                            keys = range(t, T) if u["back"] else range(0, t + 1)
                            for s in keys:
                                last = nc.tensor.matmul(ps[:, 6 + j % 2, t * u["w"]:(t + 1) * u["w"]],
                                                        wq[:, j % 2, s, t * P:(t + 1) * P], u["v"](s),
                                                        start=(s == keys[0]), stop=(s == keys[-1]))
                        last.then_inc(out_ready, 1)

            @block.vector
            def _(dve):
                link = Link(dve, step)
                groups = 0
                for i in range(1, N + 2):
                    if i <= N:
                        j = i - 1
                        u = units[j]
                        groups += new_group[j]
                        if j >= 2:
                            dve.wait_ge(out_ready, j - 1)
                        for s in range(T):
                            a, b = span(u, s)
                            dve.wait_ge(products_ready, T * (groups - 1) + s + 1)
                            dve.wait_ge(exp_done, T * j + s + 1)
                            nc.vector.scalar_tensor_tensor(out=wq[:, j % 2, s, a:b], in0=ps[:, s, a:b],
                                                           scalar=u["weight"](s), in1=gap[:, j % 2, s, a:b],
                                                           op0=ALU.mult, op1=ALU.mult).then_inc(weighted, 1)
                    if i >= 2:
                        j = i - 2
                        dve.wait_ge(out_ready, j + 1)
                        out = ps[:, 6 + j % 2, 0:T * units[j]["w"]].rearrange("p (t c) -> p t c", t=T)
                        units[j]["store"](nc, link, out, tmp).then_inc(out_stored, 1)
                        dve.wait_ge(out_stored, j + 1)

            @block.scalar
            def _(act):
                for i in range(N):
                    act.wait_ge(row_ready, i + 1)
                    if i >= 2:
                        act.wait_ge(weighted, T * (i - 1))
                    for s in range(T):
                        a, b = span(units[i], s)
                        col = units[i]["col"]
                        nc.scalar.activation(gap[:, i % 2, s, a:b], ps[:, 4 + i % 2, a:b], ACT.Relu,
                                             bias=minus_cols[:, s, col:col + 1]).then_inc(gap_ready, 1)
                    for s in range(T):
                        a, b = span(units[i], s)
                        act.wait_ge(gap_ready, T * i + s + 1)
                        nc.scalar.activation(gap[:, i % 2, s, a:b], gap[:, i % 2, s, a:b], ACT.Exp, scale=-1.0
                                             ).then_inc(exp_done, 1)

            @block.gpsimd
            def _(pool):
                for i in range(N):
                    for s in range(T):
                        pool.wait_ge(weighted, T * i + s + 1)
                        d = wq[:, i % 2, s, s * P:(s + 1) * P]
                        nc.gpsimd.tensor_tensor(d, d, env.keep_le if units[i]["back"] else env.keep_ge, ALU.mult
                                                ).then_inc(masked, 1)


def decay_units(proj, cols, dt, vx, h_sum, y_ssd):
    units = []
    for h in range(ML_H):
        base, chunk = (h % 2) * ML_D, h // 2
        for d in range(2):
            k = d * ML_H + h

            def store(nc, link, out, tmp, h=h, d=d, k=k):
                v = nc.vector
                den = out[:, :, ML_D]
                link(v.tensor_scalar(tmp[:, :, 0], den, -1.0, None, ALU.mult))
                link(v.tensor_tensor(tmp[:, :, 0], tmp[:, :, 0], den, ALU.max))
                link(v.tensor_tensor(tmp[:, :, 0], tmp[:, :, 0], cols[:, :, 16 + k], ALU.max))
                link(v.reciprocal(tmp[:, :, 0], tmp[:, :, 0]))
                for t in range(T):
                    dst = h_sum[:, t, h * ML_D:(h + 1) * ML_D]
                    if d == 0:
                        last = v.tensor_scalar(dst, out[:, t, 0:ML_D], tmp[:, t, 0:1], None, ALU.mult)
                    else:
                        last = v.scalar_tensor_tensor(out=dst, in0=out[:, t, 0:ML_D], scalar=tmp[:, t, 0:1],
                                                      in1=dst, op0=ALU.mult, op1=ALU.add)
                return last

            units.append(dict(group=("m", h), k=turned_block(proj, MK + chunk * P)[base:base + ML_D],
                              q=turned_block(proj, MQ + chunk * P)[base:base + ML_D],
                              weight=lambda s: ML_D ** -0.5, row=8 + k, col=k, back=d == 1,
                              v=lambda s, h=h: vx[:, s, h, :], w=ML_D + 1, store=store))
    for h in range(SSD_H):
        g = h // (SSD_H // SSD_G)
        for d in range(2):
            k = d * SSD_H + h

            def store(nc, link, out, tmp, h=h, d=d):
                dst = y_ssd[:, :, h * SSD_P:(h + 1) * SSD_P]
                if d == 0:
                    return nc.vector.tensor_copy(dst, out)
                return nc.vector.tensor_tensor(dst, out, dst, ALU.add)

            units.append(dict(group=("s", g), k=turned_block(proj, XBC + (2 + g) * P),
                              q=turned_block(proj, XBC + (2 + SSD_G + g) * P),
                              weight=lambda s, k=k: dt[:, s, k:k + 1], row=24 + k, col=24 + k, back=d == 1,
                              v=lambda s, h=h: proj[:, s, XBC + h * SSD_P:XBC + (h + 1) * SSD_P], w=SSD_P, store=store))
    return units


def values_stage(env, proj, vx, cols, minus_cols):
    nc = env.nc
    negated = env.sem("values", "negated")
    with nc.Block() as block:
        @block.scalar
        def _(act):
            act.wait_ge(negated, 1)
            nc.scalar.activation(cols[:, :, 16:24], cols[:, :, 16:24], ACT.Exp, scale=-1.0)
            nc.scalar.activation(vx[:, 3, :, 0:ML_D], by_head(proj[:, 3, MV:MV + ML_H * ML_D], ML_H), ACT.Copy)

        @block.vector
        def _(dve):
            nc.vector.tensor_scalar(minus_cols[:, :, :], cols[:, :, :], -1.0, None, ALU.mult).then_inc(negated, 1)
            for t in range(2):
                nc.vector.tensor_copy(vx[:, t, :, 0:ML_D], by_head(proj[:, t, MV:MV + ML_H * ML_D], ML_H))

        @block.gpsimd
        def _(pool):
            nc.gpsimd.tensor_copy(vx[:, 2, :, 0:ML_D], by_head(proj[:, 2, MV:MV + ML_H * ML_D], ML_H))
            nc.gpsimd.memset(vx[:, :, :, ML_D:ML_D + 1], 1.0)


def mixer_end_stage(env, proj, vec, h_sum, y_ssd):
    nc = env.nc
    names = ("silu_done", "sigmoid_done", "ssd_gated", "squares_summed", "ssd_root", "ssd_inverse", "times_gain",
             "variances", "root", "vector_step", "pool_step")
    silu, sig, gated, squared, ssd_root, ssd_inverse, times_gain, variances, root, step, pool_step = (
        env.sem("mixer_end", n) for n in names)
    ME, GE = ML_H, SSD_G
    W = ML_H * ML_D
    with ExitStack() as local:
        sq = local.enter_context(nc.sbuf_tensor("end_sq", [P, T, W], F32))
        ssd_sq = local.enter_context(nc.sbuf_tensor("end_ssd_sq", [P, T, W], F32))
        mean = local.enter_context(nc.sbuf_tensor("end_mean", [P, T * ME], F32))
        var = local.enter_context(nc.sbuf_tensor("end_var", [P, T * ME], F32))
        ss = local.enter_context(nc.sbuf_tensor("end_ss", [P, T * GE], F32))
        o = local.enter_context(nc.sbuf_tensor("end_o", [P, T, W], F32))
        z = local.enter_context(nc.sbuf_tensor("end_z", [P, T, W], F32))

        def flat(x, w):
            return x[:, :, :].rearrange("p t (h c) -> p t h c", c=w)

        def stat(a, w):
            a = a[:, :].rearrange("p (t h) -> p t h", t=T)
            return a if w is None else a.unsqueeze(3).to_broadcast([P, T, a.shape[2], w])

        def row(c):
            return vec[:, c:c + W].unsqueeze(1).to_broadcast([P, T, W])

        with nc.Block() as block:
            @block.scalar
            def _(act):
                nc.scalar.activation(z[:, :, :], proj[:, :, SZ:SZ + W], ACT.Silu).then_inc(silu, 1)
                nc.scalar.activation(o[:, :, :], proj[:, :, MO:MO + W], ACT.Sigmoid).then_inc(sig, 1)
                act.wait_ge(gated, 1)
                for t in range(T):
                    for g in range(GE):
                        c = slice(g * W // GE, (g + 1) * W // GE)
                        nc.scalar.activation(ssd_sq[:, t, c], y_ssd[:, t, c], ACT.Square,
                                             accum_out=ss[:, t * GE + g:t * GE + g + 1]).then_inc(squared, 1)
                act.wait_ge(squared, T * GE)
                nc.scalar.activation(ss[:, :], ss[:, :], ACT.Sqrt, scale=SSD_G / W, bias=env.eps6).then_inc(ssd_root, 1)
                act.wait_ge(variances, 1)
                nc.scalar.activation(var[:, :], var[:, :], ACT.Sqrt, scale=1.0 / ML_D, bias=env.eps5).then_inc(root, 1)

            @block.gpsimd
            def _(pool):
                link = Link(pool, pool_step)
                pool.wait_ge(sig, 1)
                nc.gpsimd.tensor_tensor(o[:, :, :], o[:, :, :], row(V_MN), ALU.mult).then_inc(times_gain, 1)
                pool.wait_ge(ssd_inverse, 1)
                yf = flat(y_ssd, W // GE)
                link(nc.gpsimd.tensor_tensor(yf, yf, stat(ss, W // GE), ALU.mult))
                nc.gpsimd.tensor_tensor(y_ssd[:, :, :], y_ssd[:, :, :], row(V_SN), ALU.mult)

            @block.vector
            def _(dve):
                link = Link(dve, step)
                v = nc.vector
                for h in range(SSD_H):
                    c = slice(h * SSD_P, (h + 1) * SSD_P)
                    last = v.scalar_tensor_tensor(out=y_ssd[:, :, c], in0=proj[:, :, XBC + h * SSD_P:XBC + (h + 1) * SSD_P],
                                                  scalar=vec[:, V_SD + h:V_SD + h + 1], in1=y_ssd[:, :, c],
                                                  op0=ALU.mult, op1=ALU.add)
                link(last)
                dve.wait_ge(silu, 1)
                v.tensor_tensor(y_ssd[:, :, :], y_ssd[:, :, :], z[:, :, :], ALU.mult).then_inc(gated, 1)
                hf, sf = flat(h_sum, ML_D), flat(sq, ML_D)
                link(v.reduce_sum(stat(mean, None), hf, AX))
                link(v.tensor_scalar(mean[:, :], mean[:, :], 1.0 / ML_D, None, ALU.mult))
                link(v.tensor_tensor(hf, hf, stat(mean, ML_D), ALU.subtract))
                link(v.tensor_tensor(sf, hf, hf, ALU.mult))
                v.reduce_sum(stat(var, None), sf, AX).then_inc(variances, 1)
                dve.wait_ge(ssd_root, 1)
                v.reciprocal(ss[:, :], ss[:, :]).then_inc(ssd_inverse, 1)
                dve.wait_ge(times_gain, 1)
                link(v.tensor_tensor(h_sum[:, :, :], h_sum[:, :, :], o[:, :, :], ALU.mult))
                dve.wait_ge(root, 1)
                link(v.reciprocal(var[:, :], var[:, :]))
                v.tensor_tensor(hf, hf, stat(var, ML_D), ALU.mult)


def router_stage(env, xt, router_w, vec, combine, oh, rank, passes, x, xp):
    nc, ps = env.nc, env.ps
    names = ("weights_loaded", "logits_ready", "shifted", "exp_done", "groups_chosen", "ranked", "x_hi", "x_lo",
             "vector_step")
    loaded, logits_ready, shifted, exp_done, chosen, ranked, x_hi, x_lo, step = (env.sem("router", n) for n in names)
    with ExitStack() as local:
        def tile(name, *shape):
            return local.enter_context(nc.sbuf_tensor(f"router_{name}", [P, *shape], F32))
        wr = tile("w", KD, NR)
        lg, e, acc = tile("logits", T, NR), tile("e", T, GROUPS), tile("acc", T, PER_GROUP)
        top, eq, rem = tile("top", T, 1), tile("eq", T, 4), tile("rem", T, 1)
        most, more = tile("most", 1), tile("more", 1)
        first, second, gp, tmp = tile("first", T, 4), tile("second", T, 4), tile("gp", T, 1), tile("tmp", T, 4)
        with nc.Block() as block:
            @block.sync
            def _(sp):
                sp.dma_start(wr[:, :, :], router_w.rearrange("(k p) c -> p k c", p=P),
                             allow_slow_non_contiguous=True).then_inc(loaded, 16)

            @block.tensor
            def _(pe):
                pe.wait_ge(loaded, 16)
                for t in range(T):
                    for k in range(KD):
                        last = nc.tensor.matmul(ps[:, 0, t * NR:(t + 1) * NR], xt[:, k, t * P:(t + 1) * P],
                                                wr[:, k, :], start=(k == 0), stop=(k == KD - 1))
                last.then_inc(logits_ready, 1)
                pe.wait_ge(chosen, 1)
                for t in range(T):
                    for b in range(t + 1):
                        nc.tensor.matmul(ps[:, 1, t * 4:(t + 1) * 4], env.keep_ge if b == t else env.ones,
                                         oh[:, b, :], start=(b == 0), stop=(b == t))
                for b in range(T):
                    last = nc.tensor.matmul(ps[:, 1, T * 4:T * 4 + 4], env.ones, oh[:, b, :],
                                            start=(b == 0), stop=(b == T - 1))
                last.then_inc(ranked, 1)

            @block.vector
            def _(dve):
                link = Link(dve, step)
                v = nc.vector

                def wide(x):
                    return x[:, :, :].to_broadcast([P, T, 4])

                def first_of_max(x, out):
                    link(v.reduce_max(top[:, :, 0], x, AX))
                    link(v.tensor_tensor(eq[:, :, :], x, wide(top), ALU.is_equal))
                    link(v.tensor_scalar(rem[:, :, :], top[:, :, :], 0.0, 1.0, ALU.mult, ALU.add))
                    for j in range(4):
                        link(v.tensor_tensor(out[:, :, j:j + 1], eq[:, :, j:j + 1], rem[:, :, :], ALU.mult))
                        if j < 3:
                            link(v.tensor_tensor(rem[:, :, :], rem[:, :, :], out[:, :, j:j + 1], ALU.subtract))

                dve.wait_ge(logits_ready, 1)
                src = ps[:, 0, 0:T * NR].rearrange("p (t c) -> p t c", t=T)
                bias = vec[:, V_RB:V_RB + NR].unsqueeze(1).to_broadcast([P, T, NR])
                link(v.tensor_tensor(lg[:, :, :], src, bias, ALU.add))
                first_of_max(lg[:, :, 0:GROUPS], oh)
                v.tensor_copy(eq[:, :, :], oh[:, :, :]).then_inc(chosen, 1)
                v.tensor_tensor(e[:, :, :], lg[:, :, 0:GROUPS], wide(top), ALU.subtract).then_inc(shifted, 1)
                dve.wait_ge(exp_done, 1)
                link(v.reduce_sum(gp[:, :, 0], e[:, :, :], AX))
                link(v.reciprocal(gp[:, :, :], gp[:, :, :]))
                for g in range(GROUPS):
                    c = GROUPS + g * PER_GROUP
                    dst = acc if g == 0 else tmp
                    link(v.tensor_tensor(dst[:, :, :], lg[:, :, c:c + PER_GROUP], oh[:, :, g:g + 1].to_broadcast([P, T, 4]),
                                         ALU.mult))
                    if g:
                        link(v.tensor_tensor(acc[:, :, :], acc[:, :, :], tmp[:, :, :], ALU.add))
                first_of_max(acc[:, :, :], first)
                v.tensor_tensor(e[:, :, :], acc[:, :, :], wide(top), ALU.subtract).then_inc(shifted, 1)
                link(v.scalar_tensor_tensor(out=tmp[:, :, :], in0=first[:, :, :], scalar=-3e38, in1=acc[:, :, :],
                                            op0=ALU.mult, op1=ALU.add))
                dve.wait_ge(shifted, 2)
                first_of_max(tmp[:, :, :], second)
                dve.wait_ge(exp_done, 2)
                link(v.tensor_tensor(first[:, :, :], first[:, :, :], second[:, :, :], ALU.add))
                link(v.tensor_tensor(e[:, :, :], e[:, :, :], first[:, :, :], ALU.mult))
                link(v.reduce_sum(rem[:, :, 0], e[:, :, :], AX))
                link(v.reciprocal(rem[:, :, :], rem[:, :, :]))
                link(v.tensor_tensor(rem[:, :, :], rem[:, :, :], gp[:, :, :], ALU.mult))
                link(v.tensor_tensor(e[:, :, :], e[:, :, :], wide(rem), ALU.mult))
                for g in range(GROUPS):
                    last = v.tensor_tensor(lg[:, :, g * PER_GROUP:(g + 1) * PER_GROUP], e[:, :, :],
                                           oh[:, :, g:g + 1].to_broadcast([P, T, 4]), ALU.mult)
                link(last)
                link(v.tensor_copy(combine[0][:, :, :], lg[:, :, 0:EXPERTS]))
                v.tensor_tensor(combine[1][:, :, :], lg[:, :, 0:EXPERTS], combine[0][:, :, :].bitcast(F32), ALU.subtract)
                dve.wait_ge(ranked, 1)
                v.tensor_copy(rank[:, :, :], ps[:, 1, 0:T * 4].rearrange("p (t g) -> p t g", t=T))
                link(v.reduce_max(most[:, :], ps[:, 1, T * 4:T * 4 + 4], AX))
                link(v.tensor_scalar(more[:, :], most[:, :], float(2 * SLOTS), None, ALU.is_gt))
                link(v.tensor_scalar(most[:, :], most[:, :], float(SLOTS), 1.0, ALU.is_gt, ALU.add))
                v.tensor_tensor(passes[:, :], most[:, :], more[:, :], ALU.add)

            @block.scalar
            def _(act):
                for t in range(T):
                    nc.scalar.activation(xp[0][:, t, :], x[:, t, :], ACT.Copy).then_inc(x_hi, 1)
                for n in range(2):
                    act.wait_ge(shifted, n + 1)
                    nc.scalar.activation(e[:, :, :], e[:, :, :], ACT.Exp).then_inc(exp_done, 1)
                for t in range(T):
                    act.wait_ge(x_lo, t + 1)
                    nc.scalar.activation(x[:, t, :], x[:, t, :], ACT.Copy, scale=ALPHA)

            @block.gpsimd
            def _(pool):
                for t in range(T):
                    pool.wait_ge(x_hi, t + 1)
                    nc.gpsimd.tensor_tensor(xp[1][:, t, :], x[:, t, :], xp[0][:, t, :].bitcast(F32), ALU.subtract
                                            ).then_inc(x_lo, 1)


def places_stage(env, oh, rank, take, put):
    nc, ps, ident = env.nc, env.ps, env.ident
    placed, turned = env.sem("places", "placed"), env.sem("places", "turned")
    jobs = [(g, st) for g in range(GROUPS) for st in range(2)]
    with nc.Block() as block:
        @block.sync
        def _(sp):
            env.stream.load(sp, env.stream.RAW)

        @block.vector
        def _(dve):
            for g in range(GROUPS):
                for t in range(T):
                    last = nc.vector.tensor_scalar(take[:, g, t, :], env.slot_numbers, rank[:, t, g:g + 1],
                                                   oh[:, t, g:g + 1], ALU.is_equal, ALU.mult)
                last.then_inc(placed, 1)
            dve.wait_ge(placed, GROUPS)
            nc.vector.tensor_scalar(rank[:, :, :], rank[:, :, :], -float(SLOTS), None, ALU.add)

        @block.tensor
        def _(pe):
            for i, (g, st) in enumerate(jobs):
                pe.wait_ge(placed, g + 1)
                w = min(P, SLOTS - st * P)
                for t in range(T):
                    src = take[:, g, t, st * P:st * P + w].bitcast(F32)
                    last = nc.tensor.transpose(ps[0:w, i, t * P:(t + 1) * P], src, ident)
                last.then_inc(turned, 1)

        @block.scalar
        def _(act):
            for i, (g, st) in enumerate(jobs):
                w = min(P, SLOTS - st * P)
                act.wait_ge(turned, i + 1)
                nc.scalar.activation(put[0:w, g, st, :], ps[0:w, i, :], ACT.Copy)

def expert_units(at):
    units, kinds = [], []
    for g in range(GROUPS):
        for kind, e in (("gate", 0), ("up", 0), ("gate", 1), ("up", 1), ("down", 0), ("gate", 2), ("up", 2),
                        ("down", 1), ("gate", 3), ("up", 3), ("down", 2), ("down", 3)):
            w = at(f"expert_w_{kind}")[g * PER_GROUP + e]
            units.append(w.rearrange("(k p) f -> p k f", p=P))
            kinds.append((kind, g, e))
    return units, kinds


def expert_stage(env, x, xp, take, put, combine, kinds):
    nc, ps, stream = env.nc, env.ps, env.stream
    names = ("gathered", "xg_hi", "xg_lo", "rows_ready", "rows_copied", "gate_half", "gate_added", "silu_done", "up_half", "up_added",
             "times_up", "times_combine", "hidden_hi", "hidden_lo", "out_hi", "out_lo", "scattered", "added", "pad_zero")
    (gathered, xg_hi_done, xg_lo_done, rows_ready, rows_copied, gate_half, gate_added, silu_done, up_half, up_added, times_up,
     times_combine, hidden_hi, hidden_lo, out_hi, out_lo, scattered, added, pad_zero) = (
        env.sem("experts", n) for n in names)
    FC = F_CH // P
    E, N = PER_GROUP, len(kinds)
    per = N // GROUPS
    outs = [(st, half) for st in range(2) for half in range(2)]
    sums = [(tt, half) for tt in range(T) for half in range(2)]
    with ExitStack() as local:
        def pair(name, *shape):
            return tuple(local.enter_context(nc.sbuf_tensor(f"expert_{name}_{n}", [P, *shape], F32R)) for n in ("hi", "lo"))
        hidden, og = pair("hidden", E * FC, 2 * P), pair("out", 2, D)
        xg = local.enter_context(nc.sbuf_tensor("expert_xg", [P, KD, 2, SLOTS], F32R))
        gate = local.enter_context(nc.sbuf_tensor("expert_gate", [P, FC, SLOTS], F32))
        up = local.enter_context(nc.sbuf_tensor("expert_up", [P, FC, SLOTS], F32))
        rows = local.enter_context(nc.sbuf_tensor("expert_rows", [P, E, SLOTS], F32))

        def two(b):
            return ps[:, b, 0:2 * SLOTS].rearrange("p (k s) -> p k s", k=2)

        def halves(b):
            return ps[:, b:b + FC, 0:SLOTS], ps[:, b:b + FC, SLOTS:2 * SLOTS]

        with nc.Block() as block:
            @block.sync
            def _(sp):
                stream.load(sp, N)

            @block.gpsimd
            def _(pool):
                for h in hidden:
                    nc.gpsimd.memset(h[:, :, SLOTS:2 * P].bitcast(F32), 0.0).then_inc(pad_zero, 1)

            @block.tensor
            def _(pe):
                def gather(g):
                    if g:
                        pe.wait_ge(gate_added, E * g)
                        pe.wait_ge(up_added, E * g)
                    if g > 1:
                        pe.wait_ge(added, len(sums) * (g - 1))
                    for b in range(4):
                        for k in range(2 * b, 2 * b + 2):
                            for t in range(T):
                                a = tuple(h[:, t, k * P:(k + 1) * P] for h in xp)
                                last = exact_product(nc, two(b)[:, k % 2, :], a, take[:, g, t, :], t == 0, t == T - 1)
                        last.then_inc(gathered, 1)

                def scatter(g):
                    pe.wait_ge(out_lo, 4 * (g + 1))
                    for i, (tt, half) in enumerate(sums):
                        b = i % 4
                        if i >= 4:
                            pe.wait_ge(added, len(sums) * g + i - 3)
                        elif g < GROUPS - 1:
                            pe.wait_ge(xg_lo_done, 4 * (g + 1) + b + 1)
                        elif i == 0:
                            pe.wait_ge(added, len(sums) * g)
                        for st in range(2):
                            w = min(P, SLOTS - st * P)
                            a = put[0:w, g, st, tt * P:(tt + 1) * P]
                            o = tuple(h[0:w, st, half * BANK:(half + 1) * BANK] for h in og)
                            last = exact_product(nc, ps[:, b, :], a, o, st == 0, st == 1)
                        last.then_inc(scattered, 1)

                gather(0)
                pe.wait_ge(pad_zero, 2)
                for n, (kind, g, e) in enumerate(kinds):
                    ex = g * E + e
                    if kind == "gate":
                        if e == 0:
                            pe.wait_ge(xg_lo_done, 4 * (g + 1))
                            if g:
                                pe.wait_ge(added, len(sums) * g)
                            for c in range(E):
                                for t in range(T):
                                    w = tuple(h[:, t, ex + c:ex + c + 1].to_broadcast([P, P]) for h in combine)
                                    last = exact_product(nc, two(2 + c // 2)[:, c % 2, :], w, take[:, g, t, :],
                                                         t == 0, t == T - 1)
                                if c % 2:
                                    last.then_inc(rows_ready, 1)
                        if ex:
                            pe.wait_ge(gate_added, ex)
                    if kind == "up":
                        if ex:
                            pe.wait_ge(up_added, ex)
                        if e == 0:
                            pe.wait_ge(rows_copied, 2 * (g + 1))
                    w_hi, w_lo = stream.ready(pe, n)
                    if kind == "down":
                        pe.wait_ge(hidden_lo, ex + 1)
                        if e == 0 and g:
                            pe.wait_ge(out_lo, 4 * g)
                        for i, (st, half) in enumerate(outs):
                            cols = slice(half * BANK, (half + 1) * BANK)
                            for f in range(FC):
                                a = tuple(h[:, e * FC + f, st * P:(st + 1) * P] for h in hidden)
                                last = product(nc, ps[:, 4 + i, :], a, (w_hi[:, f, cols], w_lo[:, f, cols]),
                                               e == 0 and f == 0, e == E - 1 and f == FC - 1)
                    else:
                        for f in range(FC):
                            cols = slice(f * P, (f + 1) * P)
                            bank = (2 if kind == "up" else 0) + f
                            for k in range(KD):
                                def lo():
                                    nc.tensor.matmul(ps[:, bank, 0:SLOTS], w_lo[:, k, cols], xg[:, k, 0, :],
                                                     start=False, stop=False)
                                if k:
                                    lo()
                                last = nc.tensor.matmul(ps[:, bank, 0:2 * SLOTS], w_hi[:, k, cols],
                                                        xg[:, k, :, :].rearrange("p h s -> p (h s)"),
                                                        start=(k == 0), stop=(k == KD - 1))
                                if not k:
                                    lo()
                    last.then_inc(stream.used, 1)
                    if (kind, e) == ("down", E - 1):
                        if g < GROUPS - 1:
                            gather(g + 1)
                        scatter(g)

            @block.scalar
            def _(act):
                def gathered_hi(g):
                    for b in range(4):
                        act.wait_ge(gathered, 4 * g + b + 1)
                        nc.scalar.activation(xg[:, 2 * b:2 * b + 2, 0, :], two(b), ACT.Copy).then_inc(xg_hi_done, 1)

                for n in range(N + 1):
                    if n < N:
                        stream.split_hi(act, n)
                    if n == 1:
                        gathered_hi(0)
                    if n % per == 1:
                        g = n // per
                        if g:
                            act.wait_ge(times_combine, E * g)
                        for i in range(2):
                            act.wait_ge(rows_ready, 2 * g + i + 1)
                            nc.scalar.activation(rows[:, 2 * i:2 * i + 2, :], two(2 + i), ACT.Copy
                                                 ).then_inc(rows_copied, 1)
                    if n >= 2 and kinds[n - 2][0] != "down":
                        kind, g, e = kinds[n - 2]
                        ex = g * E + e
                        if kind == "gate":
                            act.wait_ge(gate_added, ex + 1)
                            nc.scalar.activation(gate[:, :, :], gate[:, :, :], ACT.Silu).then_inc(silu_done, 1)
                        else:
                            act.wait_ge(times_combine, ex + 1)
                            nc.scalar.activation(hidden[0][:, e * FC:(e + 1) * FC, 0:SLOTS], gate[:, :, :], ACT.Copy
                                                 ).then_inc(hidden_hi, 1)
                    if n and n % per == 0:
                        g = n // per - 1
                        act.wait_ge(stream.used, n)
                        if g:
                            act.wait_ge(scattered, len(sums) * g)
                        for i, (st, half) in enumerate(outs):
                            nc.scalar.activation(og[0][:, st, half * BANK:(half + 1) * BANK], ps[:, 4 + i, :], ACT.Copy
                                                 ).then_inc(out_hi, 1)
                        if g < GROUPS - 1:
                            gathered_hi(g + 1)

            @block.vector
            def _(dve):
                v = nc.vector

                def gathered_lo(g):
                    for b in range(4):
                        dve.wait_ge(xg_hi_done, 4 * g + b + 1)
                        ks = slice(2 * b, 2 * b + 2)
                        v.tensor_tensor(xg[:, ks, 1, :], two(b), xg[:, ks, 0, :].bitcast(F32), ALU.subtract
                                        ).then_inc(xg_lo_done, 1)

                for n in range(N + 1):
                    kind, g, e = kinds[n - 2] if n >= 2 else (None, 0, 0)
                    ex = g * E + e
                    if kind == "gate":
                        dve.wait_ge(stream.used, n - 1)
                        if ex:
                            dve.wait_ge(hidden_lo, ex)
                        v.tensor_copy(gate[:, :, :], halves(0)[0]).then_inc(gate_half, 1)
                        dve.wait_ge(gate_half, ex + 1)
                        v.tensor_tensor(gate[:, :, :], gate[:, :, :], halves(0)[1], ALU.add).then_inc(gate_added, 1)
                    if kind == "up":
                        dve.wait_ge(stream.used, n - 1)
                        dve.wait_ge(rows_copied, 2 * (g + 1))
                        if ex:
                            dve.wait_ge(times_up, ex)
                        v.tensor_copy(up[:, :, :], halves(2)[0]).then_inc(up_half, 1)
                        dve.wait_ge(up_half, ex + 1)
                        v.tensor_tensor(up[:, :, :], up[:, :, :], halves(2)[1], ALU.add).then_inc(up_added, 1)
                        dve.wait_ge(up_added, ex + 1)
                        dve.wait_ge(silu_done, ex + 1)
                        v.tensor_tensor(gate[:, :, :], gate[:, :, :], up[:, :, :], ALU.mult).then_inc(times_up, 1)
                        dve.wait_ge(times_up, ex + 1)
                        v.tensor_tensor(gate[:, :, :], gate[:, :, :],
                                        rows[:, e, :].unsqueeze(1).to_broadcast([P, FC, SLOTS]), ALU.mult
                                        ).then_inc(times_combine, 1)
                    if n < N:
                        stream.split_lo(dve, n)
                    if n == 1:
                        gathered_lo(0)
                    if kind == "up":
                        dve.wait_ge(hidden_hi, ex + 1)
                        v.tensor_tensor(hidden[1][:, e * FC:(e + 1) * FC, 0:SLOTS], gate[:, :, :],
                                        hidden[0][:, e * FC:(e + 1) * FC, 0:SLOTS].bitcast(F32), ALU.subtract
                                        ).then_inc(hidden_lo, 1)
                    if n and n % per == 0:
                        g = n // per - 1
                        for i, (st, half) in enumerate(outs):
                            cols = slice(half * BANK, (half + 1) * BANK)
                            dve.wait_ge(out_hi, 4 * g + i + 1)
                            v.tensor_tensor(og[1][:, st, cols], ps[:, 4 + i, :], og[0][:, st, cols].bitcast(F32),
                                            ALU.subtract).then_inc(out_lo, 1)
                        if g < GROUPS - 1:
                            gathered_lo(g + 1)
                        for i, (tt, half) in enumerate(sums):
                            d = x[:, tt, half * BANK:(half + 1) * BANK]
                            dve.wait_ge(scattered, len(sums) * g + i + 1)
                            v.tensor_tensor(d, d, ps[:, i % 4, :], ALU.add).then_inc(added, 1)


def pair_tile(nc, ctx, name, *shape):
    return tuple(ctx.enter_context(nc.sbuf_tensor(f"{name}_{n}", [P, *shape], F32R)) for n in ("hi", "lo"))


def chunks_of(pair, n=KD):
    return [(pair[0][:, k, :], pair[1][:, k, :]) for k in range(n)]


def first_mixers(env, l, dram, x, vec, convw, cos, sin):
    nc = env.nc
    at = layer_of(dram, l)
    KP = [range(0, 4), range(4, 8)]
    units, jobs = first_projection_units(at("w_in"))
    first_uq = len(units)
    units += weight_units(at("mla_w_uq"), width=4 * QK) + weight_units(at("mla_w_ukv"))
    first_out = len(units)
    env.stream = WeightStream(env, units + weight_units(at("w_out")))

    with ExitStack() as mix:
        def tile(ctx, name, *shape):
            return ctx.enter_context(nc.sbuf_tensor(name, [P, *shape], F32))
        y = tile(mix, "y1", T, D)
        proj = tile(mix, "proj1", T, IN1)
        load_small_stage(env, "small1", [(vec[:, :], at("vec1").to_broadcast([P, NV1])),
                                         (convw[:, :, :], at("conv1"))], env.stream.RAW)
        gates, dt, cols = tile(mix, "gates", T, 24), tile(mix, "dt", T, 8), tile(mix, "cols", T, 32)
        with ExitStack() as early:
            NC = (Q_RANK + KV_RANK) // P
            cqt = pair_tile(nc, early, "cqt", NC, S)
            shared = tile(early, "shared", 10 * S)
            o = CC * (S + 2 * PAD)
            xc = shared[:, 0:o].rearrange("p (c s) -> p c s", c=CC)
            spare = shared[:, o:o + 2 * S].rearrange("p (i s) -> p i s", i=2)

            def scratch(i):
                return y[0:16, i // 2, (i % 2) * S:(i % 2 + 1) * S] if i < 2 * T else spare[0:16, i - 2 * T, :]
            with ExitStack() as local:
                xt = pair_tile(nc, local, "xt", KD, S)
                transpose_stage(env, "x_t", pair_transposes(lambda t, k: x[:, t, k * P:(k + 1) * P], xt), 0)
                first_projection_stage(env, xt, jobs, proj, vec, convw, gates, dt[:, :, :], cols, cqt, xc, scratch)
            mla_part(env, early, proj, y, shared, cqt, first_uq, first_out, cos, sin)

        with ExitStack() as rec:
            vx = tile(rec, "vx", T, ML_H, ML_D + 1)
            minus_cols = tile(rec, "minus_cols", T, 32)
            values_stage(env, proj, vx, cols, minus_cols)
            h_sum, y_ssd = y[:, :, 512:768], y[:, :, 768:1024]
            decay_stage(env, decay_units(proj, cols, dt, vx, h_sum, y_ssd), cols, minus_cols)
            mixer_end_stage(env, proj, vec, h_sum, y_ssd)

        with ExitStack() as local:
            yt = pair_tile(nc, local, "yt", KD, S)
            transpose_stage(env, "y_t", pair_transposes(lambda t, k: y[:, t, k * P:(k + 1) * P], yt),
                            first_out)
            jobs = [(chunks_of(yt), KP, BANK, [(lambda b: b, lambda t, n=n: x[:, t, n * BANK:(n + 1) * BANK])])
                    for n in range(2)]
            project_stage(env, "out1", first_out, jobs, alpha_x=ALPHA)


def mla_part(env, ctx, proj, y, shared, cqt, first_uq, first_out, cos, sin):
    nc = env.nc

    def tile(name, *shape):
        return ctx.enter_context(nc.sbuf_tensor(name, [P, *shape], F32))
    NC = (Q_RANK + KV_RANK) // P
    v = y[:, :, D // 2:].rearrange("p t (h c) -> p t h c", h=MLA_H)
    qn, kn = tile("qn", T, MLA_H, QK), tile("kn", T, MLA_H, QK)
    jobs = []
    for n in range(2):
        hs = slice(n * 4, n * 4 + 4)
        jobs.append((chunks_of(cqt, NC), [range(0, 2)], 4 * QK,
                     [(lambda b: by_head(b[:, 0:4 * QK], 4), lambda t, hs=hs: qn[:, t, hs, :])]))
    for n in range(2):
        hs = slice(n * 4, n * 4 + 4)
        jobs.append((chunks_of(cqt, NC)[2:], [range(0, 1)], BANK,
                     [(lambda b: by_head(b, 4)[:, :, 0:NOPE], lambda t, hs=hs: kn[:, t, hs, 0:NOPE]),
                      (lambda b: by_head(b, 4)[:, :, NOPE:], lambda t, hs=hs: v[:, t, hs, :])]))
    project_stage(env, "mla_proj", first_uq, jobs)
    H2 = ROPE // 2
    a, b = (shared[:, i * T * MLA_H * H2:(i + 1) * T * MLA_H * H2].rearrange("p (t h c) -> p t h c", t=T, h=MLA_H)
            for i in range(2))
    mla_rope_stage(env, proj, qn, kn, cos, sin, a, b)
    more = tile("more_heads", 2 * MLA_H - 10, S)
    heads = [shared[0:QK, i * S:(i + 1) * S] if i < 10 else more[0:QK, i - 10, :] for i in range(2 * MLA_H)]
    transpose_stage(env, "mla_t", [([src[:, t, h, :] for t in range(T)], heads[2 * h + i], None)
                                   for h in range(MLA_H) for i, src in enumerate((qn, kn))])
    attn = [dict(q=heads[2 * h][:, t * P:(t + 1) * P], k=heads[2 * h + 1], nk=S, mask=None,
                 v=[v[:, b, h, :] for b in range(T)], dst=y[:, t, h * MLA_V:(h + 1) * MLA_V])
            for h in range(MLA_H) for t in range(T)]

    def slots(tile_, n):
        flat = tile_[:, :, :, :].rearrange("p t h c -> p (t h c)")
        return flat[:, 0:n * S].rearrange("p (n s) -> p n s", n=n)
    attention_stage(env, "mla", attn, QK ** -0.5, slots(qn, 4), slots(kn, 2), prefetch=first_out + 3)


def first_experts(env, l, dram, x, vec):
    nc = env.nc
    at = layer_of(dram, l)
    layernorm_stage(env, "ln1", at("ln1"), x)
    with ExitStack() as local:
        def tile(name, *shape):
            return local.enter_context(nc.sbuf_tensor(name, [P, *shape], F32))
        oh, rank = tile("group_choice", T, GROUPS), tile("group_rank", T, GROUPS)
        combine = pair_tile(nc, local, "combine", T, EXPERTS)
        passes = local.enter_context(nc.sbuf_tensor("passes", [P, 1], I32))
        xp = pair_tile(nc, local, "x_pair", T, D)
        with nc.sbuf_tensor("router_xt", [P, KD, S], F32) as xt:
            transpose_stage(env, "x1_t", x_transposes(x, xt))
            router_stage(env, xt, at("router"), vec, combine, oh, rank, passes, x, xp)
        env.end_layer()
        take = local.enter_context(nc.sbuf_tensor("take", [P, GROUPS, T, SLOTS], F32R))
        put = local.enter_context(nc.sbuf_tensor("put", [P, GROUPS, 2, S], F32R))
        units, kinds = expert_units(at)
        env.stream = WeightStream(env, units)
        n = nc.values_load(passes[0:1, 0:1], min_val=1, max_val=-(-S // SLOTS))
        with nc.Fori(0, n):
            places_stage(env, oh, rank, take, put)
            expert_stage(env, x, xp, take, put, combine, kinds)
            env.end_layer()
    layernorm_stage(env, "ln2", at("ln2"), x)


def layer_of(dram, l):
    def at(name):
        ap = dram[name]
        ap = ap[tuple([bass.ds(l, 1)] + [slice(None)] * (len(ap.shape) - 1))]
        if len(ap.shape) == 2:
            return ap
        dims = [f"d{i}" for i in range(1, len(ap.shape))]
        return ap.rearrange(f"a {' '.join(dims)} -> (a {dims[0]}) {' '.join(dims[1:])}")
    return at


def load_small_stage(env, stage, pairs, prefetch):
    nc = env.nc
    loaded = env.sem(stage, "loaded")
    with nc.Block() as block:
        @block.sync
        def _(sp):
            for dst, src in pairs:
                sp.dma_start(dst, src).then_inc(loaded, 16)
            env.stream.load(sp, prefetch)
            sp.wait_ge(loaded, 16 * len(pairs))



def rms_stage(env, stage, x, out):
    nc = env.nc
    squares, roots, step = (env.sem(stage, n) for n in ("squares_summed", "roots", "vector_step"))
    with nc.sbuf_tensor(f"{stage}_ss", [P, T], F32) as ss:
        with nc.Block() as block:
            @block.scalar
            def _(act):
                for t in range(T):
                    nc.scalar.activation(out[:, t, :], x[:, t, :], ACT.Square, accum_out=ss[:, t:t + 1]
                                         ).then_inc(squares, 1)
                act.wait_ge(squares, T)
                nc.scalar.activation(ss[:, :], ss[:, :], ACT.Sqrt, scale=1.0 / D, bias=env.eps6).then_inc(roots, 1)

            @block.vector
            def _(dve):
                link = Link(dve, step)
                dve.wait_ge(roots, 1)
                link(nc.vector.reciprocal(ss[:, :], ss[:, :]))
                for t in range(T):
                    nc.vector.tensor_scalar(out[:, t, :], x[:, t, :], ss[:, t:t + 1], None, ALU.mult)


def index_score(proj, t):
    return proj[:, t, B_IQ:B_IQ + (t + 1) * P]


def second_projection_units(w_in):
    units, jobs = [], []
    for c, w, heads in ((B_IK, B_IW + IDX_H - B_IK, None), (B_IQ, BANK, None), (B_MQ, BANK, (0, (0, 1))),
                        (B_DQ, BANK, (1, (0, 0))), (B_DK, BANK, (1, (1, 1))), (B_SQ, BANK, (2, (0, 1))),
                        (B_MV, 256, None), (B_SV, 256, None), (B_DV, BANK, None)):
        rows = P * min(KD, WeightStream.UNIT // w)
        jobs.append((len(units), D // rows, c, w, heads))
        units += weight_units(w_in[:, c:c + w], rows=rows)
    return units, jobs


def second_projection_stage(env, ht, jobs, proj, vec2, iw, lam, subln, diff_gain):
    nc, ps, ident, causal, stream = env.nc, env.ps, env.ident, env.causal, env.stream
    names = ("tile_done", "tile_stored", "squared", "roots", "inverses", "scaled", "lambda_dots", "lambda_exps", "rotated",
             "turned", "turned_copied", "logits_ready", "relu_done", "added", "vector_step")
    (tile_done, tile_stored, squared, roots, inverses, scaled, dots, exps, rotated, turned, turned_copied, logits_ready,
     relu_done, added, step) = (env.sem("proj2", n) for n in names)
    TAKEN = -3e38
    NH = BANK // HD
    N = jobs[-1][0] + jobs[-1][1]
    normed = [c for c, j in enumerate(jobs) if j[4]]
    ends = {c: jobs[c][0] + jobs[c][1] - 1 for c in range(len(jobs))}
    index_done = 2
    tiles = list(range(N_TOP // P, T))
    logits = [(t, h) for t in tiles for h in range(IDX_H)]
    NTURN = IDX_H // 2 + 1
    first = jobs[index_done][0] + 1
    slots = [(u, t) for u in range(first, N) for t in range(T)]
    turns_at = {slots[i // 2]: range(i, min(i + 2, NTURN)) for i in range(0, NTURN, 2)}
    after = (NTURN + 1) // 2
    logits_at = {slots[after + i // 3]: range(i, min(i + 3, len(logits))) for i in range(0, len(logits), 3)}

    with ExitStack() as local:
        def tile(name, *shape):
            return local.enter_context(nc.sbuf_tensor(name, [P, *shape], F32))
        ss = tile("head_ss", len(normed), T, NH)
        squares = tile("head_squares", NH, HD)
        ik2 = tile("ik2", T, P)
        iqk_t = tile("iqk_t", NTURN, S)
        relu = tile("index_relu", 2, S)
        top = tile("index_top", T, 8)
        a, b = tile("rope_a", T, NH + 1, HALF), tile("rope_b", T, NH + 1, HALF)
        tables = tile("rope_tables", 2, 4, T, HALF)
        lt, dot = tile("lam_tmp", HD), tile("lam_dot", 2)
        iq = proj[:, :, B_IQ:B_IK + HD].rearrange("p t (h c) -> p t h c", h=IDX_H + 1)

        with nc.Block() as block:
            @block.sync
            def _(sp):
                stream.load(sp, N + stream.RAW)

            @block.tensor
            def _(pe):
                def between(n, t):
                    for i in turns_at.get((n, t), ()):
                        pe.wait_ge(rotated, 1)
                        if i >= 4:
                            pe.wait_ge(turned_copied, i - 3)
                        for s in range(T):
                            src = ik2[:, s, :] if i == NTURN - 1 else proj[:, s, B_IQ + i * P:B_IQ + (i + 1) * P]
                            last = nc.tensor.transpose(ps[:, T + i % 4, s * P:(s + 1) * P], src, ident)
                        last.then_inc(turned, 1)
                    for i in logits_at.get((n, t), ()):
                        s, h = logits[i]
                        base = (h % 2) * HD
                        pe.wait_ge(turned_copied, NTURN)
                        if i >= 4:
                            pe.wait_ge(relu_done, i - 3)
                        nc.tensor.matmul(ps[:, T + i % 4, 0:(s + 1) * P],
                                         iqk_t[base:base + HD, h // 2, s * P:(s + 1) * P],
                                         iqk_t[base:base + HD, NTURN - 1, 0:(s + 1) * P], start=True, stop=True
                                         ).then_inc(logits_ready, 1)

                project_between(env, pe, jobs, ht, tile_done, tile_stored, between)

            @block.scalar
            def _(act):
                act.wait_ge(dots, 1)
                nc.scalar.activation(dot[:, :], dot[:, :], ACT.Exp).then_inc(exps, 1)

                def tile_work(c, t):
                    if c not in normed:
                        return
                    i, col = normed.index(c), jobs[c][2]
                    act.wait_ge(tile_stored, c * T + t + 1)
                    if i * T + t:
                        act.wait_ge(squared, (i * T + t) * NH)
                    for h in range(NH):
                        nc.scalar.activation(squares[:, h, :], proj[:, t, col + h * HD:col + (h + 1) * HD], ACT.Square,
                                             accum_out=ss[:, i, t, h:h + 1]).then_inc(squared, 1)
                    if t == T - 1:
                        act.wait_ge(squared, (i + 1) * T * NH)
                        nc.scalar.activation(ss[:, i, :, :], ss[:, i, :, :], ACT.Sqrt, scale=1.0 / HD, bias=env.eps6
                                             ).then_inc(roots, 1)

                def between(n, t):
                    for i in turns_at.get((n, t), ()):
                        act.wait_ge(turned, i + 1)
                        nc.scalar.activation(iqk_t[:, i, :], ps[:, T + i % 4, :], ACT.Copy).then_inc(turned_copied, 1)
                    for i in logits_at.get((n, t), ()):
                        s, h = logits[i]
                        act.wait_ge(logits_ready, i + 1)
                        if i >= 2:
                            act.wait_ge(added, i - 1)
                        nc.scalar.activation(relu[:, i % 2, 0:(s + 1) * P], ps[:, T + i % 4, 0:(s + 1) * P],
                                             ACT.Relu, scale=HD ** -0.5).then_inc(relu_done, 1)

                store_between(env, act, jobs, proj, tile_done, tile_stored, tile_work, between)

            @block.gpsimd
            def _(pool):
                for n in range(N):
                    stream.split_lo(pool, n)
                    for i, c in enumerate(normed):
                        if n == ends[c] + 3:
                            pool.wait_ge(inverses, i + 1)
                            x = proj[:, :, jobs[c][2]:jobs[c][2] + BANK]
                            for t in range(T):
                                last = nc.gpsimd.tensor_tensor(by_head(x[:, t], NH), by_head(x[:, t], NH),
                                                               per_tile(ss[:, i, t, :], HD), ALU.mult)
                            last.then_inc(scaled, 1)

            @block.vector
            def _(dve):
                link = Link(dve, step)
                v = nc.vector
                cos2, sin2 = env.cos2, env.sin2

                def make_tables(g):
                    for side, gains in enumerate((V2_Q, V2_K)):
                        for half in range(2):
                            o = gains + g * HD + half * HALF
                            gain = vec2[:, o:o + HALF].unsqueeze(1).to_broadcast([P, T, HALF])
                            v.tensor_tensor(tables[:, side, 2 * half], cos2, gain, ALU.mult)
                            last = v.tensor_tensor(tables[:, side, 2 * half + 1], sin2, gain, ALU.mult)
                    link(last)

                def rotate(x1, x2, c1, s1, c2, s2, nh):
                    shape = [P, T, nh, HALF]
                    c1, s1, c2, s2 = (m.unsqueeze(2).to_broadcast(shape) for m in (c1, s1, c2, s2))
                    p, q = a[:, :, 0:nh, :], b[:, :, 0:nh, :]
                    v.tensor_tensor(p, x1, s1, ALU.mult)
                    v.tensor_tensor(q, x2, s2, ALU.mult)
                    v.tensor_tensor(x1, x1, c1, ALU.mult)
                    link(v.tensor_tensor(x2, x2, c2, ALU.mult))
                    v.tensor_tensor(x1, x1, q, ALU.subtract)
                    return v.tensor_tensor(x2, x2, p, ALU.add)

                def invert(i):
                    dve.wait_ge(roots, i + 1)
                    v.reciprocal(ss[:, i, :, :], ss[:, i, :, :]).then_inc(inverses, 1)

                def rotate_job(i):
                    _, _, col, w, (g, sides) = jobs[normed[i]]
                    if i == 0 or jobs[normed[i - 1]][4][0] != g:
                        make_tables(g)
                    dve.wait_ge(scaled, i + 1)
                    x = proj[:, :, col:col + BANK].rearrange("p t (h c) -> p t h c", h=NH)
                    for part, side in enumerate(sides):
                        xs = x[:, :, part * NH // 2:(part + 1) * NH // 2, :]
                        last = rotate(xs[:, :, :, 0:HALF], xs[:, :, :, HALF:HD], *(tables[:, side, m] for m in range(4)),
                                      NH // 2)
                        link(last)

                def add_up(which):
                    for i in which:
                        t, h = logits[i]
                        dve.wait_ge(relu_done, i + 1)
                        sc, w = index_score(proj, t), iw[:, t, h:h + 1]
                        r = relu[:, i % 2, 0:(t + 1) * P]
                        if h == 0:
                            ins = v.tensor_scalar(sc, r, w, None, ALU.mult)
                        else:
                            ins = v.scalar_tensor_tensor(out=sc, in0=r, scalar=w, in1=sc, op0=ALU.mult, op1=ALU.add)
                        ins.then_inc(added, 1)
                        dve.wait_ge(added, i + 1)

                def find_top(rounds):
                    for r in rounds:
                        for t in tiles:
                            last = v.max(top[:, t, :], index_score(proj, t))
                        link(last)
                        for t in tiles:
                            last = v.match_replace(index_score(proj, t), top[:, t, :], index_score(proj, t), TAKEN)
                        link(last)

                for n in range(2):
                    o = V2_L + 2 * n * HD
                    link(v.tensor_tensor(lt[:, :], vec2[:, o:o + HD], vec2[:, o + HD:o + 2 * HD], ALU.mult))
                    link(v.reduce_sum(dot[:, n:n + 1], lt[:, :], AX))
                v.tensor_scalar(dot[:, :], dot[:, :], 1.0, None, ALU.mult).then_inc(dots, 1)
                dve.wait_ge(exps, 1)
                link(v.tensor_tensor(lam, dot[:, 1:2], dot[:, 0:1], ALU.subtract))
                link(v.tensor_tensor(lam, lam, env.lam_c[:, 0:1], ALU.subtract))
                v.tensor_tensor(diff_gain, subln, env.lam_c[:, 1:2], ALU.mult)
                dve.wait_ge(tile_stored, index_done * T)
                link(rotate(iq[:, :, :, 0:HALF], iq[:, :, :, HALF:HD], cos2, sin2, cos2, sin2, IDX_H + 1))
                link(v.tensor_scalar(iw[:, :, :], proj[:, :, B_IW:B_IW + IDX_H], IDX_H ** -0.5, None, ALU.mult))
                for n in range(2):
                    last = v.tensor_copy(ik2[:, :, n * HD:(n + 1) * HD], proj[:, :, B_IK:B_IK + HD])
                last.then_inc(rotated, 1)
                add_up(range(0, IDX_H))
                invert(0)
                add_up(range(IDX_H, len(logits)))
                for t in tiles:
                    diag = index_score(proj, t)[:, t * P:(t + 1) * P]
                    last = v.tensor_tensor(diag, diag, causal, ALU.add)
                link(last)
                ROUNDS = N_TOP // 8
                share = ROUNDS // len(normed)
                for i in range(len(normed)):
                    rotate_job(i)
                    if i + 1 < len(normed):
                        invert(i + 1)
                    find_top(range(i * share, (i + 1) * share if i + 1 < len(normed) else ROUNDS))
                for t in tiles:
                    v.tensor_scalar(index_score(proj, t), index_score(proj, t), TAKEN, MASKED, ALU.not_equal, ALU.mult)


class DiffEnd:
    NH, W = 4, 128

    def __init__(self, env, ctx, after, before_end, d1, d2, lam):
        self.env, self.after, self.d1, self.d2, self.lam = env, after, d1, d2, lam
        self.at = before_end
        self.squares = ctx.enter_context(env.nc.sbuf_tensor("diff_squares", [P, T, self.NH, self.W], F32))
        self.ss = ctx.enter_context(env.nc.sbuf_tensor("diff_ss", [P, T, self.NH], F32))
        names = ("combined", "squared", "root", "inverse")
        self.combined, self.squared, self.root, self.inverse = (env.sem("diff_end", n) for n in names)

    def pool(self, pool, out_stored):
        g = self.env.nc.gpsimd
        pool.wait_ge(out_stored, self.after)
        for t in range(T):
            g.tensor_scalar(self.d2[:, t, :], self.d2[:, t, :], self.lam, None, ALU.mult).then_inc(self.combined, 1)
        for t in range(T):
            pool.wait_ge(self.combined, t + 1)
            g.tensor_tensor(self.d1[:, t, :], self.d1[:, t, :], self.d2[:, t, :], ALU.add).then_inc(self.combined, 1)
        pool.wait_ge(self.inverse, 1)
        for t in range(T):
            y = by_head(self.d1[:, t, :], self.NH)
            g.tensor_tensor(y, y, per_tile(self.ss[:, t, :], self.W), ALU.mult)

    def scalar(self, act, i):
        nc, t = self.env.nc, i - self.at
        if 0 <= t < T:
            act.wait_ge(self.combined, T + t + 1)
            for h in range(self.NH):
                nc.scalar.activation(self.squares[:, t, h, :], self.d1[:, t, h * self.W:(h + 1) * self.W], ACT.Square,
                                     accum_out=self.ss[:, t, h:h + 1]).then_inc(self.squared, 1)
        if t == T:
            act.wait_ge(self.squared, T * self.NH)
            nc.scalar.activation(self.ss[:, :, :], self.ss[:, :, :], ACT.Sqrt, scale=1.0 / self.W, bias=self.env.eps6
                                 ).then_inc(self.root, 1)

    def vector(self, dve, i):
        if i == self.at + T + 1:
            dve.wait_ge(self.root, 1)
            self.env.nc.vector.reciprocal(self.ss[:, :, :], self.ss[:, :, :]).then_inc(self.inverse, 1)


def second_layer(env, l, dram, x):
    nc = env.nc
    at = layer_of(dram, l)
    KP = [range(0, 4), range(4, 8)]
    w_gate, w_up, w_down = at("w_gate_2"), at("w_up_2"), at("w_down_2")
    units, jobs = second_projection_units(at("w_in_2"))
    first_out = len(units)
    first_ffn = first_out + 4
    units += weight_units(at("w_out_2"))
    for c in range(0, D_FF, F_CH):
        for w in (w_gate, w_up):
            units.append(w[:, c:c + F_CH].rearrange("(k p) w -> p k w", p=P))
    env.stream = WeightStream(env, units + weight_units(w_down))

    with ExitStack() as local:
        def tile(ctx, name, *shape):
            return ctx.enter_context(nc.sbuf_tensor(name, [P, *shape], F32))
        vec2, gains = tile(local, "vec2", NV2), tile(local, "gains2", 2 * KD + 1)
        env.lam_c = tile(local, "lam_c", 2)
        load_small_stage(env, "small2", [(vec2[:, :], at("vec2").to_broadcast([P, NV2])),
                                         (gains[:, :], at("gains2")),
                                         (env.lam_c[:, :], at("lam_init").to_broadcast([P, 2]))], env.stream.RAW)

        def normed_turned(ctx, stage, gain, first):
            ht = pair_tile(nc, ctx, f"{stage}_ht", KD, S)
            with nc.sbuf_tensor(f"{stage}_h", [P, T, D], F32) as h:
                rms_stage(env, f"{stage}_rms", x, h)
                transpose_stage(env, f"{stage}_t", pair_transposes(lambda t, k: h[:, t, k * P:(k + 1) * P], ht, gain),
                                first)
            return ht

        with ExitStack() as mix:
            proj = tile(mix, "proj2", T, IN2)
            iw, lam = tile(mix, "iw", T, IDX_H), tile(mix, "lam", 1)
            diff_gain = tile(mix, "diff_gain", 1)
            with ExitStack() as pre:
                ht = normed_turned(pre, "attn", gains[:, 0:KD], 0)
                second_projection_stage(env, ht, jobs, proj, vec2, iw, lam[:, 0:1], gains[:, 2 * KD:2 * KD + 1],
                                        diff_gain[:, 0:1])
            with ExitStack() as heads:
                qk_t = tile(heads, "qk_t", 16, S)
                cols = ([B_MQ + c * P for c in range(4)] + [B_DQ + c * P for c in range(8)]
                        + [B_SQ + c * P for c in range(4)])
                transpose_stage(env, "qk_t", [([proj[:, t, c:c + P] for t in range(T)], qk_t[:, n, :], None)
                                              for n, c in enumerate(cols)])

                second_of_pair = proj[:, :, B_DK:B_DK + 512]

                def half(chunk, h):
                    base = (h % 2) * HD
                    return qk_t[base:base + HD, chunk + h // 2, :]

                units = []
                for name, nh, q0, k0 in (("diff", 8, 4, 8), ("moba", 4, 0, 2), ("dsa", 4, 12, 14)):
                    for h in range(nh):
                        for t in range(T):
                            nk = (t + 1) * P
                            u = dict(q=half(q0, h)[:, t * P:nk], k=half(k0, h)[:, 0:nk], nk=nk, mask="diag")
                            if name == "moba":
                                u["v"] = [proj[:, b, B_MV + h * HD:B_MV + (h + 1) * HD] for b in range(t + 1)]
                                u["dst"] = proj[:, t, B_MQ + h * HD:B_MQ + (h + 1) * HD]
                            elif name == "dsa":
                                u["v"] = [proj[:, b, B_SV + h * HD:B_SV + (h + 1) * HD] for b in range(t + 1)]
                                u["dst"] = proj[:, t, B_SQ + h * HD:B_SQ + (h + 1) * HD]
                                if t >= N_TOP // P:
                                    u["mask"] = index_score(proj, t)
                            else:
                                g = slice((h // 2) * P, (h // 2 + 1) * P)
                                u["v"] = [proj[:, b, B_DV:B_DV + 512][:, g] for b in range(t + 1)]
                                u["dst"] = second_of_pair[:, t, g] if h % 2 else proj[:, t, B_DQ:B_DQ + 512][:, g]
                            units.append(u)
                diff_end = DiffEnd(env, heads, 8 * T, len(units) - T, proj[:, :, B_DQ:B_DQ + 512], second_of_pair, lam[:, 0:1])
                attention_stage(env, "attn2", units, HD ** -0.5, prefetch=first_out + 3, meanwhile=diff_end)
            yt = pair_tile(nc, mix, "y2t", KD, S)
            place = [B_MQ, B_MQ + P] + [B_DQ + c * P for c in range(4)] + [B_SQ, B_SQ + P]
            turns = pair_transposes(lambda t, k: proj[:, t, place[k]:place[k] + P], yt)
            for k in range(2, 6):
                turns[k] = (*turns[k][:2], diff_gain[:, 0:1])
            transpose_stage(env, "y2_t", turns, first_out)
            jobs = [(chunks_of(yt), KP, BANK, [(lambda b: b, lambda t, n=n: x[:, t, n * BANK:(n + 1) * BANK])])
                    for n in range(2)]
            project_stage(env, "out2", first_out, jobs, alpha_x=1.0, prefetch=3)
        ht = normed_turned(local, "ffn", gains[:, KD:2 * KD], first_ffn)
        ffn_stage(env, "ffn", first_ffn, ht, FF_CH, x)


def build(nc, dram, out):
    with ExitStack() as ctx:
        env = Env(nc)

        def tile(name, *shape):
            return ctx.enter_context(nc.sbuf_tensor(name, [P, *shape], F32))
        x = tile("x", T, D)
        env.raw = tile("weights_raw", WeightStream.RAW, WeightStream.UNIT)
        env.w_hi, env.w_lo = pair_tile(nc, ctx, "weights", WeightStream.SPLIT, WeightStream.UNIT)
        env.consts = tile("consts", NK)
        eps = tile("eps", 2)
        cos1, sin1 = tile("cos1", T, ROPE // 2), tile("sin1", T, ROPE // 2)
        env.ps = ctx.enter_context(nc.psum_tensor("ps", [P, NBANK, BANK], F32))
        env.ident = env.consts[:, K_ID:K_ID + P]
        env.keep_ge = env.consts[:, K_GE:K_GE + P]
        env.ones = env.consts[:, K_ONES:K_ONES + P]
        env.slot_numbers = env.consts[:, K_SLOT:K_SLOT + SLOTS]
        env.keep_le = env.consts[:, K_LE:K_LE + P]
        env.causal = env.consts[:, K_CAUSAL:K_CAUSAL + P]
        env.cos2 = env.consts[:, K_COS:K_COS + T * HALF].rearrange("p (t c) -> p t c", t=T)
        env.sin2 = env.consts[:, K_SIN:K_SIN + T * HALF].rearrange("p (t c) -> p t c", t=T)
        env.eps5, env.eps6 = eps[:, 0:1], eps[:, 1:2]
        saved = ctx.enter_context(nc.semaphore("output_saved"))
        start_loaded = ctx.enter_context(nc.semaphore("start_loaded"))

        with nc.Block() as block:
            @block.sync
            def _(sp):
                sp.dma_start(x[:, :, :], dram["x"].rearrange("a (t p) d -> p (a t) d", p=P)).then_inc(start_loaded, 16)
                sp.dma_start(env.consts[:, :], dram["consts"]).then_inc(start_loaded, 16)
                sp.wait_ge(start_loaded, 32)

            @block.vector
            def _(dve):
                nc.vector.memset(eps[:, 0:1], 1e-5)
                nc.vector.memset(eps[:, 1:2], 1e-6)
        with env.semaphores():
            rope_table_stage(env, dram["positions"], cos1[:, :, :], sin1[:, :, :])
            env.end_layer()
        with env.semaphores(), nc.Fori(0, DEPTH) as l, ExitStack() as local:
            vec = local.enter_context(nc.sbuf_tensor("vec1", [P, NV1], F32))
            with nc.sbuf_tensor("convw", [P, CC, CONV + 1], F32) as convw:
                first_mixers(env, l, dram, x, vec, convw, cos1[:, :, :], sin1[:, :, :])
            env.end_layer()
            first_experts(env, l, dram, x, vec)
            env.end_layer()
        with env.semaphores(), nc.Fori(0, DEPTH) as l:
            second_layer(env, l, dram, x)
            env.end_layer()
        with nc.Block() as block:
            @block.sync
            def _(sp):
                sp.dma_start(out.rearrange("a (t p) d -> p (a t) d", p=P), x[:, :, :]).then_inc(saved, 16)
                sp.wait_ge(saved, 16)


def constants():
    c = np.zeros((P, NK), np.float32)
    i = np.arange(P)
    c[:, K_ID:K_ID + P] = np.eye(P)
    c[:, K_GE:K_GE + P] = i[None, :] >= i[:, None]
    c[:, K_LE:K_LE + P] = i[None, :] <= i[:, None]
    c[:, K_CAUSAL:K_CAUSAL + P] = np.where(i[None, :] <= i[:, None], 0.0, MASKED)
    c[:, K_ONES:K_ONES + P] = 1.0
    c[:, K_SLOT:K_SLOT + SLOTS] = np.arange(1, SLOTS + 1)
    f = np.float32
    inv = f(1.0) / f(10000.0) ** (np.arange(0, HD, 2, dtype=f) / f(HD))
    ang = (np.arange(S, dtype=f)[:, None] * inv[None, :]).reshape(T, P, HALF).transpose(1, 0, 2)
    c[:, K_COS:K_COS + T * HALF] = np.cos(ang).reshape(P, -1)
    c[:, K_SIN:K_SIN + T * HALF] = np.sin(ang).reshape(P, -1)
    c[:, K_INV:K_INV + ROPE // 2] = f(10000.0) ** (-np.arange(0, ROPE, 2, dtype=f) / f(ROPE))
    return c


def packed(i):
    n = DEPTH

    def rows(*names):
        return np.concatenate([np.asarray(i[k]).reshape(n, -1) for k in names], 1)

    def by_partition(a):
        return np.asarray(a).reshape(n, KD, P).transpose(0, 2, 1)

    conv = np.concatenate([np.asarray(i["ssd_conv_w"]), np.asarray(i["ssd_conv_b"])[:, None]], 1)
    lam0 = [0.8 - 0.6 * float(np.exp(-0.3 * l)) for l in range(n)]
    arrays = {
        "consts": constants(),
        "vec1": rows("mla_q_norm", "mla_kv_norm", "mlstm_gate_bias", "mlstm_norm", "ssd_dt_bias", "ssd_a_log",
                     "ssd_d", "ssd_norm", "router_group_b", "router_expert_b"),
        "conv1": conv.transpose(0, 2, 1).reshape(n, CC, P, CONV + 1).transpose(0, 2, 1, 3),
        "ln1": rows("ln1_g", "ln1_b"), "ln2": rows("ln2_g", "ln2_b"),
        "router": np.concatenate([np.asarray(i["router_group_w"]),
                                  np.asarray(i["router_expert_w"]).transpose(0, 2, 1, 3).reshape(n, D, EXPERTS)], 2),
        "vec2": rows("q_norm_g_2", "k_norm_g_2", "diff_lambda_2"),
        "gains2": np.concatenate([by_partition(i["attn_norm_g_2"]), by_partition(i["ffn_norm_g_2"]),
                                  np.asarray(i["diff_subln_g_2"]).reshape(n, P, 1)], 2),
        "lam_init": np.array([[a, 1.0 - a] for a in lam0], np.float32),
    }
    for k in ("x", "positions", "w_in", "mla_w_uq", "mla_w_ukv", "w_out", "expert_w_gate", "expert_w_up",
              "expert_w_down", "w_in_2", "w_out_2", "w_gate_2", "w_up_2", "w_down_2"):
        arrays[k] = np.asarray(i[k])
    return {k: np.ascontiguousarray(v) for k, v in arrays.items()}


def kernel(**inputs):
    import concourse.bacc as bacc
    from concourse.bass_utils import run_bass_kernel_spmd

    nc = bacc.Bacc("TRN2", target_bir_lowering=False, num_devices=1)
    arrays = packed(inputs)
    dram = {k: nc.dram_tensor(f"in_{k}", list(a.shape), mybir.dt.from_np(a.dtype), kind="ExternalInput").ap()
            for k, a in arrays.items()}
    out = nc.dram_tensor("out_x", [1, S, D], F32, kind="ExternalOutput").ap()
    build(nc, dram, out)
    r = run_bass_kernel_spmd(nc, [{f"in_{k}": a for k, a in arrays.items()}], core_ids=[0])
    return r.results[0]["out_x"]
```
